# Optimizing a Trainium2 kernel written in Bass

```python
import math
import jax, jax.numpy as jnp
from jax import lax
import numpy as np

D_MODEL = 1024
BATCH = 1
SEQ = 512
DEPTH = 2

N_Q_HEADS = 8
N_KV_HEADS = 2
HEAD_DIM = 64
Q_GROUP = N_Q_HEADS // N_KV_HEADS
WINDOW = 128
BLOCK = 128
ROPE_THETA = 500000.0
ROT_DIM = HEAD_DIM // 4
ATTN_WIDTH = N_Q_HEADS * HEAD_DIM
KV_WIDTH = N_KV_HEADS * HEAD_DIM
NEG_INF = -1e30
CONV_WIDTH = D_MODEL // 2
CONV_K = 3
SSM_WIDTH = D_MODEL // 2
SSM_GROUP = 16
SSM_GROUPS = SSM_WIDTH // SSM_GROUP
SSM_STATE = 64
DT_MIN = 1e-3
DT_MAX = 1e-1
N_BRANCH = 3
GATE_WIDTH = N_BRANCH * D_MODEL
FFN_HIDDEN = -(-8 * D_MODEL // (3 * 256)) * 256
NORM_EPS = 1e-6

IN_SIZES = (ATTN_WIDTH, KV_WIDTH, KV_WIDTH, CONV_WIDTH, CONV_WIDTH, CONV_WIDTH, SSM_WIDTH, GATE_WIDTH)
IN_COLS = sum(IN_SIZES)
IN_SPLITS = tuple(int(v) for v in np.cumsum(IN_SIZES)[:-1])


def rmsnorm(x, g):
    xf = x.astype(jnp.float32)
    y = xf * lax.rsqrt(jnp.mean(xf * xf, axis=-1, keepdims=True) + NORM_EPS)
    return (y * g.astype(jnp.float32)).astype(x.dtype)

def rope_tables(seq_len):
    pos = jnp.arange(seq_len, dtype=jnp.float32)
    inv_freq = ROPE_THETA ** (-jnp.arange(0, ROT_DIM, 2, dtype=jnp.float32) / ROT_DIM)
    ang = pos[:, None] * inv_freq[None, :]
    return jnp.cos(ang), jnp.sin(ang)

def partial_rope(t, cos, sin):
    half = ROT_DIM // 2
    tf = t.astype(jnp.float32)
    t1, t2, rest = tf[..., :half], tf[..., half:ROT_DIM], tf[..., ROT_DIM:]
    c = cos[None, :, None, :]
    s = sin[None, :, None, :]
    out = jnp.concatenate([t1 * c - t2 * s, t2 * c + t1 * s, rest], axis=-1)
    return out.astype(t.dtype)

def sliding_window_attention(q, k, v, sinks):
    b, l = q.shape[0], q.shape[1]
    nb = l // BLOCK
    qb = q.reshape(b, nb, BLOCK, N_KV_HEADS, Q_GROUP, HEAD_DIM).astype(jnp.float32)

    def band(t):
        tp = jnp.pad(t, ((0, 0), (BLOCK, 0), (0, 0), (0, 0)))
        tp = tp.reshape(b, nb + 1, BLOCK, N_KV_HEADS, HEAD_DIM)
        return jnp.concatenate([tp[:, :-1], tp[:, 1:]], axis=2).astype(jnp.float32)

    kb, vb = band(k), band(v)
    s = jnp.einsum("bnqkgd,bnskd->bnkgqs", qb, kb) * (HEAD_DIM ** -0.5)
    qi = jnp.arange(BLOCK)[:, None]
    kj = jnp.arange(2 * BLOCK)[None, :]
    delta = qi + BLOCK - kj
    band_ok = (delta >= 0) & (delta < WINDOW)
    kpos = jnp.arange(nb)[:, None] * BLOCK - BLOCK + kj
    mask = band_ok[None, :, :] & (kpos >= 0)[:, None, :]
    s = jnp.where(mask[None, :, None, None, :, :], s, NEG_INF)
    sink = sinks.astype(jnp.float32).reshape(N_KV_HEADS, Q_GROUP)[None, None, :, :, None, None]
    m = jnp.maximum(jnp.max(s, axis=-1, keepdims=True), sink)
    p = jnp.exp(s - m)
    denom = jnp.sum(p, axis=-1, keepdims=True) + jnp.exp(sink - m)
    o = jnp.einsum("bnkgqs,bnskd->bnqkgd", p / denom, vb)
    return o.reshape(b, l, ATTN_WIDTH).astype(q.dtype)

def short_conv(z, w):
    l = z.shape[1]
    zp = jnp.pad(z, ((0, 0), (CONV_K - 1, 0), (0, 0)))
    y = w[0] * zp[:, 0:l]
    for j in range(1, CONV_K):
        y = y + w[j] * zp[:, j:j + l]
    return y

def s5_ssm(u, a_re, a_im, b_re, b_im, c_re, c_im, d, log_dt):
    bsz, l = u.shape[0], u.shape[1]
    uf = u.astype(jnp.float32).reshape(bsz, l, SSM_GROUPS, SSM_GROUP)
    lam = lax.complex(a_re.astype(jnp.float32), a_im.astype(jnp.float32))
    dt = jnp.exp(log_dt.astype(jnp.float32))[:, None]
    lam_bar = jnp.exp(lam * dt)
    b_c = lax.complex(b_re.astype(jnp.float32), b_im.astype(jnp.float32))
    b_bar = ((lam_bar - 1.0) / lam)[..., None] * b_c
    bu = jnp.einsum("blgh,gph->blgp", uf.astype(jnp.complex64), b_bar)
    a_elems = jnp.broadcast_to(lam_bar, bu.shape)

    def combine(e1, e2):
        a1, x1 = e1
        a2, x2 = e2
        return a1 * a2, a2 * x1 + x2

    _, states = lax.associative_scan(combine, (a_elems, bu), axis=1)
    c_c = lax.complex(c_re.astype(jnp.float32), c_im.astype(jnp.float32))
    y = jnp.einsum("blgp,ghp->blgh", states, c_c).real
    y = y + d.astype(jnp.float32).reshape(SSM_GROUPS, SSM_GROUP) * uf
    return y.reshape(bsz, l, SSM_WIDTH).astype(u.dtype)

def first_inputs(seed: int = 0) -> dict:
    key = jax.random.key(seed)
    ks = jax.random.split(key, 24)
    L = DEPTH

    def nrm(k, shape, fan_in):
        return jax.random.normal(k, shape, jnp.float32) * (fan_in ** -0.5)

    x = jax.random.normal(ks[0], (BATCH, SEQ, D_MODEL), jnp.float32)
    norm_mix = 1.0 + 0.02 * jax.random.normal(ks[1], (L, D_MODEL), jnp.float32)
    w_in = nrm(ks[2], (L, D_MODEL, IN_COLS), D_MODEL)
    b_gate = 0.02 * jax.random.normal(ks[3], (L, GATE_WIDTH), jnp.float32)
    attn_sinks = 0.5 * jax.random.normal(ks[4], (L, N_Q_HEADS), jnp.float32)
    w_attn_o = nrm(ks[5], (L, ATTN_WIDTH, D_MODEL), ATTN_WIDTH)
    conv_w = nrm(ks[6], (L, CONV_K, CONV_WIDTH), CONV_K)
    w_conv_o = nrm(ks[7], (L, CONV_WIDTH, D_MODEL), CONV_WIDTH)
    ssm_a_re = -0.5 + 0.01 * jax.random.normal(ks[8], (L, SSM_GROUPS, SSM_STATE), jnp.float32)
    ssm_a_im = (math.pi * jnp.arange(SSM_STATE, dtype=jnp.float32))[None, None, :] \
        + 0.01 * jax.random.normal(ks[9], (L, SSM_GROUPS, SSM_STATE), jnp.float32)
    ssm_b_re = nrm(ks[10], (L, SSM_GROUPS, SSM_STATE, SSM_GROUP), 2 * SSM_GROUP)
    ssm_b_im = nrm(ks[11], (L, SSM_GROUPS, SSM_STATE, SSM_GROUP), 2 * SSM_GROUP)
    ssm_c_re = nrm(ks[12], (L, SSM_GROUPS, SSM_GROUP, SSM_STATE), 2 * SSM_STATE)
    ssm_c_im = nrm(ks[13], (L, SSM_GROUPS, SSM_GROUP, SSM_STATE), 2 * SSM_STATE)
    ssm_d = jax.random.normal(ks[14], (L, SSM_WIDTH), jnp.float32)
    ssm_log_dt = jax.random.uniform(ks[15], (L, SSM_GROUPS), jnp.float32,
                                    minval=math.log(DT_MIN), maxval=math.log(DT_MAX))
    w_ssm_glu = nrm(ks[16], (L, SSM_WIDTH, SSM_WIDTH), SSM_WIDTH)
    w_ssm_o = nrm(ks[17], (L, SSM_WIDTH, D_MODEL), SSM_WIDTH)
    w_mix_o = nrm(ks[18], (L, D_MODEL, D_MODEL), D_MODEL)
    norm_ffn = 1.0 + 0.02 * jax.random.normal(ks[19], (L, D_MODEL), jnp.float32)
    w_ffn_in = nrm(ks[20], (L, D_MODEL, 2 * FFN_HIDDEN), D_MODEL)
    w_ffn_out = nrm(ks[21], (L, FFN_HIDDEN, D_MODEL), FFN_HIDDEN)
    norm_final = 1.0 + 0.02 * jax.random.normal(ks[22], (D_MODEL,), jnp.float32)
    return {"x": x, "norm_mix": norm_mix, "w_in": w_in, "b_gate": b_gate,
            "attn_sinks": attn_sinks, "w_attn_o": w_attn_o, "conv_w": conv_w, "w_conv_o": w_conv_o,
            "ssm_a_re": ssm_a_re, "ssm_a_im": ssm_a_im, "ssm_b_re": ssm_b_re, "ssm_b_im": ssm_b_im,
            "ssm_c_re": ssm_c_re, "ssm_c_im": ssm_c_im, "ssm_d": ssm_d, "ssm_log_dt": ssm_log_dt,
            "w_ssm_glu": w_ssm_glu, "w_ssm_o": w_ssm_o, "w_mix_o": w_mix_o, "norm_ffn": norm_ffn,
            "w_ffn_in": w_ffn_in, "w_ffn_out": w_ffn_out, "norm_final": norm_final}

def first_block(x, norm_mix, w_in, b_gate, attn_sinks, w_attn_o, conv_w, w_conv_o,
              ssm_a_re, ssm_a_im, ssm_b_re, ssm_b_im, ssm_c_re, ssm_c_im, ssm_d, ssm_log_dt,
              w_ssm_glu, w_ssm_o, w_mix_o, norm_ffn, w_ffn_in, w_ffn_out, norm_final):
    b, l = x.shape[0], x.shape[1]
    cos, sin = rope_tables(l)
    for i in range(DEPTH):
        h = rmsnorm(x, norm_mix[i])
        proj = h @ w_in[i]
        q, k, v, cb, cc, cx, u, g = jnp.split(proj, IN_SPLITS, axis=-1)
        q = partial_rope(q.reshape(b, l, N_Q_HEADS, HEAD_DIM), cos, sin)
        k = partial_rope(k.reshape(b, l, N_KV_HEADS, HEAD_DIM), cos, sin)
        v = v.reshape(b, l, N_KV_HEADS, HEAD_DIM)
        y_attn = sliding_window_attention(q, k, v, attn_sinks[i]) @ w_attn_o[i]
        y_conv = (cb * short_conv(cc * cx, conv_w[i])) @ w_conv_o[i]
        ys = jax.nn.gelu(s5_ssm(u, ssm_a_re[i], ssm_a_im[i], ssm_b_re[i], ssm_b_im[i],
                                ssm_c_re[i], ssm_c_im[i], ssm_d[i], ssm_log_dt[i]))
        y_ssm = (ys * jax.nn.sigmoid(ys @ w_ssm_glu[i])) @ w_ssm_o[i]
        gates = jax.nn.sigmoid(g + b_gate[i]).reshape(b, l, N_BRANCH, D_MODEL)
        merged = gates[:, :, 0] * y_attn + gates[:, :, 1] * y_conv + gates[:, :, 2] * y_ssm
        x = x + merged @ w_mix_o[i]
        h = rmsnorm(x, norm_ffn[i])
        gt, up = jnp.split(h @ w_ffn_in[i], 2, axis=-1)
        x = x + (jax.nn.silu(gt) * up) @ w_ffn_out[i]
    return rmsnorm(x, norm_final)


DEPTH_2 = 1

V_DIM = 2 * HEAD_DIM
N_HEADS = D_MODEL // V_DIM
D_QK = 2 * N_HEADS * HEAD_DIM
D_V = N_HEADS * V_DIM
D_CONV = D_MODEL
CONV_WIDTH_2 = 31
D_FF = 4 * D_MODEL
N_BRANCH_2 = 2
N_MOD = 6
ROPE_THETA_2 = 10000.0
Q_BLOCK = 128
EPS = 1e-6
D_IN = 2 * D_CONV + 2 * D_QK + D_V + N_BRANCH_2 * D_MODEL


def rms_norm(x, g):
    xf = x.astype(jnp.float32)
    y = xf * lax.rsqrt(jnp.mean(xf * xf, axis=-1, keepdims=True) + EPS)
    return (y * g.astype(jnp.float32)).astype(x.dtype)

def layer_norm(x, g, b):
    xf = x.astype(jnp.float32)
    mu = jnp.mean(xf, axis=-1, keepdims=True)
    xc = xf - mu
    y = xc * lax.rsqrt(jnp.mean(xc * xc, axis=-1, keepdims=True) + EPS)
    return (y * g.astype(jnp.float32) + b.astype(jnp.float32)).astype(x.dtype)

def rope(x, pos):
    half = HEAD_DIM // 2
    inv_freq = ROPE_THETA_2 ** (-jnp.arange(0, HEAD_DIM, 2, dtype=jnp.float32) / HEAD_DIM)
    ang = pos.astype(jnp.float32)[:, None] * inv_freq[None, :]
    cos = jnp.cos(ang)[None, :, None, :]
    sin = jnp.sin(ang)[None, :, None, :]
    xf = x.astype(jnp.float32)
    x1, x2 = xf[..., :half], xf[..., half:]
    return jnp.concatenate([x1 * cos - x2 * sin, x2 * cos + x1 * sin], axis=-1).astype(x.dtype)

def lambda_init(layer_idx):
    return 0.8 - 0.6 * math.exp(-0.3 * (layer_idx - 1))

def causal_diff_attention(q1, q2, k1, k2, v, lam):
    B, T, H, Dh = q1.shape
    nb = T // Q_BLOCK
    scale = 1.0 / math.sqrt(HEAD_DIM)
    kpos = jnp.arange(T)

    def to_blocks(q):
        return q.reshape(B, nb, Q_BLOCK, H, Dh).transpose(1, 0, 2, 3, 4)

    def one_block(args):
        i, qb1, qb2 = args
        qpos = i * Q_BLOCK + jnp.arange(Q_BLOCK)
        mask = kpos[None, :] <= qpos[:, None]

        def probs(qb, k):
            s = jnp.einsum('bqhd,bkhd->bhqk', qb, k, preferred_element_type=jnp.float32) * scale
            s = jnp.where(mask[None, None], s, -jnp.inf)
            return jax.nn.softmax(s, axis=-1)

        a = probs(qb1, k1) - lam * probs(qb2, k2)
        return jnp.einsum('bhqk,bkhe->bqhe', a.astype(v.dtype), v)

    out = lax.map(one_block, (jnp.arange(nb), to_blocks(q1), to_blocks(q2)))
    return out.transpose(1, 0, 2, 3, 4).reshape(B, T, H, V_DIM)

def second_inputs(seed: int = 0) -> dict:
    key = jax.random.key(seed)
    ks = jax.random.split(key, 24)
    f32 = jnp.float32
    L = DEPTH_2

    def nrm(k, shape, s):
        return jax.random.normal(k, shape, f32) * s

    def gain(k, shape):
        return 1.0 + 0.02 * jax.random.normal(k, shape, f32)

    return {
        "x": jax.random.normal(ks[0], (BATCH, SEQ, D_MODEL), f32),
        "c": jax.random.normal(ks[1], (BATCH, D_MODEL), f32),
        "w_ada": nrm(ks[2], (L, D_MODEL, N_MOD * D_MODEL), D_MODEL ** -0.5),
        "b_ada": nrm(ks[3], (L, N_MOD * D_MODEL), 0.01),
        "pre_norm1": gain(ks[4], (L, D_MODEL)),
        "post_norm1": gain(ks[5], (L, D_MODEL)),
        "w_in": nrm(ks[6], (L, D_MODEL, D_IN), D_MODEL ** -0.5),
        "conv_w": nrm(ks[7], (L, CONV_WIDTH_2, D_CONV), CONV_WIDTH_2 ** -0.5),
        "conv_b": nrm(ks[8], (L, D_CONV), 0.01),
        "conv_ln_g": gain(ks[9], (L, D_CONV)),
        "conv_ln_b": nrm(ks[10], (L, D_CONV), 0.01),
        "conv_w_out": nrm(ks[11], (L, D_CONV, D_MODEL), D_CONV ** -0.5),
        "conv_b_out": nrm(ks[12], (L, D_MODEL), 0.01),
        "lambda_q1": nrm(ks[13], (L, HEAD_DIM), 0.1),
        "lambda_k1": nrm(ks[14], (L, HEAD_DIM), 0.1),
        "lambda_q2": nrm(ks[15], (L, HEAD_DIM), 0.1),
        "lambda_k2": nrm(ks[16], (L, HEAD_DIM), 0.1),
        "head_norm": gain(ks[17], (L, V_DIM)),
        "w_o": nrm(ks[18], (L, D_MODEL, D_MODEL), D_MODEL ** -0.5),
        "pre_norm2": gain(ks[19], (L, D_MODEL)),
        "post_norm2": gain(ks[20], (L, D_MODEL)),
        "w_ff1": nrm(ks[21], (L, D_MODEL, D_FF), D_MODEL ** -0.5),
        "w_ff2": nrm(ks[22], (L, D_FF, D_MODEL), D_FF ** -0.5),
    }

def second_block(x, c, w_ada, b_ada, pre_norm1, post_norm1, w_in, conv_w, conv_b, conv_ln_g,
              conv_ln_b, conv_w_out, conv_b_out, lambda_q1, lambda_k1, lambda_q2, lambda_k2,
              head_norm, w_o, pre_norm2, post_norm2, w_ff1, w_ff2):
    B, T, _ = x.shape
    pos = jnp.arange(T)
    cs = jax.nn.silu(c)
    for l in range(DEPTH_2):
        mod = (cs @ w_ada[l] + b_ada[l])[:, None, :]
        sh1, sc1, g1, sh2, sc2, g2 = jnp.split(mod, N_MOD, axis=-1)

        h = rms_norm(x, pre_norm1[l]) * (1.0 + sc1) + sh1
        proj = h @ w_in[l]
        o1 = 2 * D_CONV
        o2 = o1 + D_QK
        o3 = o2 + D_QK
        o4 = o3 + D_V
        u_glu, q, k, v, gate_logits = proj[..., :o1], proj[..., o1:o2], proj[..., o2:o3], proj[..., o3:o4], proj[..., o4:]

        ua, ub = jnp.split(u_glu, 2, axis=-1)
        u = ua * jax.nn.sigmoid(ub)
        u = lax.conv_general_dilated(
            u, conv_w[l][:, None, :].astype(u.dtype), window_strides=(1,),
            padding=[(CONV_WIDTH_2 - 1, 0)], dimension_numbers=('NWC', 'WIO', 'NWC'),
            feature_group_count=D_CONV) + conv_b[l]
        u = jax.nn.silu(layer_norm(u, conv_ln_g[l], conv_ln_b[l]))
        y_conv = u @ conv_w_out[l] + conv_b_out[l]

        q = q.reshape(B, T, 2, N_HEADS, HEAD_DIM)
        k = k.reshape(B, T, 2, N_HEADS, HEAD_DIM)
        v = v.reshape(B, T, N_HEADS, V_DIM)
        q1, q2 = rope(q[:, :, 0], pos), rope(q[:, :, 1], pos)
        k1, k2 = rope(k[:, :, 0], pos), rope(k[:, :, 1], pos)
        lam_init = lambda_init(l + 1)
        lam = (jnp.exp(jnp.sum(lambda_q1[l].astype(jnp.float32) * lambda_k1[l].astype(jnp.float32)))
               - jnp.exp(jnp.sum(lambda_q2[l].astype(jnp.float32) * lambda_k2[l].astype(jnp.float32)))
               + lam_init)
        att = causal_diff_attention(q1, q2, k1, k2, v, lam)
        att = rms_norm(att, head_norm[l]) * (1.0 - lam_init)
        y_att = att.reshape(B, T, D_V)

        g_conv, g_att = jnp.split(jax.nn.sigmoid(gate_logits), N_BRANCH_2, axis=-1)
        y = (g_conv * y_conv + g_att * y_att) @ w_o[l]
        x = x + g1 * rms_norm(y, post_norm1[l])

        h = rms_norm(x, pre_norm2[l]) * (1.0 + sc2) + sh2
        f = jnp.square(jax.nn.relu(h @ w_ff1[l])) @ w_ff2[l]
        x = x + g2 * rms_norm(f, post_norm2[l])
    return x


_first_inputs = second_inputs


def second_inputs(seed=0):
    import zlib

    import numpy as np

    out = dict(_first_inputs(seed))
    spreads = {}
    factors = {'b_ada': 3.704,
     'pre_norm1': 5.268,
     'post_norm1': 4.935,
     'conv_b': 30.505,
     'conv_ln_g': 29.883,
     'conv_ln_b': 61.302,
     'conv_b_out': 42.071,
     'lambda_q1': 3.805,
     'lambda_k1': 5.853,
     'lambda_q2': 3.746,
     'lambda_k2': 5.252,
     'head_norm': 27.089,
     'pre_norm2': 18.689,
     'post_norm2': 24.601}
    for name, (base, spread) in spreads.items():
        noise = np.random.default_rng([zlib.crc32(name.encode()), seed]).standard_normal(out[name].shape)
        drawn = base * np.exp(spread * noise) if base else spread * noise
        out[name] = __import__('jax').numpy.asarray(drawn.astype(out[name].dtype))
    for name, factor in factors.items():
        out[name] = (out[name] * factor).astype(out[name].dtype)
    return out


_narrow_inputs = second_inputs


def second_inputs(seed=0):

    out = dict(_narrow_inputs(seed))
    wider = {'conv_ln_g': 4.22,
     'conv_ln_b': 4.24,
     'conv_b_out': 4.23,
     'head_norm': 4.21,
     'post_norm2': 3.41}
    for name, times in wider.items():
        mean = out[name].mean()
        out[name] = (mean + times * (out[name] - mean)).astype(out[name].dtype)
    return out


def setup_inputs(seed=0):
    out = dict(first_inputs(seed))
    for name, value in second_inputs(seed + 1).items():
        if name != "x":
            out[name + "_2"] = value
    return out


def reference(
    x, norm_mix, w_in, b_gate, attn_sinks, w_attn_o, conv_w, w_conv_o, ssm_a_re, ssm_a_im,
    ssm_b_re, ssm_b_im, ssm_c_re, ssm_c_im, ssm_d, ssm_log_dt, w_ssm_glu, w_ssm_o, w_mix_o,
    norm_ffn, w_ffn_in, w_ffn_out, norm_final, c_2, w_ada_2, b_ada_2, pre_norm1_2, post_norm1_2,
    w_in_2, conv_w_2, conv_b_2, conv_ln_g_2, conv_ln_b_2, conv_w_out_2, conv_b_out_2,
    lambda_q1_2, lambda_k1_2, lambda_q2_2, lambda_k2_2, head_norm_2, w_o_2, pre_norm2_2,
    post_norm2_2, w_ff1_2, w_ff2_2,
):
    x = first_block(
        x, norm_mix, w_in, b_gate, attn_sinks, w_attn_o, conv_w, w_conv_o, ssm_a_re, ssm_a_im,
        ssm_b_re, ssm_b_im, ssm_c_re, ssm_c_im, ssm_d, ssm_log_dt, w_ssm_glu, w_ssm_o, w_mix_o,
        norm_ffn, w_ffn_in, w_ffn_out, norm_final,
    )
    return second_block(
        x, c_2, w_ada_2, b_ada_2, pre_norm1_2, post_norm1_2, w_in_2, conv_w_2, conv_b_2,
        conv_ln_g_2, conv_ln_b_2, conv_w_out_2, conv_b_out_2, lambda_q1_2, lambda_k1_2,
        lambda_q2_2, lambda_k2_2, head_norm_2, w_o_2, pre_norm2_2, post_norm2_2, w_ff1_2,
        w_ff2_2,
    )


_drawn_inputs = setup_inputs


def setup_inputs(seed=0):
    import zlib

    import numpy as np

    out = dict(_drawn_inputs(seed))
    spreads = {}
    factors = {'ssm_a_re': 200.0,
     'lambda_q2_2': 8.0,
     'lambda_k2_2': 8.0,
     'b_gate': 4.754,
     'attn_sinks': 3.469,
     'ssm_a_im': 40.224,
     'ssm_b_re': 55.024,
     'ssm_b_im': 55.296,
     'ssm_c_re': 56.288,
     'ssm_c_im': 55.144,
     'ssm_log_dt': 44.096}
    for name, (base, spread) in spreads.items():
        noise = np.random.default_rng([zlib.crc32(name.encode()), seed]).standard_normal(out[name].shape)
        drawn = base * np.exp(spread * noise) if base else spread * noise
        out[name] = __import__('jax').numpy.asarray(drawn.astype(out[name].dtype))
    for name, factor in factors.items():
        out[name] = (out[name] * factor).astype(out[name].dtype)
    return out
```

```python
import concourse.bass as bass
from concourse import mybir
from contextlib import ExitStack, contextmanager
import math

F32 = mybir.dt.float32
F32R = mybir.dt.float32r
ALU = mybir.AluOpType
ACT = mybir.ActivationFunctionType
AX = mybir.AxisListType

P = 128
T = 512
NB = T // P
D = 1024
KD = D // P
DEPTH = 2
EPS = 1e-6
UNIT = 1024
SLOTS = 4
AHEAD = SLOTS - 1

NQ, NKV, HD = 8, 2, 64
GROUP = NQ // NKV
CONV_K = 3
SSM_PAIRS = 16
FFN = 2816
CHUNKS1 = FFN // 256

HEADS2, VD = 8, 128
TAPS = 31
PAD = TAPS - 1
FF2 = 4096
CHUNKS2 = FF2 // 256
LAM_INIT = 0.8 - 0.6 * math.exp(-0.3 * 0)

IN_U, IN_K, IN_V, IN_Q, IN_CB, IN_CC, IN_CX, IN_G = 2304, 512, 640, 0, 768, 1280, 1792, 2816

P1 = {}
_at = 0
for _n, _w in (("norm_mix", 8), ("norm_ffn", 8), ("b_gate", 24), ("conv_w", 12), ("ssm_d", 4), ("a_re", 16),
               ("a_im", 16), ("log_dt", 16), ("sinks", 8)):
    P1[_n] = (_at, _at + _w)
    _at += _w
NP1 = _at
P2 = {}
_at = 0
for _n, _w in (("norm_final", 8), ("c", 8), ("b_ada", 48), ("pre_norm1", 8), ("post_norm1", 8),
               ("conv_b", 8), ("conv_ln_g", 8), ("conv_ln_b", 8), ("conv_b_out", 8), ("head_norm", 1),
               ("pre_norm2", 8), ("post_norm2", 8), ("conv_w", 248), ("lambdas", 256)):
    P2[_n] = (_at, _at + _w)
    _at += _w
NP2 = _at
NP2_COLS = P2["conv_w"][0]
CONST = {}
_at = 0
for _n, _w in (("ident", 128), ("rot1", 128), ("rot2", 128), ("band", 256), ("t", 512), ("cos1", 512), ("sin1", 512),
               ("cos2", 512), ("sin2", 512)):
    CONST[_n] = (_at, _at + _w)
    _at += _w
NCONST = _at

ROUND = 1.5 * 2.0 ** 23
TWO_PI = 2.0 * math.pi
TURN = 6.2831845
PI_HI, PI_MID, PI_LO = 6.28125, 0.0019350051879882812, 3.019916050988e-07


class Count:

    def __init__(self, eng, sem):
        self.eng, self.sem, self.base, self.k = eng, sem, 0, 0

    def done(self, ins):
        ins.then_inc(self.sem, 1)
        self.k += 1
        self.eng.wait_ge(self.sem, self.base + self.k)


@contextmanager
def rounds(eng, n, counts):
    start = {c: c.k for c in counts}
    with eng.Fori(0, n) as i:
        for c, per in counts.items():
            c.base, c.k = start[c] + i * per, 0
        yield i
        for c, per in counts.items():
            assert c.k == per, (c.sem, c.k, per)
    for c, per in counts.items():
        c.base, c.k = 0, start[c] + n * per


def build(nc, d):
    with ExitStack() as top:
        def sb(stack, name, shape, dt=F32):
            return stack.enter_context(nc.sbuf_tensor("sb_" + name, shape, dt))

        all_sems = []

        def sem(name):
            s = top.enter_context(nc.semaphore(name))
            all_sems.append(s)
            return s

        x = sb(top, "x", [P, KD, T])
        raw = sb(top, "raw", [P, SLOTS, UNIT])
        w_hi = sb(top, "w_hi", [P, SLOTS, UNIT], F32R)
        w_lo = sb(top, "w_lo", [P, SLOTS, UNIT], F32R)
        ident = sb(top, "ident", [P, P])
        band = sb(top, "band", [P, 2 * P])
        ones = sb(top, "ones", [P, 2])
        neg_half = sb(top, "neg_half", [P, 32])
        rstd = sb(top, "rstd", [P, 32])
        mod_t = sb(top, "mod", [P, 48])
        mod = mod_t[:, :]
        ps = top.enter_context(nc.psum_tensor("ps", [P, 8, T], F32))

        raw_in = [sem(f"raw_in{s}") for s in range(SLOTS)]
        hi_done = [sem(f"hi_done{s}") for s in range(SLOTS)]
        lo_done = [sem(f"lo_done{s}") for s in range(SLOTS)]
        used = [sem(f"used{s}") for s in range(SLOTS)]
        acc_free = [sem(f"acc_free{a}") for a in range(2)]
        small_in = sem("small_in")
        dve_step = sem("dve_step")
        act_step = sem("act_step")
        squares = sem("squares")
        sums_done = sem("sums_done")
        mean_done = sem("mean_done")
        rstd_done = sem("rstd_done")
        spread = sem("spread")
        normed = sem("normed")
        h_hi_done = sem("h_hi_done")
        h_lo_done = sem("h_lo_done")

        def phase_end():
            nc.all_engine_barrier()
            nums = sorted(s.num for s in all_sems)
            assert nums == list(range(nums[0], nums[-1] + 1))
            nc.sync.sem_clear(range(nums[0], nums[-1] + 1))
            nc.all_engine_barrier()

        def place(u, turn0):
            return u % SLOTS, turn0 + u // SLOTS

        def load_unit(sp, u, src, turn0=0):
            s, turn = place(u, turn0)
            if not (isinstance(turn, int) and turn == 0):
                sp.wait_ge(lo_done[s], turn)
            k, n = src.shape[0] // P, src.shape[1]
            dst = raw[:, s, :].rearrange("p (k n) -> p k n", k=k)
            assert k * n == UNIT
            sp.dma_start(dst, src.rearrange("(k p) n -> p k n", p=P)).then_inc(raw_in[s], 16)

        def round_unit(act, u, turn0=0):
            s, turn = place(u, turn0)
            act.wait_ge(raw_in[s], 16 * (turn + 1))
            if not (isinstance(turn, int) and turn == 0):
                act.wait_ge(used[s], turn)
            act.activation(w_hi[:, s, :], raw[:, s, :], ACT.Copy).then_inc(hi_done[s], 1)

        def rest_unit(pool, u, turn0=0):
            s, turn = place(u, turn0)
            pool.wait_ge(hi_done[s], turn + 1)
            pool.tensor_tensor(w_lo[:, s, :], raw[:, s, :], w_hi[:, s, :].bitcast(F32), ALU.subtract)\
                .then_inc(lo_done[s], 1)

        def multiply_unit(pe, u, outs, rhs, first, last, turn0=0):
            s, turn = place(u, turn0)
            pe.wait_ge(lo_done[s], turn + 1)
            n = len(outs) * P
            for o, out in enumerate(outs):
                for i, (hi, lo) in enumerate(rhs):
                    at = i * n + o * P
                    wh, wl = w_hi[:, s, at:at + P], w_lo[:, s, at:at + P]
                    pe.matmul(out, wh, hi, start=first and i == 0, stop=False)
                    pe.matmul(out, wh, lo, start=False, stop=False)
                    ins = pe.matmul(out, wl, hi, start=False, stop=last and i == len(rhs) - 1)
            ins.then_inc(used[s], 1)

        def multiplied(eng, u, turn0=0):
            s, turn = place(u, turn0)
            eng.wait_ge(used[s], turn + 1)

        def act_squares(act, src, sq):
            for kt in range(KD):
                act.activation(sq[:, kt, :], src[:, kt, :], ACT.Square).then_inc(squares, 1)

        def pe_sum(pe, sq, bank, before=None, n_sq=KD):
            if before is not None:
                pe.wait_ge(squares, before + n_sq)
            for n in range(NB):
                for kt in range(n_sq):
                    ins = pe.matmul(ps[:, bank, n:n + 1], sq[:, kt, n * P:(n + 1) * P], ones[:, 0:1],
                                    start=kt == 0, stop=kt == n_sq - 1)
            ins.then_inc(sums_done, 1)

        def dve_mean(dve, bank, turn, c_mean, width=NB, div=D):
            dve.wait_ge(sums_done, turn + 1)
            c_mean.done(dve.tensor_scalar(rstd[:, 0:width], ps[:, bank, 0:width], 1.0 / div, EPS, ALU.mult, ALU.add))

        def pool_rsqrt(pool, turn, width=NB):
            pool.wait_ge(mean_done, turn + 1)
            pool.tensor_tensor(rstd[:, 0:width], rstd[:, 0:width], neg_half[:, 0:width], ALU.pow).then_inc(rstd_done, 1)

        def pe_spread(pe, src, bank, sem_in, turn):
            pe.wait_ge(sem_in, turn + 1)
            for n in range(NB):
                ins = pe.matmul(ps[:, bank, n * P:(n + 1) * P], src[:, n:n + 1].to_broadcast([P, P]), ident[:, :],
                                start=True, stop=True)
            ins.then_inc(spread, 1)

        SUM_BANK, SPREAD_BANK = 7, 6

        def pe_norm(pe, sq, turn=0):
            pe_sum(pe, sq, SUM_BANK, turn * KD)
            pe_spread(pe, rstd, SPREAD_BANK, rstd_done, turn)

        with nc.Block() as block:
            @block.sync
            def _(sp):
                sp.dma_start(x[:, :, :], d["xT"].rearrange("(k p) t -> p k t", p=P)).then_inc(small_in, 16)
                for t, n in ((ident, "ident"), (band, "band")):
                    sp.dma_start(t[:, :], d["const"][:, CONST[n][0]:CONST[n][1]]).then_inc(small_in, 16)
                sp.wait_ge(small_in, 48)

            @block.vector
            def _(dve):
                c = Count(dve, dve_step)
                c.done(dve.memset(ones[:, :], 1.0))
                c.done(dve.memset(neg_half[:, :], -0.5))
        phase_end()

        def order1():
            groups = [("u", 0), ("u", 1), ("kv", 0), ("q", 0), ("q", 1)]
            for p in range(2):
                groups += [("cc", p), ("cx", p), ("cb", p)]
            for p in range(4):
                groups += [("gc", p), ("co", p)]
            for name, n in (("ga", 4), ("gs", 4), ("ao", 4), ("gl", 2), ("so", 4), ("mx", 4)):
                groups += [(name, p) for p in range(n)]
            return groups

        G1 = order1()
        HALF = {"co", "ao", "gl", "so"}
        START1 = []
        n_units = 0
        for name, _p in G1:
            START1.append(n_units)
            n_units += 1 if name in HALF else 2
        UNITS1 = n_units
        at1 = {g: i for i, g in enumerate(G1)}
        SSM_AT = 2
        ATT_AT = at1[("co", 3)]
        ITEMS = [(n, g) for n in range(NB) for g in range(NKV)]

        bu_full = sem("bu_full")
        bu_free = sem("bu_free")
        ssm_x = sem("ssm_x")
        ssm_y = sem("ssm_y")
        ssm_y_free = sem("ssm_y_free")
        arg_done = sem("arg_done")
        frac_done = sem("frac_done")
        trig_done = sem("trig_done")
        par_act = sem("par_act")
        par_dve = sem("par_dve")
        gelu_in = sem("gelu_in")
        gelu_th = sem("gelu_th")
        ys_done = sem("ys_done")
        c7_full = sem("c7_full")
        c7_free = sem("c7_free")
        kdup = sem("kdup")
        prod_ready = sem("prod_ready")
        prod_hi = sem("prod_hi")
        prod_lo = sem("prod_lo")
        s_full = sem("s_full")
        s_max = sem("s_max")
        s_exp = sem("s_exp")
        p_ready = sem("p_ready")
        pt_full = sem("pt_full")
        pt_done = sem("pt_done")
        o_full = sem("o_full")
        o_hi = sem("o_hi")
        o_lo = sem("o_lo")
        out_done = sem("out_done")
        gt_free = sem("gt_free")
        up_free = sem("up_free")
        th_done = sem("th_done")
        hid_hi_done = sem("hid_hi_done")
        hid_lo_done = sem("hid_lo_done")
        down_free = sem("down_free")
        x_done = sem("x_done")
        spilled = sem("spilled")
        clipped = sem("clipped")
        rstd_kept = sem("rstd_kept")
        x_back = sem("x_back")
        heads_done = sem("heads_done")
        exps_done = sem("exps_done")
        vt_full = sem("vt_full")
        vt_done = sem("vt_done")
        conv_done = sem("conv_done")
        centred = sem("centred")
        ln_ready = sem("ln_ready")
        ln_th = sem("ln_th")
        ln_mean = sem("ln_mean")
        glu_done = sem("glu_done")
        spill = nc.dram_tensor("x_spill", (P, KD * T), F32, kind="Internal").ap()

        def mixer1(l):
            with ExitStack() as st:
                h_hi = sb(st, "h_hi", [P, KD, T], F32R)
                h_lo = sb(st, "h_lo", [P, KD, T], F32R)
                s_hi = sb(st, "s_hi", [P, 4, T], F32R)
                s_lo = sb(st, "s_lo", [P, 4, T], F32R)
                m = sb(st, "m", [P, KD, T])
                ga = sb(st, "ga", [P, KD, T])
                gs = sb(st, "gs", [P, KD, T])
                u = sb(st, "u", [P, 4, T])
                q = sb(st, "q", [P, 4, T])
                k = sb(st, "k", [P, 2, T])
                vtok = sb(st, "vtok", [P, NB, P])
                trig = sb(st, "trig", [P, 2, 2 * T])
                bT = sb(st, "bT", [P, 2, 4, P])
                cT = sb(st, "cT", [P, 2, 4, P])
                par = sb(st, "par", [P, NP1])
                rot = sb(st, "rot", [P, P])
                trow = sb(st, "trow", [P, T])
                sin_t = sb(st, "sin_t", [P, T])
                col = sb(st, "col", [P, 16, 16])
                bias = sb(st, "bias", [P, 32])
                att = sb(st, "att", [P, 6, 4])
                z = m[:, 0:3, :].rearrange("p a t -> p (a t)")[:, 0:2 * (T + 2)].rearrange("p (a t) -> p a t", a=2)
                conv = m[:, 3:5, :]
                cc = m[:, 5:7, :]
                cos_t = m[:, 7, :]
                t1, t2, v1, v2 = (ga[:, i, :] for i in range(4))
                arg, argr = (ga[:, i:i + 2, :].rearrange("p a t -> p (a t)") for i in (4, 6))
                xo = gs[:, 0:4, :].rearrange("p (b a) t -> p b a t", b=2)
                gconv, vT, yw = gs[:, 4:6, :], gs[:, 6, :], gs[:, 7, :]
                sc = trig[:, 0, :].rearrange("p (h k) -> p h k", h=4)
                pt = trig[:, 1, :].rearrange("p (h b q) -> p h b q", h=4, b=2)

                def pcol(name, i, w=1):
                    return par[:, P1[name][0] + i:P1[name][0] + i + w]

                def banks(gi):
                    a = gi % 2
                    return ps[:, 2 * a:2 * a + 2, :]

                def full(eng, gi):
                    multiplied(eng, START1[gi] + (0 if G1[gi][0] in HALF else 1))

                def emptied(eng, gi):
                    eng.wait_ge(acc_free[gi % 2], gi // 2 + 1)

                DT, RD, TH, MAG, NN, TAU, PHC, SN, CS, LR, DEN, FR, FI, TA, TB = (col[:, i, :] for i in range(15))

                with nc.Block() as block:
                    @block.sync
                    def _(sp):
                        for t, src in ((par[:, :], d["par1"][l, :, :]), (rot[:, :], d["const"][:, CONST["rot1"][0]:CONST["rot1"][1]]),
                                       (trow[:, :], d["const"][:, CONST["t"][0]:CONST["t"][1]]),
                                       (cos_t, d["const"][:, CONST["cos1"][0]:CONST["cos1"][1]]),
                                       (sin_t[:, :], d["const"][:, CONST["sin1"][0]:CONST["sin1"][1]]),
                                       (bT[:, :, :, :], d["bT"][l, :, :, :, :]), (cT[:, :, :, :], d["cT"][l, :, :, :, :])):
                            sp.dma_start(t, src).then_inc(small_in, 16)
                        win = d["w_in"]
                        for gi, (name, p) in enumerate(G1):
                            def unit(w, k0, cols):
                                load_unit(sp, START1[gi] + k0, w[l, k0 * 512:k0 * 512 + 512, cols:cols + 256])
                            if name in ("ao", "co", "so", "gl"):
                                unit(d[{"ao": "w_attn_o", "co": "w_conv_o", "so": "w_ssm_o", "gl": "w_ssm_glu"}[name]],
                                     0, 256 * p)
                            elif name == "mx":
                                unit(d["w_mix_o"], 0, 256 * p)
                                unit(d["w_mix_o"], 1, 256 * p)
                            else:
                                at = {"u": IN_U, "kv": IN_K, "q": IN_Q, "cc": IN_CC, "cx": IN_CX, "cb": IN_CB,
                                      "gc": IN_G + D, "ga": IN_G, "gs": IN_G + 2 * D}[name] + 256 * p
                                unit(win, 0, at)
                                unit(win, 1, at)

                    @block.gpsimd
                    def _(pool):
                        for un in range(UNITS1):
                            if un == 2:
                                pool_rsqrt(pool, 0)
                            rest_unit(pool, un)

                    @block.tensor
                    def _(pe):
                        pe_norm(pe, ga)
                        b7 = iter(range(6))

                        def rotate(src):
                            i = next(b7)
                            if i:
                                pe.wait_ge(c7_free, i)
                            pe.matmul(ps[:, 7, :], rot[:, :], src, start=True, stop=True).then_inc(c7_full, 1)

                        def inputs(s):
                            ct, j = s // 4, s % 4
                            r = slice(32 * j, 32 * j + 32)
                            if s:
                                pe.wait_ge(bu_free, s)
                            for part in range(2):
                                ins = pe.matmul(ps[:, 4 + part, :], bT[r, part, ct, :], u[r, ct, :], start=True, stop=True)
                            ins.then_inc(bu_full, 1)

                        def outputs(s):
                            ct, j = s // 4, s % 4
                            r = slice(32 * j, 32 * j + 32)
                            pe.wait_ge(ssm_x, s + 1)
                            if j == 0 and ct:
                                pe.wait_ge(ssm_y_free, ct)
                            pe.matmul(ps[r, 6, :], cT[:, 0, ct, r], xo[:, s % 2, 0, :], start=True, stop=False)
                            pe.matmul(ps[r, 6, :], cT[:, 1, ct, r], xo[:, s % 2, 1, :], start=False, stop=True)\
                                .then_inc(ssm_y, 1)

                        def scores(a):
                            n, g = ITEMS[a]
                            if a:
                                pe.wait_ge(s_max, 2 * a - 1)
                            lo = 0 if n else P
                            for hh in range(GROUP):
                                h = GROUP * g + hh
                                r = slice(64 * (h % 2), 64 * (h % 2) + 64)
                                out = ps[:, 4 + hh % 2, (hh // 2) * 256 + lo:(hh // 2) * 256 + 256]
                                ins = pe.matmul(out, q[r, h // 2, n * P:(n + 1) * P],
                                                k[r, g, (n - 1) * P + lo:(n + 1) * P], start=True, stop=True)
                            ins.then_inc(s_full, 1)

                        def probs(a):
                            n, g = ITEMS[a]
                            pe.wait_ge(p_ready, a + 1)
                            if a:
                                pe.wait_ge(o_lo, a)
                            else:
                                pe.wait_ge(ssm_y_free, 4)
                            for hh in range(GROUP):
                                for b in range(0 if n else 1, 2):
                                    at = (hh * 2 + b) * P
                                    ins = pe.transpose(ps[:, 6 + at // T, at % T:at % T + P],
                                                       sc[:, hh, b * P:(b + 1) * P], ident[:, :])
                            ins.then_inc(pt_full, 1)

                        def values(a):
                            n, g = ITEMS[a]
                            pe.wait_ge(pt_done, a + 1)
                            for hh in range(GROUP):
                                for b in range(0 if n else 1, 2):
                                    half, tile = hh // 2, hh % 2
                                    r = slice(64 * half, 64 * half + 64)
                                    ins = pe.matmul(ps[r, 6, tile * P:(tile + 1) * P],
                                                    vtok[:, n - 1 + b, 64 * g:64 * g + 64], pt[:, hh, b, :],
                                                    start=b == (0 if n else 1), stop=b == 1)
                            ins.then_inc(o_full, 1)

                        for gi, (name, p) in enumerate(G1):
                            s = gi - SSM_AT
                            a = gi - ATT_AT
                            if s == 0:
                                pe.wait_ge(small_in, 7 * 16)
                                emptied(pe, 1)
                                inputs(0)
                            if 1 <= a <= 8:
                                probs(a - 1)
                            if 0 <= a < 8:
                                if a == 0:
                                    pe.wait_ge(kdup, 32)
                                    pe.wait_ge(c7_free, 6)
                                    pe.wait_ge(bu_free, 16)
                                scores(a)
                            if gi >= 2:
                                emptied(pe, gi - 2)
                            outs = [banks(gi)[:, 0, :], banks(gi)[:, 1, :]]
                            n_u = 1 if name in HALF else 2
                            if name in ("co", "ao", "so"):
                                if name == "co":
                                    pe.wait_ge(prod_lo, 2)
                                elif name == "ao":
                                    pe.wait_ge(o_lo, 8)
                                else:
                                    pe.wait_ge(prod_lo, 5)
                                src = [(s_hi[:, i, :], s_lo[:, i, :]) for i in range(4)]
                            elif name == "gl":
                                pe.wait_ge(prod_lo, 3)
                                src = [(h_hi[:, i, :], h_lo[:, i, :]) for i in range(4)]
                            elif name == "mx":
                                src = [(h_hi[:, i, :], h_lo[:, i, :]) for i in range(8)]
                            else:
                                src = [(h_hi[:, i, :], h_lo[:, i, :]) for i in range(8)]
                            for i in range(n_u):
                                if gi == 0:
                                    pe.wait_ge(h_lo_done, 4 * i + 4)
                                if name == "mx":
                                    pe.wait_ge(prod_lo, 5 + 2 * i + 2)
                                multiply_unit(pe, START1[gi] + i, outs, src[4 * i:4 * i + 4], i == 0, i == n_u - 1)
                                if i == 0 and 1 <= a <= 8:
                                    values(a - 1)
                            if 0 <= s:
                                if s + 1 < SSM_PAIRS:
                                    inputs(s + 1)
                                if 1 <= s <= SSM_PAIRS:
                                    outputs(s - 1)
                            if gi == 3:
                                emptied(pe, 2)
                                rotate(k[:, 0, :])
                            if gi == 4:
                                next(b7)
                                pe.wait_ge(c7_free, 1)
                                for n in range(NB):
                                    ins = pe.transpose(ps[:, 7, n * P:(n + 1) * P], vT[:, n * P:(n + 1) * P], ident[:, :])
                                ins.then_inc(c7_full, 1)
                            if 5 <= gi <= 8:
                                if gi == 5:
                                    emptied(pe, 3)
                                    emptied(pe, 4)
                                rotate(q[:, gi - 5, :])

                    @block.scalar
                    def _(act):
                        step = Count(act, act_step)
                        ahead = [0]

                        def prefetch(n):
                            while ahead[0] < min(n, UNITS1):
                                round_unit(act, ahead[0])
                                ahead[0] += 1

                        prefetch(SLOTS)
                        act_squares(act, x, ga)
                        pa = Count(act, par_act)
                        act.wait_ge(small_in, 7 * 16)
                        pa.done(act.activation(DT, pcol("log_dt", 0, 16), ACT.Exp))
                        act.wait_ge(par_dve, 1)
                        pa.done(act.activation(MAG, RD, ACT.Exp))
                        for kt in range(KD):
                            act.wait_ge(normed, kt + 1)
                            act.activation(h_hi[:, kt, :], ga[:, kt, :], ACT.Copy).then_inc(h_hi_done, 1)
                        act.wait_ge(par_dve, 2)
                        pa.done(act.activation(SN, TAU, ACT.Sin, scale=TURN))
                        pa.done(act.activation(CS, PHC, ACT.Sin, scale=-TURN))

                        args = Count(act, arg_done)
                        trigs = Count(act, trig_done)

                        def angles(s):
                            if s:
                                act.wait_ge(frac_done, s)
                            step.done(act.activation(arg[:, 0:T], trow[:, :], ACT.Copy, scale=TAU[:, s:s + 1]))
                            step.done(act.activation(arg[:, T:2 * T], trow[:, :], ACT.Identity, scale=TAU[:, s:s + 1],
                                                     bias=bias[:, 25:26]))
                            args.done(act.activation(argr[:, :], arg[:, :], ACT.Identity, bias=bias[:, 24:25]))

                        def sines(s):
                            act.wait_ge(frac_done, s + 1)
                            if s >= 2:
                                act.wait_ge(ssm_x, s - 1)
                            trigs.done(act.activation(trig[:, s % 2, :], arg[:, :], ACT.Sin, scale=-TURN))

                        def exps(a):
                            n, g = ITEMS[a]
                            lo = 0 if n else P
                            act.wait_ge(s_max, 2 * a + 2)
                            step.done(act.activation(att[:, 3, :], att[:, 2, :], ACT.Exp))
                            for hh in range(GROUP):
                                ins = act.activation(sc[:, hh, lo:], sc[:, hh, lo:], ACT.Exp, bias=att[:, 1, hh:hh + 1],
                                                     accum_out=att[:, 4, hh:hh + 1])
                                if hh == GROUP - 1:
                                    ins.then_inc(s_exp, 1)
                                else:
                                    step.done(ins)

                        def pt_copy(a):
                            act.wait_ge(pt_full, a + 1)
                            n, g = ITEMS[a]
                            src = ps[:, 6:8, :].rearrange("p a (h b q) -> p (a h) b q", b=2, q=P)
                            b0 = 0 if n else 1
                            act.activation(pt[:, :, b0:, :], src[:, :, b0:, :], ACT.Copy).then_inc(pt_done, 1)

                        def o_round(a):
                            n, g = ITEMS[a]
                            act.wait_ge(o_full, a + 1)
                            act.activation(s_hi[:, 2 * g:2 * g + 2, n * P:(n + 1) * P],
                                           ps[:, 6, 0:2 * P].rearrange("p (a q) -> p a q", a=2), ACT.Copy)\
                                .then_inc(o_hi, 1)

                        n_prod = [0]

                        def prod_round(dst, src, scale, wait=True):
                            if wait:
                                n_prod[0] += 1
                                act.wait_ge(prod_ready, n_prod[0])
                            act.activation(dst, src, ACT.Copy, scale=scale).then_inc(prod_hi, 1)

                        act.wait_ge(par_dve, 3)
                        for gi, (name, p) in enumerate(G1):
                            s = gi - SSM_AT
                            a = gi - ATT_AT
                            two = slice(2 * p, 2 * p + 2)
                            done = acc_free[gi % 2]
                            if 1 <= a <= 8:
                                pt_copy(a - 1)
                            if gi == 0:
                                angles(0)
                                sines(0)
                                angles(1)
                            if s in (6, 10, 14, 18):
                                act.wait_ge(gelu_in, (s - 2) // 4)
                                act.activation(yw, yw, ACT.Tanh, scale=math.sqrt(2 / math.pi)).then_inc(gelu_th, 1)
                            if 0 <= s and s + 1 < SSM_PAIRS:
                                sines(s + 1)
                                if s + 2 < SSM_PAIRS:
                                    angles(s + 2)
                            prefetch(START1[gi] + 1 + AHEAD)
                            if 0 <= a < 8:
                                exps(a)
                            if 1 <= a <= 8:
                                o_round(a - 1)
                            if gi == 5:
                                act.wait_ge(c7_free, 1)
                                act.dma_start(k[64:128, 0, :], k[0:64, 0, :]).then_inc(kdup, 16)
                                act.dma_start(k[0:64, 1, :], k[64:128, 1, :]).then_inc(kdup, 16)
                            if name == "ao" and p == 1:
                                act.wait_ge(ys_done, 4)
                                prod_round(h_hi[:, 0:4, :], u[:, :, :], 0.5, wait=False)
                            if name not in HALF:
                                prefetch(START1[gi] + 2 + AHEAD)
                            src = banks(gi)
                            if name in ("u", "q", "cc", "kv"):
                                full(act, gi)
                                if name == "kv":
                                    step.done(act.activation(k[:, 0, :], src[:, 0, :], ACT.Copy))
                                    act.activation(vT, src[:, 1, :], ACT.Copy).then_inc(done, 1)
                                else:
                                    if name == "cc" and p == 1:
                                        emptied(act, at1[("cx", 0)])
                                    dst = {"u": u, "q": q}[name][:, two, :] if name != "cc" else cc
                                    act.activation(dst, src, ACT.Copy).then_inc(done, 1)
                            elif name in ("gc", "ga", "gs"):
                                full(act, gi)
                                dst = {"gc": gconv, "ga": ga[:, two, :], "gs": gs[:, two, :]}[name]
                                if name == "gc" and p:
                                    emptied(act, gi - 1)
                                if name == "ga" and p == 0:
                                    act.wait_ge(ssm_x, SSM_PAIRS)
                                if name == "gs" and p == 0:
                                    act.wait_ge(ssm_y, SSM_PAIRS)
                                    emptied(act, at1[("co", 3)])
                                    act.wait_ge(ys_done, 4)
                                b = {"ga": 0, "gc": 8, "gs": 16}[name] + 2 * p
                                step.done(act.activation(dst[:, 0, :], src[:, 0, :], ACT.Tanh, scale=0.5,
                                                         bias=bias[:, b:b + 1]))
                                act.activation(dst[:, 1, :], src[:, 1, :], ACT.Tanh, scale=0.5,
                                               bias=bias[:, b + 1:b + 2]).then_inc(done, 1)
                            elif name == "cb":
                                emptied(act, gi)
                                prod_round(s_hi[:, two, :], conv, 1.0, wait=False)
                            elif name == "gl":
                                full(act, gi)
                                if p:
                                    act.wait_ge(prod_ready, 1)
                                act.activation(q[:, 0:2, :], src, ACT.Tanh, scale=0.5).then_inc(done, 1)
                                prod_round(s_hi[:, two, :], q[:, 2:4, :], 0.25)
                            elif name == "so":
                                prod_round(h_hi[:, two, :], m[:, two, :], 0.5)

                    @block.vector
                    def _(dve):
                        step = Count(dve, dve_step)
                        tt, ts, stt = dve.tensor_tensor, dve.tensor_scalar, dve.scalar_tensor_tensor
                        pd = Count(dve, par_dve)
                        dve.wait_ge(small_in, 7 * 16)
                        step.done(ts(bias[:, 0:24], pcol("b_gate", 0, 24), 0.5, None, ALU.mult))
                        step.done(dve.memset(bias[:, 24:25], ROUND))
                        step.done(dve.memset(bias[:, 25:26], 0.25))
                        dve.wait_ge(par_act, 1)
                        a_re, a_im = pcol("a_re", 0, 16), pcol("a_im", 0, 16)
                        step.done(tt(TH, a_im, DT, ALU.mult))
                        pd.done(tt(RD, a_re, DT, ALU.mult))
                        step.done(ts(NN, TH, 1.0 / TWO_PI, ROUND, ALU.mult, ALU.add))
                        step.done(ts(NN, NN, ROUND, None, ALU.subtract))
                        for c in (PI_HI, PI_MID, PI_LO):
                            step.done(stt(TH, NN, -c, TH, ALU.mult, ALU.add))
                        step.done(ts(TH, TH, 1.0 / TWO_PI, 0.5, ALU.mult, ALU.min))
                        step.done(ts(TAU, TH, -0.5, None, ALU.max))
                        step.done(ts(TA, TAU, 0.25, None, ALU.add))
                        step.done(ts(TB, TA, ROUND, None, ALU.add))
                        pd.done(stt(PHC, TB, ROUND, TA, ALU.subtract, ALU.subtract))

                        cm = Count(dve, mean_done)
                        dve_mean(dve, SUM_BANK, 0, cm)
                        dve.wait_ge(spread, 1)
                        nd = Count(dve, normed)
                        for kt in range(KD + 1):
                            if kt < KD:
                                nd.done(stt(ga[:, kt, :], x[:, kt, :], pcol("norm_mix", kt), ps[:, SPREAD_BANK, :],
                                            ALU.mult, ALU.mult))
                            if kt:
                                dve.wait_ge(h_hi_done, kt)
                                tt(h_lo[:, kt - 1, :], ga[:, kt - 1, :], h_hi[:, kt - 1, :].bitcast(F32), ALU.subtract)\
                                    .then_inc(h_lo_done, 1)
                        dve.wait_ge(h_lo_done, KD)

                        dve.wait_ge(par_act, 4)
                        step.done(tt(TA, MAG, CS, ALU.mult))
                        step.done(ts(LR, TA, -1.0, None, ALU.add))
                        step.done(tt(TB, MAG, SN, ALU.mult))
                        step.done(tt(DEN, a_re, a_re, ALU.mult))
                        step.done(tt(TA, a_im, a_im, ALU.mult))
                        step.done(tt(DEN, DEN, TA, ALU.add))
                        step.done(dve.reciprocal(DEN, DEN))
                        step.done(tt(FR, LR, a_re, ALU.mult))
                        step.done(tt(TA, TB, a_im, ALU.mult))
                        step.done(tt(FR, FR, TA, ALU.add))
                        step.done(tt(FR, FR, DEN, ALU.mult))
                        step.done(tt(FI, TB, a_re, ALU.mult))
                        step.done(tt(TA, LR, a_im, ALU.mult))
                        step.done(tt(FI, FI, TA, ALU.subtract))
                        step.done(tt(FI, FI, DEN, ALU.mult))

                        def by_pair(ap):
                            return ap.rearrange("p c (j h) -> p (c j) h", j=4)

                        def flat(ap):
                            return ap.rearrange("p (s h) -> p s h", h=32)

                        c_re, c_im = by_pair(cT[:, 0, :, :]), by_pair(cT[:, 1, :, :])
                        f_re = FR.unsqueeze(2).to_broadcast([P, 16, 32])
                        f_im = FI.unsqueeze(2).to_broadcast([P, 16, 32])
                        step.done(tt(flat(t1), c_re, f_re, ALU.mult))
                        step.done(tt(flat(t2), c_im, f_im, ALU.mult))
                        step.done(tt(flat(v1), c_re, f_im, ALU.mult))
                        step.done(tt(flat(v2), c_im, f_re, ALU.mult))
                        step.done(tt(c_re, flat(t1), flat(t2), ALU.subtract))
                        step.done(stt(c_im, flat(v1), -1.0, flat(v2), ALU.mult, ALU.subtract))
                        pd.done(dve.memset(z[:, :, 0:2], 0.0))

                        n_prod = [0]
                        pr = Count(dve, prod_ready)
                        pl = Count(dve, prod_lo)

                        def prod_rest(dst_lo, dst_hi, src, scale):
                            n_prod[0] += 1
                            dve.wait_ge(prod_hi, n_prod[0])
                            if scale == 1.0:
                                pl.done(tt(dst_lo, src, dst_hi.bitcast(F32), ALU.subtract))
                            else:
                                pl.done(stt(dst_lo, src, scale, dst_hi.bitcast(F32), ALU.mult, ALU.subtract))

                        fr = Count(dve, frac_done)

                        def fractions(s):
                            dve.wait_ge(arg_done, s + 1)
                            fr.done(stt(arg, argr, ROUND, arg, ALU.subtract, ALU.subtract))

                        bf = Count(dve, bu_free)
                        sx = Count(dve, ssm_x)

                        def states(s):
                            dve.wait_ge(trig_done, s + 1)
                            dve.wait_ge(bu_full, s + 1)
                            sin, cos = trig[:, s % 2, 0:T], trig[:, s % 2, T:2 * T]
                            b_re, b_im = ps[:, 4, :], ps[:, 5, :]
                            step.done(tt(t1, b_re, cos, ALU.mult))
                            step.done(tt(t2, b_im, sin, ALU.mult))
                            step.done(tt(v1, t1, t2, ALU.add))
                            step.done(tt(t1, b_im, cos, ALU.mult))
                            bf.done(tt(t2, b_re, sin, ALU.mult))
                            step.done(tt(v2, t1, t2, ALU.subtract))
                            mag = MAG[:, s:s + 1].to_broadcast([P, T])
                            step.done(dve.tensor_tensor_scan(t1, mag, v1, 0.0, ALU.mult, ALU.add))
                            step.done(dve.tensor_tensor_scan(t2, mag, v2, 0.0, ALU.mult, ALU.add))
                            step.done(tt(v1, t1, cos, ALU.mult))
                            step.done(tt(v2, t2, sin, ALU.mult))
                            if s >= 2:
                                dve.wait_ge(ssm_y, s - 1)
                            step.done(tt(xo[:, s % 2, 0, :], v1, v2, ALU.subtract))
                            step.done(tt(v1, t1, sin, ALU.mult))
                            step.done(tt(v2, t2, cos, ALU.mult))
                            sx.done(tt(xo[:, s % 2, 1, :], v1, v2, ALU.add))

                        yf = Count(dve, ssm_y_free)
                        gi_in = Count(dve, gelu_in)
                        yd = Count(dve, ys_done)

                        def gelu_start(ct):
                            dve.wait_ge(ssm_y, 4 * ct + 4)
                            yf.done(stt(u[:, ct, :], u[:, ct, :], pcol("ssm_d", ct), ps[:, 6, :], ALU.mult, ALU.add))
                            step.done(tt(yw, u[:, ct, :], u[:, ct, :], ALU.mult))
                            step.done(ts(yw, yw, 0.044715, 1.0, ALU.mult, ALU.add))
                            gi_in.done(tt(yw, yw, u[:, ct, :], ALU.mult))

                        def gelu_end(ct):
                            dve.wait_ge(gelu_th, ct + 1)
                            yd.done(stt(u[:, ct, :], yw, 1.0, u[:, ct, :], ALU.add, ALU.mult))

                        c7 = Count(dve, c7_free)

                        def rope_tile(i, src, outs):
                            dve.wait_ge(c7_full, i + 1)
                            step.done(tt(v1, ps[:, 7, :], sin_t[:, :], ALU.mult))
                            step.done(tt(v2, src, cos_t, ALU.mult))
                            for n, (dst, r) in enumerate(outs):
                                ins = tt(dst, v1[r, :], v2[r, :], ALU.add)
                                (c7 if n == len(outs) - 1 else step).done(ins)

                        sm = Count(dve, s_max)
                        pr_ready = Count(dve, p_ready)

                        def softmax(a):
                            n, g = ITEMS[a]
                            lo = 0 if n else P
                            dve.wait_ge(s_full, a + 1)
                            if a:
                                dve.wait_ge(pt_full, a)
                            src = ps[:, 4:6, :].rearrange("p a (h k) -> p (a h) k", h=2)[:, :, lo:]
                            mask = band[:, lo:].unsqueeze(1).to_broadcast([P, 4, 2 * P - lo])
                            part = sc[:, :, lo:]
                            sm.done(stt(part, src, HD ** -0.5, mask, ALU.mult, ALU.add))
                            step.done(dve.tensor_reduce(att[:, 0, :], part, AX.X, ALU.max))
                            sink = pcol("sinks", GROUP * g, GROUP)
                            step.done(tt(att[:, 0, :], att[:, 0, :], sink, ALU.max))
                            step.done(ts(att[:, 1, :], att[:, 0, :], -1.0, None, ALU.mult))
                            sm.done(tt(att[:, 2, :], sink, att[:, 1, :], ALU.add))
                            dve.wait_ge(s_exp, a + 1)
                            step.done(tt(att[:, 5, :], att[:, 4, :], att[:, 3, :], ALU.add))
                            step.done(dve.reciprocal(att[:, 5, :], att[:, 5, :]))
                            pr_ready.done(tt(part, part, att[:, 5, :].unsqueeze(2).to_broadcast([P, 4, 2 * P - lo]), ALU.mult))

                        ol = Count(dve, o_lo)

                        def o_rest(a):
                            n, g = ITEMS[a]
                            dve.wait_ge(o_hi, a + 1)
                            r = (slice(None), slice(2 * g, 2 * g + 2), slice(n * P, (n + 1) * P))
                            ol.done(tt(s_lo[r], ps[:, 6, 0:2 * P].rearrange("p (a q) -> p a q", a=2),
                                       s_hi[r].bitcast(F32), ALU.subtract))

                        free = [Count(dve, acc_free[0]), Count(dve, acc_free[1])]
                        pending = []
                        fractions(0)
                        for gi, (name, p) in enumerate(G1):
                            s = gi - SSM_AT
                            a = gi - ATT_AT
                            two = slice(2 * p, 2 * p + 2)
                            src = banks(gi)

                            def freed(ins):
                                ins.then_inc(acc_free[gi % 2], 1)
                                dve.wait_ge(acc_free[gi % 2], gi // 2 + 1)

                            while pending:
                                prod_rest(*pending.pop(0))
                            if gi == 0:
                                fractions(1)
                            if 0 <= s < SSM_PAIRS:
                                states(s)
                                if s + 2 < SSM_PAIRS:
                                    fractions(s + 2)
                            if s in (5, 9, 13, 17):
                                gelu_start((s - 5) // 4)
                            if s in (6, 10, 14, 18):
                                gelu_end((s - 6) // 4)
                            if 4 <= gi <= 9:
                                i = gi - 4
                                if i == 0:
                                    rope_tile(0, k[:, 0, :], [(k[0:64, 0, :], slice(0, 64)), (k[64:128, 1, :], slice(64, 128))])
                                elif i == 1:
                                    dve.wait_ge(c7_full, 2)
                                    c7.done(dve.tensor_copy(vtok[:, :, :], ps[:, 7, :].rearrange("p (n c) -> p n c", n=NB)))
                                else:
                                    rope_tile(i, q[:, i - 2, :], [(q[:, i - 2, :], slice(0, P))])
                            if 0 <= a < 8:
                                softmax(a)
                            if 1 <= a <= 8:
                                o_rest(a - 1)
                            if name == "ao" and p == 0:
                                pending.append((h_lo[:, 0:4, :], h_hi[:, 0:4, :], u[:, :, :], 0.5))
                            if name == "cx":
                                full(dve, gi)
                                emptied(dve, gi - 1)
                                freed(tt(z[:, :, 2:], src, cc, ALU.mult))
                                for i in range(2):
                                    w = [pcol("conv_w", 4 * j + 2 * p + i) for j in range(3)]
                                    step.done(ts(conv[:, i, :], z[:, i, 0:T], w[0], None, ALU.mult))
                                    for j in (1, 2):
                                        step.done(stt(conv[:, i, :], z[:, i, j:j + T], w[j], conv[:, i, :],
                                                      ALU.mult, ALU.add))
                            elif name == "cb":
                                full(dve, gi)
                                freed(tt(conv, src, conv, ALU.mult))
                                pending.append((s_lo[:, two, :], s_hi[:, two, :], conv, 1.0))
                            elif name == "co":
                                full(dve, gi)
                                emptied(dve, gi - 1)
                                freed(stt(m[:, two, :], gconv, 1.0, src, ALU.add, ALU.mult))
                            elif name in ("ao", "so"):
                                gate = {"ao": ga, "so": gs}[name][:, two, :]
                                full(dve, gi)
                                emptied(dve, at1[({"ao": "ga", "so": "gs"}[name], p)])
                                freed(stt(gate, gate, 1.0, src, ALU.add, ALU.mult))
                                if name == "ao":
                                    step.done(tt(m[:, two, :], m[:, two, :], gate, ALU.add))
                                else:
                                    pr.done(tt(m[:, two, :], m[:, two, :], gate, ALU.add))
                                    pending.append((h_lo[:, two, :], h_hi[:, two, :], m[:, two, :], 0.5))
                            elif name == "gl":
                                emptied(dve, gi)
                                pr.done(stt(q[:, 2:4, :], q[:, 0:2, :], 1.0, u[:, two, :], ALU.add, ALU.mult))
                                pending.append((s_lo[:, two, :], s_hi[:, two, :], q[:, 2:4, :], 0.25))
                            elif name == "mx":
                                full(dve, gi)
                                freed(tt(x[:, two, :], x[:, two, :], src, ALU.add))
                phase_end()

        def ffn(kind, l):
            chunks = CHUNKS1 if kind == 1 else CHUNKS2
            ups = 4 if kind == 1 else 2
            per = ups + 2
            down_at = (2, 5) if kind == 1 else (1, 3)
            up_at = (0, 1, 3, 4) if kind == 1 else (0, 2)
            peeled = 1 if kind == 1 else 2
            n_rounds = (chunks - peeled) // 2
            first_u = ups + (peeled - 1) * per
            ahead = 2
            total = ups + (chunks - 1) * per + 2
            assert (2 * per) % SLOTS == 0 and peeled + 2 * n_rounds == chunks
            turns = 2 * per // SLOTS
            with ExitStack() as st:
                tag = f"f{kind}_"
                h_hi = sb(st, tag + "h_hi", [P, KD, T], F32R)
                h_lo = sb(st, tag + "h_lo", [P, KD, T], F32R)
                hid_hi = sb(st, tag + "hid_hi", [P, 2, 2, T], F32R)
                hid_lo = sb(st, tag + "hid_lo", [P, 2, 2, T], F32R)
                sq = sb(st, tag + "sq", [P, KD, T])
                th = sb(st, tag + "th", [P, 2, T])
                act_in = sb(st, tag + "act_in", [P, 2, T])
                par = sb(st, tag + "par", [P, NP1 if kind == 1 else NP2_COLS])
                sums = x if kind == 1 else sb(st, "f2_sums", [P, KD, T])
                scale = sb(st, tag + "scale", [P, 16])

                with nc.Block() as block:
                    @block.sync
                    def _(sp):
                        sp.dma_start(par[:, :], d["par1"][l, :, :] if kind == 1 else d["par2"][:, 0:NP2_COLS]).then_inc(small_in, 16)

                        def load_up(c, u, turn0, i):
                            rows = slice(512 * (i % 2), 512 * (i % 2) + 512)
                            if kind == 1:
                                src = d["w_ffn_in"][l, rows, bass.ds(c * 256 + (FFN if i >= 2 else 0), 256)]
                            else:
                                src = d["w_ff12"][rows, bass.ds(c * 256, 256)]
                            load_unit(sp, u, src, turn0)

                        def load_down(c, u, turn0, i):
                            cols = slice(512 * i, 512 * i + 512)
                            if kind == 1:
                                src = d["w_ffn_out"][l, bass.ds(c * 256, 256), cols]
                            else:
                                src = d["w_ff22"][bass.ds(c * 256, 256), cols]
                            load_unit(sp, u, src, turn0)

                        def load_chunk(c, u, turn0):
                            for n in range(per):
                                if n in down_at:
                                    load_down(c - 1, u + n, turn0, down_at.index(n))
                                else:
                                    load_up(c, u + n, turn0, up_at.index(n))

                        for n in range(ups):
                            load_up(0, n, 0, n)
                        for c in range(1, peeled):
                            load_chunk(c, ups + (c - 1) * per, 0)
                        with sp.Fori(0, n_rounds) as i:
                            for n in range(2):
                                load_chunk(2 * i + (peeled + n), first_u + n * per, i * turns)
                        for n in range(2):
                            load_down(chunks - 1, total - 2 + n, 0, n)
                        if kind == 2:
                            sp.wait_ge(x_done, 2)
                            sp.dma_start(d["out"].rearrange("(k p) t -> p k t", p=P), x[:, :, :]).then_inc(out_done, 16)
                            sp.wait_ge(out_done, 16)

                    @block.gpsimd
                    def _(pool):
                        for n in range(first_u):
                            if n == 2:
                                pool_rsqrt(pool, 0)
                            rest_unit(pool, n)
                        with pool.Fori(0, n_rounds) as i:
                            for n in range(2 * per):
                                rest_unit(pool, first_u + n, i * turns)
                        for n in range(total - 2, total):
                            rest_unit(pool, n)
                        if kind == 2:
                            pool_rsqrt(pool, 1)

                    @block.tensor
                    def _(pe):
                        pe_norm(pe, sq)
                        h = [(h_hi[:, i, :], h_lo[:, i, :]) for i in range(KD)]

                        def go_up(c, u, turn0, i, parity, first):
                            b = 2 * (i // 2) if kind == 1 else 2 * parity
                            if i % 2 == 0 and not first:
                                if kind == 1:
                                    pe.wait_ge(up_free if i else gt_free, c)
                                else:
                                    pe.wait_ge(th_done, c - 1)
                            if isinstance(c, int) and c == 0 and i < 2:
                                pe.wait_ge(h_lo_done, 4 * i + 4)
                            k = i % 2
                            multiply_unit(pe, u, [ps[:, b, :], ps[:, b + 1, :]], h[4 * k:4 * k + 4], k == 0, k == 1, turn0)

                        def go_down(c, u, turn0, i, parity, first):
                            if i == 0:
                                pe.wait_ge(hid_lo_done, c + 1)
                            if i or not first:
                                pe.wait_ge(down_free, 2 * c + i)
                            multiply_unit(pe, u, [ps[:, 4 + o, :] for o in range(4)],
                                          [(hid_hi[:, parity, k, :], hid_lo[:, parity, k, :]) for k in range(2)],
                                          True, True, turn0)

                        def chunk(c, u, turn0, parity, first=False):
                            for n in range(per):
                                if n in down_at:
                                    go_down(c - 1, u + n, turn0, down_at.index(n), 1 - parity, first)
                                else:
                                    go_up(c, u + n, turn0, up_at.index(n), parity, first and kind == 2)

                        for n in range(ups):
                            go_up(0, n, 0, n, 0, True)
                        for c in range(1, peeled):
                            chunk(c, ups + (c - 1) * per, 0, c % 2, first=True)
                        with pe.Fori(0, n_rounds) as i:
                            for n in range(2):
                                chunk(2 * i + (peeled + n), first_u + n * per, i * turns, (peeled + n) % 2)
                        for n in range(2):
                            go_down(chunks - 1, total - 2 + n, 0, n, (chunks - 1) % 2, False)
                        if kind == 2:
                            pe_sum(pe, sq, SUM_BANK, KD)
                            pe_spread(pe, rstd, SPREAD_BANK, rstd_done, 1)

                    @block.scalar
                    def _(act):
                        for n in range(SLOTS):
                            round_unit(act, n)
                        act_squares(act, x, sq)
                        for kt in range(KD):
                            act.wait_ge(normed, kt + 1)
                            act.activation(h_hi[:, kt, :], sq[:, kt, :], ACT.Copy).then_inc(h_hi_done, 1)
                        tanh = Count(act, th_done)
                        hid = Count(act, hid_hi_done)

                        def chunk(c, u, turn0, parity, whole, start=0):
                            steps = [n for n in range(per)] if whole else [up_at[n] for n in range(ups)]
                            for at, n in enumerate(steps):
                                if at >= start:
                                    round_unit(act, u + at + ahead, turn0)
                                if kind == 1 and n == up_at[1]:
                                    multiplied(act, u + at, turn0)
                                    if not (isinstance(c, int) and c == 0):
                                        act.wait_ge(gt_free, c)
                                    tanh.done(act.activation(th[:, :, :], ps[:, 0:2, :], ACT.Tanh, scale=0.5))
                                if n == up_at[-1]:
                                    if kind == 2:
                                        multiplied(act, u + at, turn0)
                                        if not (isinstance(c, int) and c == 0):
                                            act.wait_ge(up_free, c)
                                        b = 2 * parity
                                        tanh.done(act.activation(th[:, :, :], ps[:, b:b + 2, :], ACT.Relu))
                                    act.wait_ge(up_free, c + 1)
                                    hid.done(act.activation(hid_hi[:, parity, :, :], act_in[:, :, :], ACT.Copy))

                        chunk(0, 0, 0, 0, False, start=SLOTS - ahead)
                        for c in range(1, peeled):
                            chunk(c, ups + (c - 1) * per, 0, c % 2, True, start=max(0, SLOTS - ahead - ups))
                        with rounds(act, n_rounds, {tanh: 2, hid: 2}) as i:
                            for n in range(2):
                                chunk(2 * i + (peeled + n), first_u + n * per, i * turns, (peeled + n) % 2, True)
                        if kind == 2:
                            act.wait_ge(down_free, 2 * chunks)
                            for kt in range(KD):
                                act.activation(sq[:, kt, :], sums[:, kt, :], ACT.Square).then_inc(squares, 1)

                    @block.vector
                    def _(dve):
                        step = Count(dve, dve_step)
                        tt, ts, stt = dve.tensor_tensor, dve.tensor_scalar, dve.scalar_tensor_tensor
                        dve.wait_ge(small_in, 16)
                        if kind == 1:
                            gain = par[:, P1["norm_ffn"][0]:P1["norm_ffn"][1]]
                        else:
                            gain = scale[:, 0:8]
                            step.done(stt(gain, mod[:, 32:40], 1.0, par[:, P2["pre_norm2"][0]:P2["pre_norm2"][1]],
                                          ALU.add, ALU.mult))
                            step.done(tt(scale[:, 8:16], mod[:, 40:48], par[:, P2["post_norm2"][0]:P2["post_norm2"][1]],
                                         ALU.mult))
                            step.done(dve.memset(sums[:, :, :], 0.0))
                        cm = Count(dve, mean_done)
                        nd = Count(dve, normed)
                        dve_mean(dve, SUM_BANK, 0, cm)
                        dve.wait_ge(spread, 1)
                        for kt in range(KD + 1):
                            if kt < KD:
                                ins = stt(sq[:, kt, :], x[:, kt, :], gain[:, kt:kt + 1], ps[:, SPREAD_BANK, :],
                                          ALU.mult, ALU.mult)
                                if kind == 1:
                                    nd.done(ins)
                                else:
                                    step.done(ins)
                                    nd.done(ts(sq[:, kt, :], sq[:, kt, :], mod[:, 24 + kt:25 + kt], None, ALU.add))
                            if kt:
                                dve.wait_ge(h_hi_done, kt)
                                tt(h_lo[:, kt - 1, :], sq[:, kt - 1, :], h_hi[:, kt - 1, :].bitcast(F32), ALU.subtract)\
                                    .then_inc(h_lo_done, 1)
                        dve.wait_ge(h_lo_done, KD)
                        gf, uf, hl, df = (Count(dve, q) for q in (gt_free, up_free, hid_lo_done, down_free))

                        def add_down(u, turn0, i):
                            multiplied(dve, u, turn0)
                            out = sums[:, 4 * i:4 * i + 4, :]
                            df.done(tt(out, out, ps[:, 4:8, :], ALU.add))

                        def chunk(c, u, turn0, parity, whole):
                            steps = [n for n in range(per)] if whole else [up_at[n] for n in range(ups)]
                            for at, n in enumerate(steps):
                                if n in down_at:
                                    add_down(u + at, turn0, down_at.index(n))
                                elif kind == 1 and n == up_at[1]:
                                    dve.wait_ge(th_done, c + 1)
                                    gf.done(stt(act_in[:, :, :], th[:, :, :], 1.0, ps[:, 0:2, :], ALU.add, ALU.mult))
                                elif n == up_at[-1]:
                                    if kind == 1:
                                        multiplied(dve, u + at, turn0)
                                        uf.done(stt(act_in[:, :, :], act_in[:, :, :], 0.5, ps[:, 2:4, :],
                                                    ALU.mult, ALU.mult))
                                    else:
                                        dve.wait_ge(th_done, c + 1)
                                        uf.done(tt(act_in[:, :, :], th[:, :, :], th[:, :, :], ALU.mult))
                                    dve.wait_ge(hid_hi_done, c + 1)
                                    hl.done(tt(hid_lo[:, parity, :, :], act_in[:, :, :],
                                               hid_hi[:, parity, :, :].bitcast(F32), ALU.subtract))

                        chunk(0, 0, 0, 0, False)
                        for c in range(1, peeled):
                            chunk(c, ups + (c - 1) * per, 0, c % 2, True)
                        counts = {uf: 2, hl: 2, df: 4}
                        if kind == 1:
                            counts[gf] = 2
                        with rounds(dve, n_rounds, counts) as i:
                            for n in range(2):
                                chunk(2 * i + (peeled + n), first_u + n * per, i * turns, (peeled + n) % 2, True)
                        for n in range(2):
                            add_down(total - 2 + n, 0, n)
                        if kind == 2:
                            dve_mean(dve, SUM_BANK, 1, cm)
                            dve.wait_ge(spread, 2)
                            xd = Count(dve, x_done)
                            for kt in range(KD):
                                step.done(stt(sums[:, kt, :], sums[:, kt, :], scale[:, 8 + kt:9 + kt],
                                              ps[:, SPREAD_BANK, :], ALU.mult, ALU.mult))
                                (xd if kt % 4 == 3 else step).done(tt(x[:, kt, :], x[:, kt, :], sums[:, kt, :], ALU.add))
                phase_end()

        def between():
            units = 48
            with ExitStack() as st:
                sq = sb(st, "b_sq", [P, KD, T])
                par = sb(st, "b_par", [P, NP2_COLS])
                cs = sb(st, "b_cs", [P, 16])
                c_col = par[:, P2["c"][0]:P2["c"][1]]
                with nc.Block() as block:
                    @block.sync
                    def _(sp):
                        sp.dma_start(par[:, :], d["par2"][:, 0:NP2_COLS]).then_inc(small_in, 16)
                        for u in range(units):
                            s, turn = place(u, 0)
                            if turn:
                                sp.wait_ge(used[s], turn)
                            sp.dma_start(raw[:, s, :].rearrange("p (k n) -> p k n", k=4),
                                         d["w_ada2"][512 * (u % 2):512 * (u % 2) + 512, 256 * (u // 2):256 * (u // 2) + 256]
                                         .rearrange("(k p) n -> p k n", p=P)).then_inc(raw_in[s], 16)

                    @block.gpsimd
                    def _(pool):
                        pool_rsqrt(pool, 0)

                    @block.tensor
                    def _(pe):
                        pe_norm(pe, sq)
                        pe.wait_ge(normed, 1)
                        for u in range(units):
                            s, turn = place(u, 0)
                            pe.wait_ge(raw_in[s], 16 * (turn + 1))
                            for o in range(2):
                                for k in range(4):
                                    kt = 4 * (u % 2) + k
                                    at = k * 256 + o * P
                                    ins = pe.matmul(ps[:, o, u // 2:u // 2 + 1], raw[:, s, at:at + P], cs[:, kt:kt + 1],
                                                    start=kt == 0, stop=kt == KD - 1)
                            ins.then_inc(used[s], 1)

                    @block.scalar
                    def _(act):
                        act_squares(act, x, sq)
                        act.wait_ge(small_in, 16)
                        act.activation(cs[:, 8:16], c_col, ACT.Tanh, scale=0.5).then_inc(th_done, 1)

                    @block.vector
                    def _(dve):
                        step = Count(dve, dve_step)
                        cm = Count(dve, mean_done)
                        tt, ts, stt = dve.tensor_tensor, dve.tensor_scalar, dve.scalar_tensor_tensor
                        dve_mean(dve, SUM_BANK, 0, cm)
                        dve.wait_ge(small_in, 16)
                        dve.wait_ge(th_done, 1)
                        step.done(stt(cs[:, 8:16], cs[:, 8:16], 1.0, c_col, ALU.add, ALU.mult))
                        nd = Count(dve, normed)
                        nd.done(ts(cs[:, 0:8], cs[:, 8:16], 0.5, None, ALU.mult))
                        dve.wait_ge(spread, 1)
                        for kt in range(KD):
                            g = P2["norm_final"][0] + kt
                            step.done(stt(x[:, kt, :], x[:, kt, :], par[:, g:g + 1], ps[:, SPREAD_BANK, :],
                                          ALU.mult, ALU.mult))
                        for s in range(2):
                            multiplied(dve, units - 1 - s)
                        pairs = mod.rearrange("p (a b) -> p a b", b=2)
                        b0 = P2["b_ada"][0]
                        bias = par[:, b0:b0 + 48].rearrange("p (a b) -> p a b", b=2)
                        for o in range(2):
                            step.done(tt(pairs[:, :, o], ps[:, o, 0:24], bias[:, :, o], ALU.add))
                phase_end()

        def order2():
            groups = []
            for p in range(4):
                groups += [("ua", p), ("ub", p)]
            for name in ("q", "k", "v", "gc", "ga", "cv", "wo"):
                groups += [(name, p) for p in range(4)]
            return groups

        G2 = order2()
        UNITS2 = 2 * len(G2)
        at2 = {g: i for i, g in enumerate(G2)}
        COL2 = {"ua": 0, "ub": D, "q": 2 * D, "k": 3 * D, "v": 4 * D, "gc": 5 * D, "ga": 6 * D}
        CONV_AT = 2
        LN_AT = 18
        ITEMS2 = [(h, n) for h in range(HEADS2) for n in range(NB)]
        ITEM_AT = 21
        PER_GROUP = 3
        SLOTS2 = {}
        for i in range(len(ITEMS2) + 3):
            g = min(ITEM_AT + i // PER_GROUP, at2[("cv", 3)])
            SLOTS2.setdefault(g, []).append(i)

        def mixer2():
            with ExitStack() as st:
                h_hi = sb(st, "m_h_hi", [P, KD, T], F32R)
                h_lo = sb(st, "m_h_lo", [P, KD, T], F32R)
                u = sb(st, "m_u", [P, KD, PAD + T])
                conv = sb(st, "m_conv", [P, KD, T])
                q = sb(st, "m_q", [P, KD, T])
                k = sb(st, "m_k", [P, KD, T])
                vtok = sb(st, "m_vtok", [P, NB, D])
                gc = sb(st, "m_gc", [P, KD, T])
                pr = sb(st, "m_pr", [P, 2, 2, T])
                pt = sb(st, "m_pt", [P, 2, T])
                par = sb(st, "m_par", [P, NP2_COLS])
                small = sb(st, "m_small", [P, 88])
                ga = sq = ln_tanh = u[:, :, 0:T]
                vT = gc
                att = x
                cos_t, sin_t = pr[:, 0, 0, :], pr[:, 0, 1, :]
                rot, taps_w, tmp, lambdas = pr[:, 1, 0, 0:P], pr[:, 1, 1, 0:TAPS * KD], pt[:, 0, :], pt[:, 1, 0:4 * HD]
                glu_a, glu_b = q[:, 0:2, :], q[:, 2:4, :]
                gain1, gain_post, neg_lam, head_gain, lam_t = (small[:, 0:8], small[:, 8:16], small[:, 16:17],
                                                               small[:, 17:18], small[:, 18:22])
                stat = [small[:, 24 + 16 * b:40 + 16 * b] for b in range(2)]

                in_range = small[:, 56:88]

                def pcol(name, i=0, w=1):
                    return par[:, P2[name][0] + i:P2[name][0] + i + w]

                def banks(gi):
                    return ps[:, 2 * (gi % 2):2 * (gi % 2) + 2, :]

                def full(eng, gi):
                    multiplied(eng, 2 * gi + 1)

                def emptied(eng, gi):
                    eng.wait_ge(acc_free[gi % 2], gi // 2 + 1)

                with nc.Block() as block:
                    @block.sync
                    def _(sp):
                        sp.dma_start(par[:, :], d["par2"][:, 0:NP2_COLS]).then_inc(small_in, 16)
                        for t, n in ((taps_w, "conv_w"), (lambdas, "lambdas")):
                            sp.dma_start(t, d["par2"][:, P2[n][0]:P2[n][1]]).then_inc(small_in, 16)
                        for t, n in ((rot, "rot2"), (cos_t, "cos2"), (sin_t, "sin2")):
                            sp.dma_start(t, d["const"][:, CONST[n][0]:CONST[n][1]]).then_inc(small_in, 16)

                        def group(gi):
                            name, p = G2[gi]
                            w = {"cv": d["conv_w_out2"], "wo": d["w_o2"]}.get(name, d["w_in2"])
                            c = COL2.get(name, 0) + 256 * p
                            for i in range(2):
                                load_unit(sp, 2 * gi + i, w[512 * i:512 * i + 512, c:c + 256])

                        for gi in range(len(G2)):
                            group(gi)
                            if gi == 3:
                                sp.wait_ge(h_lo_done, KD)
                                sp.dma_start(spill, x[:, :, :].rearrange("p k t -> p (k t)")).then_inc(spilled, 16)
                            if gi == at2[("wo", 1)]:
                                sp.wait_ge(spilled, 16)
                                sp.wait_ge(heads_done, HEADS2)
                                sp.dma_start(q[:, :, :].rearrange("p k t -> p (k t)"), spill).then_inc(x_back, 16)

                    @block.gpsimd
                    def _(pool):
                        for un in range(UNITS2):
                            if un == 2:
                                pool_rsqrt(pool, 0)
                            if un == 2 * (LN_AT + 3):
                                pool_rsqrt(pool, 1)
                            if un == 2 * at2[("wo", 1)] + 1:
                                pool_rsqrt(pool, 2, width=32)
                            rest_unit(pool, un)
                        pool_rsqrt(pool, 3)

                    @block.tensor
                    def _(pe):
                        pe_norm(pe, sq)
                        h = [(h_hi[:, i, :], h_lo[:, i, :]) for i in range(KD)]

                        def scores(i):
                            hd, n = ITEMS2[i]
                            if i:
                                pe.wait_ge(exps_done, 2 * i)
                            else:
                                pe.wait_ge(vt_done, 4)
                            r = slice(64 * (hd % 2), 64 * (hd % 2) + 64)
                            for c in range(2):
                                t = 4 * c + hd // 2
                                ins = pe.matmul(ps[:, 4 + c, 0:(n + 1) * P], q[r, t, n * P:(n + 1) * P],
                                                k[r, t, 0:(n + 1) * P], start=True, stop=True)
                            ins.then_inc(s_full, 1)

                        def probs(i):
                            hd, n = ITEMS2[i]
                            pe.wait_ge(p_ready, i + 1)
                            if i:
                                pe.wait_ge(pt_done, i)
                            for b in range(n + 1):
                                ins = pe.transpose(ps[:, 6, b * P:(b + 1) * P], pr[:, i % 2, 0, b * P:(b + 1) * P], ident[:, :])
                            ins.then_inc(pt_full, 1)

                        def values(i):
                            hd, n = ITEMS2[i]
                            pe.wait_ge(pt_done, i + 1)
                            if i:
                                pe.wait_ge(o_hi, i)
                            for b in range(n + 1):
                                ins = pe.matmul(ps[:, 7, 0:P], vtok[:, b, hd * P:(hd + 1) * P],
                                                pt[:, i % 2, b * P:(b + 1) * P], start=b == 0, stop=b == n)
                            ins.then_inc(o_full, 1)

                        def slot(i):
                            if 3 <= i:
                                values(i - 3)
                            if 2 <= i < len(ITEMS2) + 2:
                                probs(i - 2)
                            if i < len(ITEMS2):
                                scores(i)

                        for gi, (name, p) in enumerate(G2):
                            if gi >= 2:
                                emptied(pe, gi - 2)
                            outs = [banks(gi)[:, 0, :], banks(gi)[:, 1, :]]
                            if gi == LN_AT:
                                pe.wait_ge(conv_done, 16)
                                pe.wait_ge(c7_free, 8)
                                pe_sum(pe, conv, SUM_BANK)
                            if gi == LN_AT + 2:
                                pe_sum(pe, sq, SUM_BANK, KD)
                            if name == "wo" and p == 0:
                                pe.wait_ge(squares, 3 * KD)
                                pe.wait_ge(o_hi, len(ITEMS2))
                                for i, (hd, n) in enumerate(ITEMS2):
                                    ins = pe.matmul(ps[:, 4, i:i + 1], conv[:, hd, n * P:(n + 1) * P], ones[:, 0:1],
                                                    start=True, stop=True)
                                ins.then_inc(sums_done, 1)
                                pe.wait_ge(rstd_kept, 1)
                                for hd in range(HEADS2):
                                    if hd >= 4:
                                        pe.wait_ge(heads_done, hd - 3)
                                    for n in range(NB):
                                        i = hd * NB + n
                                        ins = pe.matmul(ps[:, 4 + hd % 4, n * P:(n + 1) * P],
                                                        rstd[:, i:i + 1].to_broadcast([P, P]), ident[:, :], start=True, stop=True)
                                    ins.then_inc(spread, 1)
                            todo = SLOTS2.get(gi, [])
                            for i in range(2):
                                if gi == 0:
                                    pe.wait_ge(h_lo_done, 4 * i + 4)
                                if name == "cv":
                                    pe.wait_ge(prod_lo, 4 * i + 4)
                                if name == "wo":
                                    pe.wait_ge(prod_lo, 8 + 4 * i + 4)
                                cut = todo[:len(todo) // 2] if i == 0 else todo[len(todo) // 2:]
                                for s in cut[:1]:
                                    slot(s)
                                multiply_unit(pe, 2 * gi + i, outs, h[4 * i:4 * i + 4], i == 0, i == 1)
                                for s in cut[1:]:
                                    slot(s)
                            if gi == LN_AT:
                                pe_spread(pe, rstd, SPREAD_BANK, ln_mean, 0)
                            if gi == LN_AT + 2:
                                pe_spread(pe, rstd, SPREAD_BANK, rstd_done, 1)
                            if 9 <= gi <= 16:
                                src = (q if gi < 13 else k)[:, 2 * ((gi - 9) % 4):2 * ((gi - 9) % 4) + 2, :]
                                emptied(pe, gi - 1)
                                if gi > 9:
                                    pe.wait_ge(c7_free, gi - 9)
                                for o in range(2):
                                    ins = pe.matmul(ps[:, 6 + o, :], rot, src[:, o, :], start=True, stop=True)
                                ins.then_inc(c7_full, 1)
                            if 17 <= gi <= 20:
                                w = gi - 17
                                emptied(pe, gi - 1)
                                if w:
                                    pe.wait_ge(vt_done, w)
                                for o in range(2):
                                    for n in range(NB):
                                        ins = pe.transpose(ps[:, 4 + o, n * P:(n + 1) * P],
                                                           vT[:, 2 * w + o, n * P:(n + 1) * P], ident[:, :])
                                ins.then_inc(vt_full, 1)
                        pe_sum(pe, conv, SUM_BANK, 3 * KD)
                        pe_spread(pe, rstd, SPREAD_BANK, rstd_done, 3)

                    @block.scalar
                    def _(act):
                        step = Count(act, act_step)
                        ahead = [0]

                        def prefetch(n):
                            while ahead[0] < min(n, UNITS2):
                                round_unit(act, ahead[0])
                                ahead[0] += 1

                        prefetch(SLOTS)
                        act_squares(act, x, sq)
                        pa = Count(act, par_act)
                        act.wait_ge(par_dve, 1)
                        pa.done(act.activation(lam_t[:, 2:4], lam_t[:, 0:2], ACT.Exp))
                        for kt in range(KD):
                            act.wait_ge(normed, kt + 1)
                            act.activation(h_hi[:, kt, :], sq[:, kt, :], ACT.Copy).then_inc(h_hi_done, 1)

                        def exps(i):
                            hd, n = ITEMS2[i]
                            w = (n + 1) * P
                            act.wait_ge(s_max, i + 1)
                            if i >= 2:
                                act.wait_ge(pt_full, i - 1)
                            for c in range(2):
                                ed.done(act.activation(pr[:, i % 2, c, 0:w], ps[:, 4 + c, 0:w], ACT.Exp, scale=HD ** -0.5,
                                                       bias=stat[i % 2][:, 2 + c:3 + c],
                                                       accum_out=stat[i % 2][:, 4 + c:5 + c]))

                        def pt_copy(i):
                            hd, n = ITEMS2[i]
                            w = (n + 1) * P
                            act.wait_ge(pt_full, i + 1)
                            act.activation(pt[:, i % 2, 0:w], ps[:, 6, 0:w], ACT.Copy).then_inc(pt_done, 1)

                        def o_copy(i):
                            hd, n = ITEMS2[i]
                            act.wait_ge(o_full, i + 1)
                            if i == 0:
                                act.wait_ge(spilled, 16)
                            act.activation(att[:, hd, n * P:(n + 1) * P], ps[:, 7, 0:P], ACT.Copy).then_inc(o_hi, 1)

                        ed, lt = Count(act, exps_done), Count(act, ln_th)
                        n_prod = [0]

                        def prod_round(dst, src, scale):
                            n_prod[0] += 1
                            act.wait_ge(prod_ready, n_prod[0])
                            act.activation(dst, src, ACT.Copy, scale=scale).then_inc(prod_hi, 1)

                        for gi, (name, p) in enumerate(G2):
                            two = slice(2 * p, 2 * p + 2)
                            done = acc_free[gi % 2]
                            todo = SLOTS2.get(gi, [])

                            def slot(i):
                                if i < len(ITEMS2):
                                    exps(i)
                                if 2 <= i < len(ITEMS2) + 2:
                                    pt_copy(i - 2)
                                if 3 <= i:
                                    o_copy(i - 3)

                            if gi == LN_AT + 1:
                                for kt in range(KD):
                                    act.wait_ge(centred, kt + 1)
                                    act.activation(sq[:, kt, :], conv[:, kt, :], ACT.Square).then_inc(squares, 1)
                            if gi == LN_AT + 3:
                                for kt in range(KD):
                                    act.wait_ge(ln_ready, kt + 1)
                                    lt.done(act.activation(ln_tanh[:, kt, :], conv[:, kt, :], ACT.Tanh, scale=0.5))
                            for i in range(2):
                                cut = todo[:len(todo) // 2] if i == 0 else todo[len(todo) // 2:]
                                for s in cut[:1]:
                                    slot(s)
                                prefetch(2 * gi + 1 + i + AHEAD)
                                for s in cut[1:]:
                                    slot(s)
                            src = banks(gi)
                            full(act, gi)
                            if name == "ua":
                                if p:
                                    act.wait_ge(glu_done, p)
                                act.activation(glu_a, src, ACT.Copy).then_inc(done, 1)
                            elif name == "ub":
                                act.activation(glu_b, src, ACT.Tanh, scale=0.5).then_inc(done, 1)
                            elif name in ("q", "k"):
                                if name == "q" and p == 0:
                                    act.wait_ge(glu_done, 4)
                                act.activation((q if name == "q" else k)[:, two, :], src, ACT.Copy).then_inc(done, 1)
                            elif name == "v":
                                act.activation(vT[:, two, :], src, ACT.Copy).then_inc(done, 1)
                            elif name in ("gc", "ga"):
                                if name == "ga" and p == 0:
                                    act.wait_ge(prod_ready, KD)
                                act.activation((gc if name == "gc" else ga)[:, two, :], src, ACT.Tanh, scale=0.5)\
                                    .then_inc(done, 1)
                            elif name == "wo":
                                act.activation(att[:, two, :], src, ACT.Copy).then_inc(done, 1)
                            if 17 <= gi <= 20:
                                w = gi - 17
                                act.wait_ge(vt_full, w + 1)
                                dst = vtok[:, :, 2 * w * P:(2 * w + 2) * P].rearrange("p n (o c) -> p o n c", o=2)
                                for o in range(2):
                                    ins = act.activation(dst[:, o, :, :], ps[:, 4 + o, :].rearrange("p (n c) -> p n c", n=NB),
                                                         ACT.Copy)
                                    if o == 0:
                                        step.done(ins)
                                    else:
                                        ins.then_inc(vt_done, 1)
                            if gi == at2[("ga", 3)]:
                                for kt in range(KD):
                                    prod_round(h_hi[:, kt, :], conv[:, kt, :], 0.5)
                            if gi == at2[("cv", 3)]:
                                for kt in range(KD):
                                    act.wait_ge(clipped, kt + 1)
                                    act.activation(conv[:, kt, :], conv[:, kt, :], ACT.Square, scale=1.0 / 16.0)\
                                        .then_inc(squares, 1)
                                for kt in range(KD):
                                    prod_round(h_hi[:, kt, :], gc[:, kt, :], 0.5)
                        act.wait_ge(acc_free[0], len(G2) // 2)
                        act.wait_ge(acc_free[1], len(G2) // 2)
                        for kt in range(KD):
                            act.activation(conv[:, kt, :], att[:, kt, :], ACT.Square).then_inc(squares, 1)

                    @block.vector
                    def _(dve):
                        step = Count(dve, dve_step)
                        tt, ts, stt = dve.tensor_tensor, dve.tensor_scalar, dve.scalar_tensor_tensor
                        dve.wait_ge(small_in, 96)
                        lam = lambdas.rearrange("p (a b c) -> p a b c", a=2, b=2)
                        prod = tmp[:, 0:2 * HD].rearrange("p (a c) -> p a c", a=2)
                        step.done(tt(prod, lam[:, :, 0, :], lam[:, :, 1, :], ALU.mult))
                        pd = Count(dve, par_dve)
                        pd.done(dve.tensor_reduce(lam_t[:, 0:2], prod, AX.X, ALU.add))
                        step.done(stt(gain1, mod[:, 8:16], 1.0, pcol("pre_norm1", 0, 8), ALU.add, ALU.mult))
                        step.done(tt(gain_post, mod[:, 16:24], pcol("post_norm1", 0, 8), ALU.mult))
                        step.done(ts(head_gain, pcol("head_norm"), 1.0 - LAM_INIT, None, ALU.mult))
                        dve.wait_ge(par_act, 1)
                        step.done(tt(neg_lam, lam_t[:, 3:4], lam_t[:, 2:3], ALU.subtract))
                        step.done(ts(neg_lam, neg_lam, LAM_INIT, None, ALU.subtract))

                        cm = Count(dve, mean_done)
                        dve_mean(dve, SUM_BANK, 0, cm)
                        dve.wait_ge(spread, 1)
                        nd = Count(dve, normed)
                        for kt in range(KD + 1):
                            if kt < KD:
                                step.done(stt(sq[:, kt, :], x[:, kt, :], gain1[:, kt:kt + 1], ps[:, SPREAD_BANK, :],
                                              ALU.mult, ALU.mult))
                                nd.done(ts(sq[:, kt, :], sq[:, kt, :], mod[:, kt:kt + 1], None, ALU.add))
                            if kt:
                                dve.wait_ge(h_hi_done, kt)
                                tt(h_lo[:, kt - 1, :], sq[:, kt - 1, :], h_hi[:, kt - 1, :].bitcast(F32), ALU.subtract)\
                                    .then_inc(h_lo_done, 1)
                        dve.wait_ge(h_lo_done, KD)
                        step.done(dve.memset(u[:, :, 0:PAD], 0.0))

                        cd = Count(dve, conv_done)

                        def taps(half):
                            kt = half // 2
                            first, last = (0, 16) if half % 2 == 0 else (16, TAPS)
                            for j in range(first, last):
                                w = taps_w[:, KD * j + kt:KD * j + kt + 1]
                                src = u[:, kt, j:j + T]
                                if j == 0:
                                    step.done(ts(conv[:, kt, :], src, w, None, ALU.mult))
                                elif j < TAPS - 1:
                                    ins = stt(conv[:, kt, :], src, w, conv[:, kt, :], ALU.mult, ALU.add)
                                    (cd if j == 15 else step).done(ins)
                                else:
                                    step.done(stt(conv[:, kt, :], src, w, conv[:, kt, :], ALU.mult, ALU.add))
                                    cd.done(ts(conv[:, kt, :], conv[:, kt, :], 0.5, pcol("conv_b", kt), ALU.mult, ALU.add))

                        sm = Count(dve, s_max)
                        rdy = Count(dve, p_ready)

                        def maxima(i):
                            hd, n = ITEMS2[i]
                            w = (n + 1) * P
                            dve.wait_ge(s_full, i + 1)
                            s = stat[i % 2]
                            diag = ps[:, 4:6, n * P:(n + 1) * P]
                            mask = band[:, P:2 * P].unsqueeze(1).to_broadcast([P, 2, P])
                            step.done(tt(diag, diag, mask, ALU.add))
                            step.done(dve.tensor_reduce(s[:, 0:2], ps[:, 4:6, 0:w], AX.X, ALU.max))
                            sm.done(ts(s[:, 2:4], s[:, 0:2], -(HD ** -0.5), None, ALU.mult))

                        def combine(i):
                            hd, n = ITEMS2[i]
                            w = (n + 1) * P
                            s = stat[i % 2]
                            dve.wait_ge(exps_done, 2 * i + 2)
                            step.done(dve.reciprocal(s[:, 6:8], s[:, 4:6]))
                            step.done(tt(s[:, 7:8], s[:, 7:8], neg_lam, ALU.mult))
                            p1, p2 = pr[:, i % 2, 0, 0:w], pr[:, i % 2, 1, 0:w]
                            step.done(ts(p1, p1, s[:, 6:7], None, ALU.mult))
                            rdy.done(stt(p1, p2, s[:, 7:8], p1, ALU.mult, ALU.add))

                        n_prod = [0]
                        pready = Count(dve, prod_ready)
                        pl = Count(dve, prod_lo)

                        def prod_rest(kt, src):
                            n_prod[0] += 1
                            dve.wait_ge(prod_hi, n_prod[0])
                            pl.done(stt(h_lo[:, kt, :], src, 0.5, h_hi[:, kt, :].bitcast(F32), ALU.mult, ALU.subtract))

                        gd, c7, ct = Count(dve, glu_done), Count(dve, c7_free), Count(dve, centred)
                        lr, hdn = Count(dve, ln_ready), Count(dve, heads_done)
                        for gi, (name, p) in enumerate(G2):
                            two = slice(2 * p, 2 * p + 2)
                            src = banks(gi)
                            todo = SLOTS2.get(gi, [])
                            if CONV_AT <= gi < CONV_AT + 16:
                                taps(gi - CONV_AT)
                            if gi == LN_AT:
                                dve.wait_ge(sums_done, 2)
                                Count(dve, ln_mean).done(ts(rstd[:, 0:NB], ps[:, SUM_BANK, 0:NB], 1.0 / D, None, ALU.mult))
                                dve.wait_ge(spread, 2)
                                for kt in range(KD):
                                    ct.done(tt(conv[:, kt, :], conv[:, kt, :], ps[:, SPREAD_BANK, :], ALU.subtract))
                            if gi == LN_AT + 2:
                                dve_mean(dve, SUM_BANK, 2, cm)
                                dve.wait_ge(spread, 3)
                                for kt in range(KD):
                                    step.done(stt(conv[:, kt, :], conv[:, kt, :], pcol("conv_ln_g", kt),
                                                  ps[:, SPREAD_BANK, :], ALU.mult, ALU.mult))
                                    lr.done(ts(conv[:, kt, :], conv[:, kt, :], pcol("conv_ln_b", kt), None, ALU.add))
                            if gi == LN_AT + 4:
                                for kt in range(KD):
                                    dve.wait_ge(ln_th, kt + 1)
                                    pready.done(stt(conv[:, kt, :], ln_tanh[:, kt, :], 1.0, conv[:, kt, :], ALU.add, ALU.mult))
                            if 10 <= gi <= 17:
                                dst = (q if gi < 14 else k)[:, 2 * ((gi - 10) % 4):2 * ((gi - 10) % 4) + 2, :]
                                dve.wait_ge(c7_full, gi - 9)
                                for o in range(2):
                                    step.done(tt(tmp, ps[:, 6 + o, :], sin_t, ALU.mult))
                                    step.done(tt(dst[:, o, :], dst[:, o, :], cos_t, ALU.mult))
                                    (c7 if o else step).done(tt(dst[:, o, :], dst[:, o, :], tmp, ALU.add))
                            for i in todo:
                                if i < len(ITEMS2):
                                    maxima(i)
                                if 1 <= i <= len(ITEMS2):
                                    combine(i - 1)
                            if name == "ub":
                                emptied(dve, gi - 1)
                                emptied(dve, gi)
                                gd.done(stt(u[:, two, PAD:], glu_b, 1.0, glu_a, ALU.add, ALU.mult))
                            if name == "cv":
                                full(dve, gi)
                                emptied(dve, at2[("gc", p)])
                                for o in range(2):
                                    t = 2 * p + o
                                    step.done(ts(gc[:, t, :], gc[:, t, :], 1.0, None, ALU.add))
                                    ins = stt(gc[:, t, :], src[:, o, :], pcol("conv_b_out", t), gc[:, t, :],
                                              ALU.add, ALU.mult)
                                    if o:
                                        ins.then_inc(acc_free[gi % 2], 1)
                                        emptied(dve, gi)
                                    else:
                                        step.done(ins)
                            if gi == at2[("ga", 3)]:
                                for kt in range(KD):
                                    prod_rest(kt, conv[:, kt, :])
                            if gi == at2[("cv", 3)]:
                                dve.wait_ge(prod_lo, KD)
                                for kt in range(KD):
                                    dve.wait_ge(o_hi, NB * (kt + 1))
                                    ts(conv[:, kt, :], att[:, kt, :], 2.0 ** 64, -2.0 ** 64, ALU.min, ALU.max)\
                                        .then_inc(clipped, 1)
                                dve.wait_ge(sums_done, 4)
                                step.done(ts(in_range, ps[:, 4, 0:32], 2.0 ** 120, None, ALU.is_lt))
                                step.done(ts(rstd[:, 0:32], ps[:, 4, 0:32], 2.0 ** 120, 256.0 / VD, ALU.min, ALU.mult))
                                cm.done(ts(rstd[:, 0:32], rstd[:, 0:32], EPS, None, ALU.add))
                                dve.wait_ge(rstd_done, 3)
                                tt(rstd[:, 0:32], rstd[:, 0:32], in_range, ALU.mult).then_inc(rstd_kept, 1)
                                emptied(dve, at2[("ga", 3)])
                                for hd in range(HEADS2):
                                    dve.wait_ge(spread, 3 + hd + 1)
                                    hdn.done(stt(att[:, hd, :], att[:, hd, :], head_gain, ps[:, 4 + hd % 4, :],
                                                 ALU.mult, ALU.mult))
                                    step.done(stt(ga[:, hd, :], ga[:, hd, :], 1.0, att[:, hd, :], ALU.add, ALU.mult))
                                    pready.done(tt(gc[:, hd, :], gc[:, hd, :], ga[:, hd, :], ALU.add))
                                for hd in range(HEADS2):
                                    prod_rest(hd, gc[:, hd, :])
                        dve_mean(dve, SUM_BANK, 4, cm)
                        dve.wait_ge(spread, 3 + HEADS2 + 1)
                        dve.wait_ge(x_back, 16)
                        for kt in range(KD):
                            step.done(stt(x[:, kt, :], x[:, kt, :], gain_post[:, kt:kt + 1], ps[:, SPREAD_BANK, :],
                                          ALU.mult, ALU.mult))
                            step.done(tt(x[:, kt, :], x[:, kt, :], q[:, kt, :], ALU.add))
                phase_end()

        with nc.Fori(0, DEPTH) as l:
            mixer1(l)
            ffn(1, l)
        between()
        mixer2()
        ffn(2, None)


def _cols(v):
    return v.reshape(-1, P).T


def _consts():
    import numpy as np

    c = np.zeros((P, NCONST), np.float32)

    def put(name, a):
        c[:, CONST[name][0]:CONST[name][1]] = a

    put("ident", np.eye(P))
    i = np.arange(P)[:, None]
    j = np.arange(2 * P)[None, :]
    delta = i + P - j
    put("band", np.where((delta >= 0) & (delta < P), 0.0, -1e30))
    put("t", np.broadcast_to(np.arange(T, dtype=np.float32), (P, T)))
    pos = np.arange(T, dtype=np.float32)
    for n, rot, theta in ((1, HD // 4, 500000.0), (2, HD, 10000.0)):
        half = rot // 2
        inv = (np.float32(theta) ** (-np.arange(0, rot, 2, dtype=np.float32) / np.float32(rot))).astype(np.float32)
        ang = (pos[None, :] * inv[:, None]).astype(np.float32).astype(np.float64)
        cos, sin = np.ones((P, T)), np.zeros((P, T))
        r = np.zeros((P, P))
        for p in range(P):
            e = p % HD
            if e < rot:
                cos[p], sin[p] = np.cos(ang[e % half]), np.sin(ang[e % half])
                if e < half:
                    r[p + half, p] = -1.0
                else:
                    r[p - half, p] = 1.0
        put(f"cos{n}", cos)
        put(f"sin{n}", sin)
        put(f"rot{n}", r)
    return c


def _lay_out(v):
    import numpy as np

    f = {n: np.asarray(a) for n, a in v.items()}
    par1 = []
    sinks = f["attn_sinks"].reshape(DEPTH, NKV, 2, 2).transpose(0, 1, 3, 2).reshape(DEPTH, NQ)
    for l in range(DEPTH):
        by_state = [np.ascontiguousarray(f[n][l].reshape(16, 2, 64).transpose(1, 2, 0)).reshape(P, 16)
                    for n in ("ssm_a_re", "ssm_a_im")]
        dt = np.broadcast_to(f["ssm_log_dt"][l].reshape(16, 2).T[:, None, :], (2, 64, 16)).reshape(P, 16)
        par1.append(np.concatenate([
            _cols(f["norm_mix"][l]), _cols(f["norm_ffn"][l]), _cols(f["b_gate"][l]), _cols(f["conv_w"][l]),
            _cols(f["ssm_d"][l]), *by_state, dt, np.broadcast_to(sinks[l], (P, NQ))], axis=1))
    bT = np.zeros((DEPTH, 4, 2, 16, 2, 4, 2, 64), np.float32)
    cT = np.zeros((DEPTH, 2, 64, 2, 4, 4, 2, 16), np.float32)
    for n, (bn, cn) in enumerate((("ssm_b_re", "ssm_c_re"), ("ssm_b_im", "ssm_c_im"))):
        b = f[bn].reshape(DEPTH, 4, 4, 2, 64, 16)
        c = f[cn].reshape(DEPTH, 4, 4, 2, 16, 64)
        for g in range(2):
            bT[:, :, g, :, n, :, g, :] = b[:, :, :, g].transpose(0, 2, 4, 1, 3)
            cT[:, g, :, n, :, :, g, :] = c[:, :, :, g].transpose(0, 4, 1, 2, 3)
    s2 = {n[:-2]: a[0] for n, a in f.items() if n.endswith("_2")}
    lambdas = np.concatenate([s2[n] for n in ("lambda_q1", "lambda_k1", "lambda_q2", "lambda_k2")])
    par2 = np.concatenate([
        _cols(f["norm_final"]), _cols(s2["c"]), _cols(s2["b_ada"]), _cols(s2["pre_norm1"]), _cols(s2["post_norm1"]),
        _cols(s2["conv_b"]), _cols(s2["conv_ln_g"]), _cols(s2["conv_ln_b"]),
        _cols(s2["conv_b_out"]), _cols(s2["head_norm"]), _cols(s2["pre_norm2"]), _cols(s2["post_norm2"]),
        _cols(s2["conv_w"]),
        np.broadcast_to(lambdas, (P, 256))], axis=1)
    ins = {"xT": f["x"][0].T, "par1": np.stack(par1), "par2": par2, "const": _consts(),
           "bT": bT.reshape(DEPTH, P, 2, 4, P), "cT": cT.reshape(DEPTH, P, 2, 4, P)}
    for n in ("w_in", "w_attn_o", "w_conv_o", "w_ssm_glu", "w_ssm_o", "w_mix_o", "w_ffn_in", "w_ffn_out"):
        ins[n] = f[n]
    for n in ("w_ada", "w_in", "conv_w_out", "w_o", "w_ff1", "w_ff2"):
        ins[n + "2"] = s2[n]
    return {n: np.ascontiguousarray(a) for n, a in ins.items()}


def kernel(**inputs):
    import numpy as np
    import concourse.bacc as bacc
    from concourse.bass_utils import run_bass_kernel_spmd

    nc = bacc.Bacc("TRN2", target_bir_lowering=False, num_devices=1)
    arrays, drams = {}, {}
    for name, a in _lay_out(inputs).items():
        arrays[f"in_{name}_dram"] = a
        drams[name] = nc.dram_tensor(f"in_{name}_dram", a.shape, mybir.dt.from_np(a.dtype), kind="ExternalInput").ap()
    drams["out"] = nc.dram_tensor("out_0_dram", (D, T), F32, kind="ExternalOutput").ap()
    build(nc, drams)
    r = run_bass_kernel_spmd(nc, [arrays], core_ids=[0])
    return np.ascontiguousarray(r.results[0]["out_0_dram"].T)[None]
```

```python
import concourse.bass as bass
from concourse import mybir
from contextlib import ExitStack, contextmanager
import math

F32 = mybir.dt.float32
F32R = mybir.dt.float32r
ALU = mybir.AluOpType
ACT = mybir.ActivationFunctionType
AX = mybir.AxisListType

P = 128
T = 512
NB = T // P
D = 1024
KD = D // P
DEPTH = 2
EPS = 1e-6
UNIT = 1024
SLOTS = 4
AHEAD = SLOTS - 1

NQ, NKV, HD = 8, 2, 64
GROUP = NQ // NKV
CONV_K = 3
SSM_PAIRS = 16
FFN = 2816
CHUNKS1 = FFN // 256
ADA_BLOCKS = 6 * 1024 // 256 // DEPTH

HEADS2, VD = 8, 128
TAPS = 31
PAD = TAPS - 1
FF2 = 4096
CHUNKS2 = FF2 // 256
LAM_INIT = 0.8 - 0.6 * math.exp(-0.3 * 0)

IN_U, IN_K, IN_V, IN_Q, IN_CB, IN_CC, IN_CX, IN_G = 2304, 512, 640, 0, 768, 1280, 1792, 2816

P1 = {}
_at = 0
for _n, _w in (("norm_mix", 8), ("norm_ffn", 8), ("b_gate", 24), ("conv_w", 12), ("ssm_d", 4), ("a_re", 16),
               ("a_im", 16), ("log_dt", 16), ("sinks", 8)):
    P1[_n] = (_at, _at + _w)
    _at += _w
NP1 = _at
P2 = {}
_at = 0
for _n, _w in (("norm_final", 8), ("c", 8), ("b_ada", 48), ("pre_norm1", 8), ("post_norm1", 8),
               ("conv_b", 8), ("conv_ln_g", 8), ("conv_ln_b", 8), ("conv_b_out", 8), ("head_norm", 1),
               ("pre_norm2", 8), ("post_norm2", 8), ("conv_w", 248), ("lambdas", 256)):
    P2[_n] = (_at, _at + _w)
    _at += _w
NP2 = _at
NP2_COLS = P2["conv_w"][0]
CONST = {}
_at = 0
for _n, _w in (("ident", 128), ("rot1", 128), ("rot2", 128), ("band", 256), ("t", 512), ("cos1", 512), ("sin1", 512),
               ("cos2", 512), ("sin2", 512)):
    CONST[_n] = (_at, _at + _w)
    _at += _w
NCONST = _at

ROUND = 1.5 * 2.0 ** 23
TWO_PI = 2.0 * math.pi
TURN = 6.2831845
PI_HI, PI_MID, PI_LO = 6.28125, 0.0019350051879882812, 3.019916050988e-07


class Count:

    def __init__(self, eng, sem, reached=0):
        self.eng, self.sem, self.base, self.k = eng, sem, 0, reached

    def done(self, ins):
        ins.then_inc(self.sem, 1)
        self.k += 1
        self.eng.wait_ge(self.sem, self.base + self.k)


@contextmanager
def rounds(eng, n, counts):
    start = {c: c.k for c in counts}
    with eng.Fori(0, n) as i:
        for c, per in counts.items():
            c.base, c.k = start[c] + i * per, 0
        yield i
        for c, per in counts.items():
            assert c.k == per, (c.sem, c.k, per)
    for c, per in counts.items():
        c.base, c.k = 0, start[c] + n * per


def build(nc, d):
    with ExitStack() as top:
        def sb(stack, name, shape, dt=F32):
            return stack.enter_context(nc.sbuf_tensor("sb_" + name, shape, dt))

        all_sems = []

        def sem(name):
            s = top.enter_context(nc.semaphore(name))
            all_sems.append(s)
            return s

        x = sb(top, "x", [P, KD, T])
        raw = sb(top, "raw", [P, SLOTS, UNIT])
        w_hi = sb(top, "w_hi", [P, SLOTS, UNIT], F32R)
        w_lo = sb(top, "w_lo", [P, SLOTS, UNIT], F32R)
        ident = sb(top, "ident", [P, P])
        band = sb(top, "band", [P, 2 * P])
        ones = sb(top, "ones", [P, 2])
        neg_half = sb(top, "neg_half", [P, 32])
        rstd = sb(top, "rstd", [P, 32])
        mod_t = sb(top, "mod", [P, 48])
        mod = mod_t[:, :]
        ps = top.enter_context(nc.psum_tensor("ps", [P, 8, T], F32))

        raw_in = [sem(f"raw_in{s}") for s in range(SLOTS)]
        hi_done = [sem(f"hi_done{s}") for s in range(SLOTS)]
        lo_done = [sem(f"lo_done{s}") for s in range(SLOTS)]
        used = [sem(f"used{s}") for s in range(SLOTS)]
        acc_free = [sem(f"acc_free{a}") for a in range(2)]
        small_in = sem("small_in")
        dve_step = sem("dve_step")
        act_step = sem("act_step")
        squares = sem("squares")
        square_sum = sem("square_sum")
        sums_done = sem("sums_done")
        mean_done = sem("mean_done")
        rstd_done = sem("rstd_done")
        spread = sem("spread")
        normed = sem("normed")
        h_hi_done = sem("h_hi_done")
        h_lo_done = sem("h_lo_done")

        def phase_end():
            nc.all_engine_barrier()
            nums = sorted(s.num for s in all_sems)
            assert nums == list(range(nums[0], nums[-1] + 1))
            nc.sync.sem_clear(range(nums[0], nums[-1] + 1))
            nc.all_engine_barrier()

        def place(u, turn0):
            return u % SLOTS, turn0 + u // SLOTS

        def load_unit(sp, u, src, turn0=0):
            s, turn = place(u, turn0)
            if not (isinstance(turn, int) and turn == 0):
                sp.wait_ge(lo_done[s], turn)
            k, n = src.shape[0] // P, src.shape[1]
            dst = raw[:, s, :].rearrange("p (k n) -> p k n", k=k)
            assert k * n == UNIT
            sp.dma_start(dst, src.rearrange("(k p) n -> p k n", p=P)).then_inc(raw_in[s], 16)

        def round_unit(act, u, turn0=0):
            s, turn = place(u, turn0)
            act.wait_ge(raw_in[s], 16 * (turn + 1))
            if not (isinstance(turn, int) and turn == 0):
                act.wait_ge(used[s], turn)
            act.activation(w_hi[:, s, :], raw[:, s, :], ACT.Copy).then_inc(hi_done[s], 1)

        def rest_unit(pool, u, turn0=0):
            s, turn = place(u, turn0)
            pool.wait_ge(hi_done[s], turn + 1)
            pool.tensor_tensor(w_lo[:, s, :], raw[:, s, :], w_hi[:, s, :].bitcast(F32), ALU.subtract)\
                .then_inc(lo_done[s], 1)

        def multiply_unit(pe, u, outs, rhs, first, last, turn0=0, only=None, ready=None):
            s, turn = place(u, turn0)
            if not only:
                pe.wait_ge(lo_done[s], turn + 1)
            n = len(outs) * P
            for o, out in enumerate(outs):
                if only is not None and o != only:
                    continue
                for i, (hi, lo) in enumerate(rhs):
                    if ready is not None and o == 0:
                        ready(i)
                    at = i * n + o * P
                    wh, wl = w_hi[:, s, at:at + P], w_lo[:, s, at:at + P]
                    pe.matmul(out, wh, hi, start=first and i == 0, stop=False)
                    pe.matmul(out, wh, lo, start=False, stop=False)
                    ins = pe.matmul(out, wl, hi, start=False, stop=last and i == len(rhs) - 1)
            if only is None or only == len(outs) - 1:
                ins.then_inc(used[s], 1)

        def multiplied(eng, u, turn0=0):
            s, turn = place(u, turn0)
            eng.wait_ge(used[s], turn + 1)

        def act_squares(act, src, sq):
            for kt in range(KD):
                act.activation(sq[:, kt, :], src[:, kt, :], ACT.Square).then_inc(squares, 1)

        def dve_add_squares(dve, steps, sq, before=0, turn=0):
            dve.wait_ge(squares, before + 1)
            for kt in range(1, KD):
                dve.wait_ge(squares, before + kt + 1)
                (steps if kt < KD - 1 else Count(dve, square_sum, turn)).done(
                    dve.tensor_tensor(sq[:, 0, :], sq[:, 0, :], sq[:, kt, :], ALU.add))

        def pe_sum(pe, sq, bank, sem_in=None, value=0, n_sq=1):
            if sem_in is not None:
                pe.wait_ge(sem_in, value)
            for n in range(NB):
                for kt in range(n_sq):
                    ins = pe.matmul(ps[:, bank, n:n + 1], sq[:, kt, n * P:(n + 1) * P], ones[:, 0:1],
                                    start=kt == 0, stop=kt == n_sq - 1)
            ins.then_inc(sums_done, 1)

        def dve_mean(dve, bank, turn, c_mean, width=NB, div=D):
            dve.wait_ge(sums_done, turn + 1)
            c_mean.done(dve.tensor_scalar(rstd[:, 0:width], ps[:, bank, 0:width], 1.0 / div, EPS, ALU.mult, ALU.add))

        def pool_rsqrt(pool, turn, width=NB):
            pool.wait_ge(mean_done, turn + 1)
            pool.tensor_tensor(rstd[:, 0:width], rstd[:, 0:width], neg_half[:, 0:width], ALU.pow).then_inc(rstd_done, 1)

        def pe_spread(pe, src, bank, sem_in, turn):
            pe.wait_ge(sem_in, turn + 1)
            for n in range(NB):
                ins = pe.matmul(ps[:, bank, n * P:(n + 1) * P], src[:, n:n + 1].to_broadcast([P, P]), ident[:, :],
                                start=True, stop=True)
            ins.then_inc(spread, 1)

        SUM_BANK, SPREAD_BANK = 7, 6

        def pe_norm(pe, sq, turn=0):
            pe_sum(pe, sq, SUM_BANK, square_sum, turn + 1)
            pe_spread(pe, rstd, SPREAD_BANK, rstd_done, turn)

        with nc.Block() as block:
            @block.sync
            def _(sp):
                sp.dma_start(x[:, :, :], d["xT"].rearrange("(k p) t -> p k t", p=P)).then_inc(small_in, 16)
                for t, n in ((ident, "ident"), (band, "band")):
                    sp.dma_start(t[:, :], d["const"][:, CONST[n][0]:CONST[n][1]]).then_inc(small_in, 16)
                sp.wait_ge(small_in, 48)

            @block.vector
            def _(dve):
                c = Count(dve, dve_step)
                c.done(dve.memset(ones[:, :], 1.0))
                c.done(dve.memset(neg_half[:, :], -0.5))
        phase_end()

        def order1():
            groups = [("u", 0), ("u", 1), ("kv", 0), ("q", 0), ("q", 1)]
            for p in range(2):
                groups += [("cc", p), ("cx", p), ("cb", p)]
            for p in range(4):
                groups += [("gc", p), ("co", p)]
            for name, n in (("ga", 4), ("gs", 4), ("ao", 4), ("gl", 2), ("so", 4), ("mx", 4)):
                groups += [(name, p) for p in range(n)]
            return groups

        G1 = order1()
        HALF = {"co", "ao", "gl", "so"}
        START1 = []
        n_units = 0
        for name, _p in G1:
            START1.append(n_units)
            n_units += 1 if name in HALF else 2
        UNITS1 = n_units
        at1 = {g: i for i, g in enumerate(G1)}
        SSM_AT = 2
        ATT_AT = at1[("co", 3)]
        ITEMS = [(n, g) for n in range(NB) for g in range(NKV)]

        bu_full = sem("bu_full")
        bu_free = sem("bu_free")
        ssm_x = sem("ssm_x")
        ssm_y = sem("ssm_y")
        ssm_y_free = sem("ssm_y_free")
        arg_done = sem("arg_done")
        frac_done = sem("frac_done")
        trig_done = sem("trig_done")
        par_act = sem("par_act")
        par_dve = sem("par_dve")
        gelu_in = sem("gelu_in")
        gelu_th = sem("gelu_th")
        ys_done = sem("ys_done")
        c7_full = sem("c7_full")
        c7_free = sem("c7_free")
        kdup = sem("kdup")
        prod_ready = sem("prod_ready")
        prod_hi = sem("prod_hi")
        prod_lo = sem("prod_lo")
        s_full = sem("s_full")
        s_max = sem("s_max")
        s_exp = sem("s_exp")
        p_ready = sem("p_ready")
        pt_full = sem("pt_full")
        pt_done = sem("pt_done")
        o_full = sem("o_full")
        o_hi = sem("o_hi")
        o_lo = sem("o_lo")
        out_done = sem("out_done")
        gt_free = sem("gt_free")
        up_free = sem("up_free")
        th_done = sem("th_done")
        hid_hi_done = sem("hid_hi_done")
        hid_lo_done = sem("hid_lo_done")
        down_free = sem("down_free")
        x_done = sem("x_done")
        x_done_odd = sem("x_done_odd")
        spilled = sem("spilled")
        clipped = sem("clipped")
        rstd_kept = sem("rstd_kept")
        x_back = sem("x_back")
        heads_done = sem("heads_done")
        exps_done = sem("exps_done")
        vt_full = sem("vt_full")
        vt_done = sem("vt_done")
        conv_done = sem("conv_done")
        centred = sem("centred")
        ln_ready = sem("ln_ready")
        ln_th = sem("ln_th")
        ln_mean = sem("ln_mean")
        glu_done = sem("glu_done")
        rope_sin = sem("rope_sin")
        tap_made = sem("tap_made")
        tap_summed = sem("tap_summed")
        half_w_done = sem("half_w_done")
        rope_done = sem("rope_done")
        pool_step = sem("pool_step")
        ada_par = sem("ada_par")
        ada_in = [sem(f"ada_in{k}") for k in range(2)]
        ada_th = sem("ada_th")
        ada_step = sem("ada_step")
        ada_used = sem("ada_used")
        ada_full = sem("ada_full")
        spill = nc.dram_tensor("x_spill", (P, KD * T), F32, kind="Internal").ap()

        def mixer1(l):
            with ExitStack() as st:
                h_hi = sb(st, "h_hi", [P, KD, T], F32R)
                h_lo = sb(st, "h_lo", [P, KD, T], F32R)
                s_hi = sb(st, "s_hi", [P, 4, T], F32R)
                s_lo = sb(st, "s_lo", [P, 4, T], F32R)
                m = sb(st, "m", [P, KD, T])
                ga = sb(st, "ga", [P, KD, T])
                gs = sb(st, "gs", [P, KD, T])
                u = sb(st, "u", [P, 4, T])
                q = sb(st, "q", [P, 4, T])
                k = sb(st, "k", [P, 2, T])
                vtok = sb(st, "vtok", [P, NB, P])
                trig = sb(st, "trig", [P, 2, 2 * T])
                bT = sb(st, "bT", [P, 2, 4, P])
                cT = sb(st, "cT", [P, 2, 4, P])
                par = sb(st, "par", [P, NP1])
                rot = sb(st, "rot", [P, P])
                trow = sb(st, "trow", [P, T])
                sin_t = sb(st, "sin_t", [P, T])
                col = sb(st, "col", [P, 16, 16])
                bias = sb(st, "bias", [P, 32])
                att = sb(st, "att", [P, 6, 4])
                z = m[:, 0:3, :].rearrange("p a t -> p (a t)")[:, 0:2 * (T + 2)].rearrange("p (a t) -> p a t", a=2)
                conv = m[:, 3:5, :]
                cc = m[:, 5:7, :]
                cos_t = m[:, 7, :]
                t1, t2, v1, v2 = (ga[:, i, :] for i in range(4))
                arg, argr = (ga[:, i:i + 2, :].rearrange("p a t -> p (a t)") for i in (4, 6))
                xo = gs[:, 0:4, :].rearrange("p (b a) t -> p b a t", b=2)
                gconv, vT, yw = gs[:, 4:6, :], gs[:, 6, :], gs[:, 7, :]
                sc = trig[:, 0, :].rearrange("p (h k) -> p h k", h=4)
                pt = trig[:, 1, :].rearrange("p (h b q) -> p h b q", h=4, b=2)

                def pcol(name, i, w=1):
                    return par[:, P1[name][0] + i:P1[name][0] + i + w]

                def banks(gi):
                    a = gi % 2
                    return ps[:, 2 * a:2 * a + 2, :]

                def full(eng, gi):
                    multiplied(eng, START1[gi] + (0 if G1[gi][0] in HALF else 1))

                def emptied(eng, gi):
                    eng.wait_ge(acc_free[gi % 2], gi // 2 + 1)

                DT, RD, TH, MAG, NN, TAU, PHC, SN, CS, LR, DEN, FR, FI, TA, TB = (col[:, i, :] for i in range(15))

                with nc.Block() as block:
                    @block.sync
                    def _(sp):
                        for t, src in ((par[:, :], d["par1"][l, :, :]), (rot[:, :], d["const"][:, CONST["rot1"][0]:CONST["rot1"][1]]),
                                       (trow[:, :], d["const"][:, CONST["t"][0]:CONST["t"][1]]),
                                       (cos_t, d["const"][:, CONST["cos1"][0]:CONST["cos1"][1]]),
                                       (sin_t[:, :], d["const"][:, CONST["sin1"][0]:CONST["sin1"][1]]),
                                       (bT[:, :, :, :], d["bT"][l, :, :, :, :]), (cT[:, :, :, :], d["cT"][l, :, :, :, :])):
                            sp.dma_start(t, src).then_inc(small_in, 16)
                        win = d["w_in"]
                        for gi, (name, p) in enumerate(G1):
                            def unit(w, k0, cols):
                                load_unit(sp, START1[gi] + k0, w[l, k0 * 512:k0 * 512 + 512, cols:cols + 256])
                            if name in ("ao", "co", "so", "gl"):
                                unit(d[{"ao": "w_attn_o", "co": "w_conv_o", "so": "w_ssm_o", "gl": "w_ssm_glu"}[name]],
                                     0, 256 * p)
                            elif name == "mx":
                                unit(d["w_mix_o"], 0, 256 * p)
                                unit(d["w_mix_o"], 1, 256 * p)
                            else:
                                at = {"u": IN_U, "kv": IN_K, "q": IN_Q, "cc": IN_CC, "cx": IN_CX, "cb": IN_CB,
                                      "gc": IN_G + D, "ga": IN_G, "gs": IN_G + 2 * D}[name] + 256 * p
                                unit(win, 0, at)
                                unit(win, 1, at)

                    @block.gpsimd
                    def _(pool):
                        fractions_at = {START1[gi] + AHEAD: gi for gi in range(2, SSM_PAIRS)}
                        fractions_at.update({SLOTS: 0, SLOTS + 1: 1})
                        for un in range(UNITS1):
                            if un == 0:
                                pool_rsqrt(pool, 0)
                            if un in fractions_at:
                                pool.wait_ge(arg_done, fractions_at[un] + 1)
                                pool.tensor_tensor(arg, argr, arg, ALU.subtract).then_inc(frac_done, 1)
                            rest_unit(pool, un)

                    @block.tensor
                    def _(pe):
                        pe_norm(pe, ga)
                        b7 = iter(range(6))

                        def rotate(src):
                            i = next(b7)
                            if i:
                                pe.wait_ge(c7_free, i)
                            pe.matmul(ps[:, 7, :], rot[:, :], src, start=True, stop=True).then_inc(c7_full, 1)

                        def inputs(s):
                            ct, j = s // 4, s % 4
                            r = slice(32 * j, 32 * j + 32)
                            if s:
                                pe.wait_ge(bu_free, s)
                            for part in range(2):
                                ins = pe.matmul(ps[:, 4 + part, :], bT[r, part, ct, :], u[r, ct, :], start=True, stop=True)
                            ins.then_inc(bu_full, 1)

                        def outputs(s):
                            ct, j = s // 4, s % 4
                            r = slice(32 * j, 32 * j + 32)
                            pe.wait_ge(ssm_x, s + 1)
                            if j == 0 and ct:
                                pe.wait_ge(ssm_y_free, ct)
                            pe.matmul(ps[r, 6, :], cT[:, 0, ct, r], xo[:, s % 2, 0, :], start=True, stop=False)
                            pe.matmul(ps[r, 6, :], cT[:, 1, ct, r], xo[:, s % 2, 1, :], start=False, stop=True)\
                                .then_inc(ssm_y, 1)

                        def scores(a):
                            n, g = ITEMS[a]
                            if a:
                                pe.wait_ge(s_max, 2 * a - 1)
                            lo = 0 if n else P
                            for hh in range(GROUP):
                                h = GROUP * g + hh
                                r = slice(64 * (h % 2), 64 * (h % 2) + 64)
                                out = ps[:, 4 + hh % 2, (hh // 2) * 256 + lo:(hh // 2) * 256 + 256]
                                ins = pe.matmul(out, q[r, h // 2, n * P:(n + 1) * P],
                                                k[r, g, (n - 1) * P + lo:(n + 1) * P], start=True, stop=True)
                            ins.then_inc(s_full, 1)

                        def probs(a):
                            n, g = ITEMS[a]
                            pe.wait_ge(p_ready, a + 1)
                            if a:
                                pe.wait_ge(o_lo, a)
                            else:
                                pe.wait_ge(ssm_y_free, 4)
                            for hh in range(GROUP):
                                for b in range(0 if n else 1, 2):
                                    at = (hh * 2 + b) * P
                                    ins = pe.transpose(ps[:, 6 + at // T, at % T:at % T + P],
                                                       sc[:, hh, b * P:(b + 1) * P], ident[:, :])
                            ins.then_inc(pt_full, 1)

                        def values(a):
                            n, g = ITEMS[a]
                            pe.wait_ge(pt_done, a + 1)
                            for hh in range(GROUP):
                                for b in range(0 if n else 1, 2):
                                    half, tile = hh // 2, hh % 2
                                    r = slice(64 * half, 64 * half + 64)
                                    ins = pe.matmul(ps[r, 6, tile * P:(tile + 1) * P],
                                                    vtok[:, n - 1 + b, 64 * g:64 * g + 64], pt[:, hh, b, :],
                                                    start=b == (0 if n else 1), stop=b == 1)
                            ins.then_inc(o_full, 1)

                        for gi, (name, p) in enumerate(G1):
                            s = gi - SSM_AT
                            a = gi - ATT_AT
                            if s == 0:
                                pe.wait_ge(small_in, 7 * 16)
                                emptied(pe, 1)
                                inputs(0)
                            if 1 <= a <= 8:
                                probs(a - 1)
                            if 0 <= a < 8:
                                if a == 0:
                                    pe.wait_ge(kdup, 32)
                                    pe.wait_ge(c7_free, 6)
                                    pe.wait_ge(bu_free, 16)
                                scores(a)
                            if gi >= 2:
                                emptied(pe, gi - 2)
                            outs = [banks(gi)[:, 0, :], banks(gi)[:, 1, :]]
                            n_u = 1 if name in HALF else 2
                            if name in ("co", "ao", "so"):
                                if name == "co":
                                    pe.wait_ge(prod_lo, 2)
                                elif name == "ao":
                                    pe.wait_ge(o_lo, 8)
                                else:
                                    pe.wait_ge(prod_lo, 5)
                                src = [(s_hi[:, i, :], s_lo[:, i, :]) for i in range(4)]
                            elif name == "gl":
                                pe.wait_ge(prod_lo, 3)
                                src = [(h_hi[:, i, :], h_lo[:, i, :]) for i in range(4)]
                            elif name == "mx":
                                src = [(h_hi[:, i, :], h_lo[:, i, :]) for i in range(8)]
                            else:
                                src = [(h_hi[:, i, :], h_lo[:, i, :]) for i in range(8)]
                            for i in range(n_u):
                                def ready(k):
                                    if gi == 0:
                                        pe.wait_ge(h_lo_done, 4 * i + k + 1)
                                    if name == "mx" and p == 0 and k % 2 == 0:
                                        pe.wait_ge(prod_lo, 5 + 2 * i + k // 2 + 1)

                                multiply_unit(pe, START1[gi] + i, outs, src[4 * i:4 * i + 4], i == 0, i == n_u - 1,
                                              ready=ready)
                                if i == 0 and 1 <= a <= 8:
                                    values(a - 1)
                            if 0 <= s:
                                if s + 1 < SSM_PAIRS:
                                    inputs(s + 1)
                                if 1 <= s <= SSM_PAIRS:
                                    outputs(s - 1)
                            if gi == 3:
                                emptied(pe, 2)
                                rotate(k[:, 0, :])
                            if gi == 4:
                                next(b7)
                                pe.wait_ge(c7_free, 1)
                                for n in range(NB):
                                    ins = pe.transpose(ps[:, 7, n * P:(n + 1) * P], vT[:, n * P:(n + 1) * P], ident[:, :])
                                ins.then_inc(c7_full, 1)
                            if 5 <= gi <= 8:
                                if gi == 5:
                                    emptied(pe, 3)
                                    emptied(pe, 4)
                                rotate(q[:, gi - 5, :])

                    @block.scalar
                    def _(act):
                        step = Count(act, act_step)
                        ahead = [0]

                        def prefetch(n):
                            while ahead[0] < min(n, UNITS1):
                                round_unit(act, ahead[0])
                                ahead[0] += 1

                        act_squares(act, x, ga)
                        pa = Count(act, par_act)
                        act.wait_ge(small_in, 7 * 16)
                        pa.done(act.activation(DT, pcol("log_dt", 0, 16), ACT.Exp))
                        prefetch(SLOTS)
                        act.wait_ge(par_dve, 1)
                        pa.done(act.activation(MAG, RD, ACT.Exp))
                        for kt in range(KD):
                            act.wait_ge(normed, kt + 1)
                            act.activation(h_hi[:, kt, :], ga[:, kt, :], ACT.Copy).then_inc(h_hi_done, 1)
                        act.wait_ge(par_dve, 2)
                        pa.done(act.activation(SN, TAU, ACT.Sin, scale=TURN))
                        pa.done(act.activation(CS, PHC, ACT.Sin, scale=-TURN))

                        args = Count(act, arg_done)
                        trigs = Count(act, trig_done)

                        def angles(s):
                            if s:
                                act.wait_ge(frac_done, s)
                            step.done(act.activation(arg[:, 0:T], trow[:, :], ACT.Copy, scale=TAU[:, s:s + 1]))
                            step.done(act.activation(arg[:, T:2 * T], trow[:, :], ACT.Identity, scale=TAU[:, s:s + 1],
                                                     bias=bias[:, 25:26]))
                            step.done(act.activation(argr[:, :], arg[:, :], ACT.Identity, bias=bias[:, 24:25]))
                            args.done(act.activation(argr[:, :], argr[:, :], ACT.Identity, bias=bias[:, 26:27]))

                        def sines(s):
                            act.wait_ge(frac_done, s + 1)
                            if s >= 2:
                                act.wait_ge(ssm_x, s - 1)
                            trigs.done(act.activation(trig[:, s % 2, :], arg[:, :], ACT.Sin, scale=-TURN))

                        def exps(a):
                            n, g = ITEMS[a]
                            lo = 0 if n else P
                            act.wait_ge(s_max, 2 * a + 2)
                            step.done(act.activation(att[:, 3, :], att[:, 2, :], ACT.Exp))
                            for hh in range(GROUP):
                                ins = act.activation(sc[:, hh, lo:], sc[:, hh, lo:], ACT.Exp, bias=att[:, 1, hh:hh + 1],
                                                     accum_out=att[:, 4, hh:hh + 1])
                                if hh == GROUP - 1:
                                    ins.then_inc(s_exp, 1)
                                else:
                                    step.done(ins)

                        def pt_copy(a):
                            act.wait_ge(pt_full, a + 1)
                            n, g = ITEMS[a]
                            src = ps[:, 6:8, :].rearrange("p a (h b q) -> p (a h) b q", b=2, q=P)
                            b0 = 0 if n else 1
                            act.activation(pt[:, :, b0:, :], src[:, :, b0:, :], ACT.Copy).then_inc(pt_done, 1)

                        def o_round(a):
                            n, g = ITEMS[a]
                            act.wait_ge(o_full, a + 1)
                            act.activation(s_hi[:, 2 * g:2 * g + 2, n * P:(n + 1) * P],
                                           ps[:, 6, 0:2 * P].rearrange("p (a q) -> p a q", a=2), ACT.Copy)\
                                .then_inc(o_hi, 1)

                        n_prod = [0]

                        def prod_round(dst, src, scale, wait=True):
                            if wait:
                                n_prod[0] += 1
                                act.wait_ge(prod_ready, n_prod[0])
                            act.activation(dst, src, ACT.Copy, scale=scale).then_inc(prod_hi, 1)

                        act.wait_ge(h_lo_done, KD)
                        for gi, (name, p) in enumerate(G1):
                            s = gi - SSM_AT
                            a = gi - ATT_AT
                            two = slice(2 * p, 2 * p + 2)
                            done = acc_free[gi % 2]
                            if 1 <= a <= 8:
                                pt_copy(a - 1)
                            if gi == 0:
                                angles(0)
                                sines(0)
                                prefetch(START1[gi] + 2 + AHEAD)
                                angles(1)
                            if s in (6, 10, 14, 18):
                                act.wait_ge(gelu_in, (s - 2) // 4)
                                act.activation(yw, yw, ACT.Tanh, scale=math.sqrt(2 / math.pi)).then_inc(gelu_th, 1)
                            if 0 <= s and s + 1 < SSM_PAIRS:
                                sines(s + 1)
                                if s + 2 < SSM_PAIRS:
                                    angles(s + 2)
                            prefetch(START1[gi] + 1 + AHEAD)
                            if 0 <= a < 8:
                                exps(a)
                            if 1 <= a <= 8:
                                o_round(a - 1)
                            if gi == 5:
                                act.wait_ge(c7_free, 1)
                                act.dma_start(k[64:128, 0, :], k[0:64, 0, :]).then_inc(kdup, 16)
                                act.dma_start(k[0:64, 1, :], k[64:128, 1, :]).then_inc(kdup, 16)
                            if name == "ao" and p == 1:
                                act.wait_ge(ys_done, 4)
                                prod_round(h_hi[:, 0:4, :], u[:, :, :], 0.5, wait=False)
                            if name not in HALF:
                                prefetch(START1[gi] + 2 + AHEAD)
                            src = banks(gi)
                            if name in ("u", "q", "cc", "kv"):
                                full(act, gi)
                                if name == "kv":
                                    step.done(act.activation(k[:, 0, :], src[:, 0, :], ACT.Copy))
                                    act.activation(vT, src[:, 1, :], ACT.Copy).then_inc(done, 1)
                                else:
                                    if name == "cc" and p == 1:
                                        emptied(act, at1[("cx", 0)])
                                    dst = {"u": u, "q": q}[name][:, two, :] if name != "cc" else cc
                                    act.activation(dst, src, ACT.Copy).then_inc(done, 1)
                            elif name in ("gc", "ga", "gs"):
                                full(act, gi)
                                dst = {"gc": gconv, "ga": ga[:, two, :], "gs": gs[:, two, :]}[name]
                                if name == "gc" and p:
                                    emptied(act, gi - 1)
                                if name == "ga" and p == 0:
                                    act.wait_ge(ssm_x, SSM_PAIRS)
                                if name == "gs" and p == 0:
                                    act.wait_ge(ssm_y, SSM_PAIRS)
                                    emptied(act, at1[("co", 3)])
                                    act.wait_ge(ys_done, 4)
                                b = {"ga": 0, "gc": 8, "gs": 16}[name] + 2 * p
                                step.done(act.activation(dst[:, 0, :], src[:, 0, :], ACT.Tanh, scale=0.5,
                                                         bias=bias[:, b:b + 1]))
                                act.activation(dst[:, 1, :], src[:, 1, :], ACT.Tanh, scale=0.5,
                                               bias=bias[:, b + 1:b + 2]).then_inc(done, 1)
                            elif name == "cb":
                                emptied(act, gi)
                                prod_round(s_hi[:, two, :], conv, 1.0, wait=False)
                            elif name == "gl":
                                full(act, gi)
                                if p:
                                    act.wait_ge(prod_ready, 1)
                                act.activation(q[:, 0:2, :], src, ACT.Tanh, scale=0.5).then_inc(done, 1)
                                prod_round(s_hi[:, two, :], q[:, 2:4, :], 0.25)
                            elif name == "so":
                                prod_round(h_hi[:, two, :], m[:, two, :], 0.5)

                    @block.vector
                    def _(dve):
                        step = Count(dve, dve_step)
                        tt, ts, stt = dve.tensor_tensor, dve.tensor_scalar, dve.scalar_tensor_tensor
                        cm = Count(dve, mean_done)
                        dve_add_squares(dve, step, ga)
                        dve.wait_ge(small_in, 7 * 16)
                        dve_mean(dve, SUM_BANK, 0, cm)
                        pd = Count(dve, par_dve)
                        step.done(ts(bias[:, 0:24], pcol("b_gate", 0, 24), 0.5, None, ALU.mult))
                        step.done(dve.memset(bias[:, 24:25], ROUND))
                        step.done(dve.memset(bias[:, 25:26], 0.25))
                        step.done(dve.memset(bias[:, 26:27], -ROUND))
                        dve.wait_ge(par_act, 1)
                        a_re, a_im = pcol("a_re", 0, 16), pcol("a_im", 0, 16)
                        step.done(tt(TH, a_im, DT, ALU.mult))
                        pd.done(tt(RD, a_re, DT, ALU.mult))
                        step.done(ts(NN, TH, 1.0 / TWO_PI, ROUND, ALU.mult, ALU.add))
                        step.done(ts(NN, NN, ROUND, None, ALU.subtract))
                        for c in (PI_HI, PI_MID, PI_LO):
                            step.done(stt(TH, NN, -c, TH, ALU.mult, ALU.add))
                        step.done(ts(TH, TH, 1.0 / TWO_PI, 0.5, ALU.mult, ALU.min))
                        step.done(ts(TAU, TH, -0.5, None, ALU.max))
                        step.done(ts(TA, TAU, 0.25, None, ALU.add))
                        step.done(ts(TB, TA, ROUND, None, ALU.add))
                        pd.done(stt(PHC, TB, ROUND, TA, ALU.subtract, ALU.subtract))

                        dve.wait_ge(spread, 1)
                        nd = Count(dve, normed)
                        for kt in range(KD + 1):
                            if kt < KD:
                                nd.done(stt(ga[:, kt, :], x[:, kt, :], pcol("norm_mix", kt), ps[:, SPREAD_BANK, :],
                                            ALU.mult, ALU.mult))
                            if kt:
                                dve.wait_ge(h_hi_done, kt)
                                tt(h_lo[:, kt - 1, :], ga[:, kt - 1, :], h_hi[:, kt - 1, :].bitcast(F32), ALU.subtract)\
                                    .then_inc(h_lo_done, 1)
                        dve.wait_ge(h_lo_done, KD)

                        dve.wait_ge(par_act, 4)
                        step.done(tt(TA, MAG, CS, ALU.mult))
                        step.done(ts(LR, TA, -1.0, None, ALU.add))
                        step.done(tt(TB, MAG, SN, ALU.mult))
                        step.done(tt(DEN, a_re, a_re, ALU.mult))
                        step.done(tt(TA, a_im, a_im, ALU.mult))
                        step.done(tt(DEN, DEN, TA, ALU.add))
                        step.done(dve.reciprocal(DEN, DEN))
                        step.done(tt(FR, LR, a_re, ALU.mult))
                        step.done(tt(TA, TB, a_im, ALU.mult))
                        step.done(tt(FR, FR, TA, ALU.add))
                        step.done(tt(FR, FR, DEN, ALU.mult))
                        step.done(tt(FI, TB, a_re, ALU.mult))
                        step.done(tt(TA, LR, a_im, ALU.mult))
                        step.done(tt(FI, FI, TA, ALU.subtract))
                        step.done(tt(FI, FI, DEN, ALU.mult))

                        def by_pair(ap):
                            return ap.rearrange("p c (j h) -> p (c j) h", j=4)

                        def flat(ap):
                            return ap.rearrange("p (s h) -> p s h", h=32)

                        c_re, c_im = by_pair(cT[:, 0, :, :]), by_pair(cT[:, 1, :, :])
                        f_re = FR.unsqueeze(2).to_broadcast([P, 16, 32])
                        f_im = FI.unsqueeze(2).to_broadcast([P, 16, 32])
                        step.done(tt(flat(t1), c_re, f_re, ALU.mult))
                        step.done(tt(flat(t2), c_im, f_im, ALU.mult))
                        step.done(tt(flat(v1), c_re, f_im, ALU.mult))
                        step.done(tt(flat(v2), c_im, f_re, ALU.mult))
                        step.done(tt(c_re, flat(t1), flat(t2), ALU.subtract))
                        step.done(stt(c_im, flat(v1), -1.0, flat(v2), ALU.mult, ALU.subtract))
                        pd.done(dve.memset(z[:, :, 0:2], 0.0))

                        n_prod = [0]
                        pr = Count(dve, prod_ready)
                        pl = Count(dve, prod_lo)

                        def prod_rest(dst_lo, dst_hi, src, scale):
                            n_prod[0] += 1
                            dve.wait_ge(prod_hi, n_prod[0])
                            if scale == 1.0:
                                pl.done(tt(dst_lo, src, dst_hi.bitcast(F32), ALU.subtract))
                            else:
                                pl.done(stt(dst_lo, src, scale, dst_hi.bitcast(F32), ALU.mult, ALU.subtract))

                        bf = Count(dve, bu_free)
                        sx = Count(dve, ssm_x)

                        def states(s):
                            dve.wait_ge(trig_done, s + 1)
                            dve.wait_ge(bu_full, s + 1)
                            sin, cos = trig[:, s % 2, 0:T], trig[:, s % 2, T:2 * T]
                            wide = [P, 2, T]
                            cos2, sin2 = cos.unsqueeze(1).to_broadcast(wide), sin.unsqueeze(1).to_broadcast(wide)
                            a, b = ga[:, 0:2, :], ga[:, 2:4, :]
                            step.done(tt(a, ps[:, 4:6, :], cos2, ALU.mult))
                            bf.done(tt(b, ps[:, 4:6, :], sin2, ALU.mult))
                            step.done(tt(t1, t1, v2, ALU.add))
                            step.done(tt(t2, t2, v1, ALU.subtract))
                            mag = MAG[:, s:s + 1].to_broadcast([P, T])
                            step.done(dve.tensor_tensor_scan(v1, mag, t1, 0.0, ALU.mult, ALU.add))
                            step.done(dve.tensor_tensor_scan(v2, mag, t2, 0.0, ALU.mult, ALU.add))
                            step.done(tt(a, b, cos2, ALU.mult))
                            step.done(tt(b, b, sin2, ALU.mult))
                            if s >= 2:
                                dve.wait_ge(ssm_y, s - 1)
                            step.done(tt(xo[:, s % 2, 0, :], t1, v2, ALU.subtract))
                            sx.done(tt(xo[:, s % 2, 1, :], v1, t2, ALU.add))

                        yf = Count(dve, ssm_y_free)
                        gi_in = Count(dve, gelu_in)
                        yd = Count(dve, ys_done)

                        def gelu_start(ct):
                            dve.wait_ge(ssm_y, 4 * ct + 4)
                            yf.done(stt(u[:, ct, :], u[:, ct, :], pcol("ssm_d", ct), ps[:, 6, :], ALU.mult, ALU.add))
                            step.done(tt(yw, u[:, ct, :], u[:, ct, :], ALU.mult))
                            step.done(ts(yw, yw, 0.044715, 1.0, ALU.mult, ALU.add))
                            gi_in.done(tt(yw, yw, u[:, ct, :], ALU.mult))

                        def gelu_end(ct):
                            dve.wait_ge(gelu_th, ct + 1)
                            yd.done(stt(u[:, ct, :], yw, 1.0, u[:, ct, :], ALU.add, ALU.mult))

                        c7 = Count(dve, c7_free)

                        def rope_tile(i, src, outs):
                            dve.wait_ge(c7_full, i + 1)
                            step.done(tt(v1, ps[:, 7, :], sin_t[:, :], ALU.mult))
                            step.done(tt(v2, src, cos_t, ALU.mult))
                            for n, (dst, r) in enumerate(outs):
                                ins = tt(dst, v1[r, :], v2[r, :], ALU.add)
                                (c7 if n == len(outs) - 1 else step).done(ins)

                        sm = Count(dve, s_max)
                        pr_ready = Count(dve, p_ready)

                        def softmax(a):
                            n, g = ITEMS[a]
                            lo = 0 if n else P
                            dve.wait_ge(s_full, a + 1)
                            if a:
                                dve.wait_ge(pt_full, a)
                            src = ps[:, 4:6, :].rearrange("p a (h k) -> p (a h) k", h=2)[:, :, lo:]
                            mask = band[:, lo:].unsqueeze(1).to_broadcast([P, 4, 2 * P - lo])
                            part = sc[:, :, lo:]
                            sm.done(stt(part, src, HD ** -0.5, mask, ALU.mult, ALU.add))
                            step.done(dve.tensor_reduce(att[:, 0, :], part, AX.X, ALU.max))
                            sink = pcol("sinks", GROUP * g, GROUP)
                            step.done(tt(att[:, 0, :], att[:, 0, :], sink, ALU.max))
                            step.done(ts(att[:, 1, :], att[:, 0, :], -1.0, None, ALU.mult))
                            sm.done(tt(att[:, 2, :], sink, att[:, 1, :], ALU.add))
                            dve.wait_ge(s_exp, a + 1)
                            step.done(tt(att[:, 5, :], att[:, 4, :], att[:, 3, :], ALU.add))
                            step.done(dve.reciprocal(att[:, 5, :], att[:, 5, :]))
                            pr_ready.done(tt(part, part, att[:, 5, :].unsqueeze(2).to_broadcast([P, 4, 2 * P - lo]), ALU.mult))

                        ol = Count(dve, o_lo)

                        def o_rest(a):
                            n, g = ITEMS[a]
                            dve.wait_ge(o_hi, a + 1)
                            r = (slice(None), slice(2 * g, 2 * g + 2), slice(n * P, (n + 1) * P))
                            ol.done(tt(s_lo[r], ps[:, 6, 0:2 * P].rearrange("p (a q) -> p a q", a=2),
                                       s_hi[r].bitcast(F32), ALU.subtract))

                        pending = []
                        for gi, (name, p) in enumerate(G1):
                            s = gi - SSM_AT
                            a = gi - ATT_AT
                            two = slice(2 * p, 2 * p + 2)
                            src = banks(gi)

                            def freed(ins):
                                ins.then_inc(acc_free[gi % 2], 1)
                                dve.wait_ge(acc_free[gi % 2], gi // 2 + 1)

                            while pending:
                                prod_rest(*pending.pop(0))
                            if 0 <= s < SSM_PAIRS:
                                states(s)
                            if s in (5, 9, 13, 17):
                                gelu_start((s - 5) // 4)
                            if s in (6, 10, 14, 18):
                                gelu_end((s - 6) // 4)
                            if 4 <= gi <= 9:
                                i = gi - 4
                                if i == 0:
                                    rope_tile(0, k[:, 0, :], [(k[0:64, 0, :], slice(0, 64)), (k[64:128, 1, :], slice(64, 128))])
                                elif i == 1:
                                    dve.wait_ge(c7_full, 2)
                                    c7.done(dve.tensor_copy(vtok[:, :, :], ps[:, 7, :].rearrange("p (n c) -> p n c", n=NB)))
                                else:
                                    rope_tile(i, q[:, i - 2, :], [(q[:, i - 2, :], slice(0, P))])
                            if 0 <= a < 8:
                                softmax(a)
                            if 1 <= a <= 8:
                                o_rest(a - 1)
                            if name == "ao" and p == 0:
                                pending.append((h_lo[:, 0:4, :], h_hi[:, 0:4, :], u[:, :, :], 0.5))
                            if name == "cx":
                                full(dve, gi)
                                emptied(dve, gi - 1)
                                freed(tt(z[:, :, 2:], src, cc, ALU.mult))
                                for i in range(2):
                                    w = [pcol("conv_w", 4 * j + 2 * p + i) for j in range(3)]
                                    step.done(ts(conv[:, i, :], z[:, i, 0:T], w[0], None, ALU.mult))
                                    for j in (1, 2):
                                        step.done(stt(conv[:, i, :], z[:, i, j:j + T], w[j], conv[:, i, :],
                                                      ALU.mult, ALU.add))
                            elif name == "cb":
                                full(dve, gi)
                                freed(tt(conv, src, conv, ALU.mult))
                                pending.append((s_lo[:, two, :], s_hi[:, two, :], conv, 1.0))
                            elif name == "co":
                                full(dve, gi)
                                emptied(dve, gi - 1)
                                freed(stt(m[:, two, :], gconv, 1.0, src, ALU.add, ALU.mult))
                            elif name in ("ao", "so"):
                                gate = {"ao": ga, "so": gs}[name][:, two, :]
                                full(dve, gi)
                                emptied(dve, at1[({"ao": "ga", "so": "gs"}[name], p)])
                                freed(stt(gate, gate, 1.0, src, ALU.add, ALU.mult))
                                if name == "ao":
                                    step.done(tt(m[:, two, :], m[:, two, :], gate, ALU.add))
                                else:
                                    pr.done(tt(m[:, two, :], m[:, two, :], gate, ALU.add))
                                    pending.append((h_lo[:, two, :], h_hi[:, two, :], m[:, two, :], 0.5))
                            elif name == "gl":
                                emptied(dve, gi)
                                pr.done(stt(q[:, 2:4, :], q[:, 0:2, :], 1.0, u[:, two, :], ALU.add, ALU.mult))
                                pending.append((s_lo[:, two, :], s_hi[:, two, :], q[:, 2:4, :], 0.25))
                            elif name == "mx":
                                full(dve, gi)
                                freed(tt(x[:, two, :], x[:, two, :], src, ALU.add))
                phase_end()

        def ffn(kind, l):
            chunks = CHUNKS1 if kind == 1 else CHUNKS2
            ups = 4 if kind == 1 else 2
            per = ups + 2
            down_at = (2, 5) if kind == 1 else (1, 3)
            up_at = (0, 1, 3, 4) if kind == 1 else (0, 2)
            peeled = 1 if kind == 1 else 2
            n_rounds = (chunks - peeled) // 2
            first_u = ups + (peeled - 1) * per
            ahead = 2
            total = ups + (chunks - 1) * per + 2
            assert (2 * per) % SLOTS == 0 and peeled + 2 * n_rounds == chunks
            turns = 2 * per // SLOTS
            with ExitStack() as st:
                tag = f"f{kind}_"
                h_hi = sb(st, tag + "h_hi", [P, KD, T], F32R)
                h_lo = sb(st, tag + "h_lo", [P, KD, T], F32R)
                hid_hi = sb(st, tag + "hid_hi", [P, 2, 2, T], F32R)
                hid_lo = sb(st, tag + "hid_lo", [P, 2, 2, T], F32R)
                sq = sb(st, tag + "sq", [P, KD, T])
                th = sb(st, tag + "th", [P, 2, T])
                act_in = sb(st, tag + "act_in", [P, 2, T])
                par = sb(st, tag + "par", [P, NP1 if kind == 1 else NP2_COLS])
                sums = x if kind == 1 else sb(st, "f2_sums", [P, KD, T])
                scale = sb(st, tag + "scale", [P, 16])
                if kind == 1:
                    ada = sb(st, "ada", [P, 2, UNIT])
                    ada_sums = sb(st, "ada_sums", [P, ADA_BLOCKS * 256])
                    c_col = sb(st, "c_col", [P, 3, 8])
                    b_ada = sb(st, "b_ada", [P, 2 * ADA_BLOCKS])

                with nc.Block() as block:
                    @block.sync
                    def _(sp):
                        sp.dma_start(par[:, :], d["par1"][l, :, :] if kind == 1 else d["par2"][:, 0:NP2_COLS]).then_inc(small_in, 16)

                        def load_up(c, u, turn0, i):
                            rows = slice(512 * (i % 2), 512 * (i % 2) + 512)
                            if kind == 1:
                                src = d["w_ffn_in"][l, rows, bass.ds(c * 256 + (FFN if i >= 2 else 0), 256)]
                            else:
                                src = d["w_ff12"][rows, bass.ds(c * 256, 256)]
                            load_unit(sp, u, src, turn0)

                        def load_down(c, u, turn0, i):
                            cols = slice(512 * i, 512 * i + 512)
                            if kind == 1:
                                src = d["w_ffn_out"][l, bass.ds(c * 256, 256), cols]
                            else:
                                src = d["w_ff22"][bass.ds(c * 256, 256), cols]
                            load_unit(sp, u, src, turn0)

                        def load_chunk(c, u, turn0):
                            for n in range(per):
                                if n in down_at:
                                    load_down(c - 1, u + n, turn0, down_at.index(n))
                                else:
                                    load_up(c, u + n, turn0, up_at.index(n))

                        def load_ada(block):
                            if not (isinstance(block, int) and block == 0):
                                sp.wait_ge(ada_used, block)
                            for k in range(2):
                                src = d["w_ada2"][512 * k:512 * k + 512, bass.ds(l * (256 * ADA_BLOCKS) + block * 256, 256)]
                                sp.dma_start(ada[:, k, :].rearrange("p (k n) -> p k n", k=4),
                                             src.rearrange("(k p) n -> p k n", p=P)).then_inc(ada_in[k], 16)

                        for n in range(ups):
                            load_up(0, n, 0, n)
                        if kind == 1:
                            sp.dma_start(c_col[:, 0, :], d["par2"][:, P2["c"][0]:P2["c"][1]]).then_inc(ada_par, 16)
                            sp.dma_start(b_ada[:, :], d["par2"][:, bass.ds(l * (2 * ADA_BLOCKS) + P2["b_ada"][0],
                                                                           2 * ADA_BLOCKS)]).then_inc(ada_par, 16)
                            load_ada(0)
                            load_ada(1)
                        for c in range(1, peeled):
                            load_chunk(c, ups + (c - 1) * per, 0)
                        with sp.Fori(0, n_rounds) as i:
                            for n in range(2):
                                load_chunk(2 * i + (peeled + n), first_u + n * per, i * turns)
                                if kind == 1:
                                    load_ada(2 * i + (peeled + 1 + n))
                        for n in range(2):
                            load_down(chunks - 1, total - 2 + n, 0, n)
                        if kind == 2:
                            out = d["out"].rearrange("(k p) t -> p k t", p=P)
                            for kt in range(0, KD, 2):
                                sp.wait_ge(x_done, 3 * (kt // 2) + 2)
                                sp.wait_ge(x_done_odd, kt // 2 + 1)
                                sp.dma_start(out[:, kt:kt + 2, :], x[:, kt:kt + 2, :]).then_inc(out_done, 16)
                            sp.wait_ge(out_done, 16 * (KD // 2))

                    @block.gpsimd
                    def _(pool):
                        for n in range(first_u):
                            if n == 0:
                                pool_rsqrt(pool, 0)
                            rest_unit(pool, n)
                        with pool.Fori(0, n_rounds) as i:
                            for n in range(2 * per):
                                rest_unit(pool, first_u + n, i * turns)
                        for n in range(total - 2, total):
                            rest_unit(pool, n)
                        if kind == 2:
                            pool_rsqrt(pool, 1)
                            for kt in range(1, KD, 2):
                                pool.wait_ge(x_done, 3 * (kt // 2) + 3)
                                pool.tensor_tensor(x[:, kt, :], x[:, kt, :], sums[:, kt, :], ALU.add).then_inc(x_done_odd, 1)

                    @block.tensor
                    def _(pe):
                        pe_norm(pe, sq)
                        h = [(h_hi[:, i, :], h_lo[:, i, :]) for i in range(KD)]

                        def go_up(c, u, turn0, i, parity, first):
                            b = 2 * (i // 2) if kind == 1 else 2 * parity
                            if i % 2 == 0 and not first:
                                if kind == 1:
                                    pe.wait_ge(up_free if i else gt_free, c)
                                else:
                                    pe.wait_ge(th_done, c - 1)
                            k = i % 2
                            ready = None
                            if isinstance(c, int) and c == 0 and i < 2:
                                def ready(kt):
                                    pe.wait_ge(h_lo_done, 4 * k + kt + 1)
                            multiply_unit(pe, u, [ps[:, b, :], ps[:, b + 1, :]], h[4 * k:4 * k + 4], k == 0, k == 1, turn0,
                                          ready=ready)

                        def go_down(c, u, turn0, i, parity, first):
                            if i == 0:
                                pe.wait_ge(hid_lo_done, c + 1)
                            if i or not first:
                                pe.wait_ge(down_free, 2 * c + i)
                            multiply_unit(pe, u, [ps[:, 4 + o, :] for o in range(4)],
                                          [(hid_hi[:, parity, k, :], hid_lo[:, parity, k, :]) for k in range(2)],
                                          True, True, turn0)

                        def chunk(c, u, turn0, parity, first=False):
                            for n in range(per):
                                if n in down_at:
                                    go_down(c - 1, u + n, turn0, down_at.index(n), 1 - parity, first)
                                else:
                                    go_up(c, u + n, turn0, up_at.index(n), parity, first and kind == 2)

                        for n in range(ups):
                            go_up(0, n, 0, n, 0, True)
                        for c in range(1, peeled):
                            chunk(c, ups + (c - 1) * per, 0, c % 2, first=True)
                        with pe.Fori(0, n_rounds) as i:
                            for n in range(2):
                                chunk(2 * i + (peeled + n), first_u + n * per, i * turns, (peeled + n) % 2)
                        go_down(chunks - 1, total - 2, 0, 0, (chunks - 1) % 2, False)
                        if kind == 1:
                            pe.wait_ge(gt_free, chunks)
                            pe.wait_ge(ada_used, ADA_BLOCKS)
                            for n in range(2 * ADA_BLOCKS):
                                ins = pe.matmul(ps[:, 0, n:n + 1], ada_sums[:, n * P:(n + 1) * P], ones[:, 0:1],
                                                start=True, stop=True)
                            ins.then_inc(ada_full, 1)
                        go_down(chunks - 1, total - 1, 0, 1, (chunks - 1) % 2, False)
                        if kind == 2:
                            pe_sum(pe, sq, SUM_BANK, square_sum, 2)
                            pe_spread(pe, rstd, SPREAD_BANK, rstd_done, 1)

                    @block.scalar
                    def _(act):
                        act_squares(act, x, sq)
                        for n in range(SLOTS):
                            round_unit(act, n)
                        for kt in range(KD):
                            act.wait_ge(normed, kt + 1)
                            shift = 0.0 if kind == 1 else mod[:, 24 + kt:25 + kt]
                            act.activation(h_hi[:, kt, :], sq[:, kt, :], ACT.Identity, bias=shift)\
                                .then_inc(h_hi_done, 1)
                        tanh = Count(act, th_done)
                        hid = Count(act, hid_hi_done)
                        if kind == 1:
                            act.wait_ge(ada_par, 32)
                            act.activation(c_col[:, 1, :], c_col[:, 0, :], ACT.Tanh, scale=0.5).then_inc(ada_th, 1)

                        def chunk(c, u, turn0, parity, whole, start=0):
                            steps = [n for n in range(per)] if whole else [up_at[n] for n in range(ups)]
                            for at, n in enumerate(steps):
                                if at >= start:
                                    round_unit(act, u + at + ahead, turn0)
                                if kind == 1 and n == up_at[1]:
                                    multiplied(act, u + at, turn0)
                                    if not (isinstance(c, int) and c == 0):
                                        act.wait_ge(gt_free, c)
                                    tanh.done(act.activation(th[:, :, :], ps[:, 0:2, :], ACT.Tanh, scale=0.5))
                                if n == up_at[-1]:
                                    if kind == 2:
                                        multiplied(act, u + at, turn0)
                                        if not (isinstance(c, int) and c == 0):
                                            act.wait_ge(up_free, c)
                                        b = 2 * parity
                                        tanh.done(act.activation(th[:, :, :], ps[:, b:b + 2, :], ACT.Relu))
                                    act.wait_ge(up_free, c + 1)
                                    hid.done(act.activation(hid_hi[:, parity, :, :], act_in[:, :, :], ACT.Copy))

                        chunk(0, 0, 0, 0, False, start=SLOTS - ahead)
                        for c in range(1, peeled):
                            chunk(c, ups + (c - 1) * per, 0, c % 2, True, start=max(0, SLOTS - ahead - ups))
                        with rounds(act, n_rounds, {tanh: 2, hid: 2}) as i:
                            for n in range(2):
                                chunk(2 * i + (peeled + n), first_u + n * per, i * turns, (peeled + n) % 2, True)
                        if kind == 2:
                            for kt in range(KD):
                                if kt % 4 == 0:
                                    act.wait_ge(down_free, 2 * chunks - 1 + kt // 4)
                                act.activation(sq[:, kt, :], sums[:, kt, :], ACT.Square).then_inc(squares, 1)

                    @block.vector
                    def _(dve):
                        step = Count(dve, dve_step)
                        tt, ts, stt = dve.tensor_tensor, dve.tensor_scalar, dve.scalar_tensor_tensor
                        dve.wait_ge(small_in, 16)
                        if kind == 1:
                            gain = par[:, P1["norm_ffn"][0]:P1["norm_ffn"][1]]
                        else:
                            gain = scale[:, 0:8]
                            step.done(stt(gain, mod[:, 32:40], 1.0, par[:, P2["pre_norm2"][0]:P2["pre_norm2"][1]],
                                          ALU.add, ALU.mult))
                            step.done(tt(scale[:, 8:16], mod[:, 40:48], par[:, P2["post_norm2"][0]:P2["post_norm2"][1]],
                                         ALU.mult))
                        cm = Count(dve, mean_done)
                        nd = Count(dve, normed)
                        dve_add_squares(dve, step, sq)
                        dve_mean(dve, SUM_BANK, 0, cm)
                        dve.wait_ge(spread, 1)
                        for kt in range(KD + 1):
                            if kt < KD:
                                nd.done(stt(sq[:, kt, :], x[:, kt, :], gain[:, kt:kt + 1], ps[:, SPREAD_BANK, :],
                                            ALU.mult, ALU.mult))
                            if kt:
                                dve.wait_ge(h_hi_done, kt)
                                shift = 0.0 if kind == 1 else mod[:, 23 + kt:24 + kt]
                                stt(h_lo[:, kt - 1, :], sq[:, kt - 1, :], shift, h_hi[:, kt - 1, :].bitcast(F32),
                                    ALU.add, ALU.subtract).then_inc(h_lo_done, 1)
                        dve.wait_ge(h_lo_done, KD)
                        if kind == 2:
                            step.done(dve.memset(sums[:, :, :], 0.0))
                        gf, uf, hl, df = (Count(dve, q) for q in (gt_free, up_free, hid_lo_done, down_free))

                        def add_down(u, turn0, i):
                            multiplied(dve, u, turn0)
                            out = sums[:, 4 * i:4 * i + 4, :]
                            df.done(tt(out, out, ps[:, 4:8, :], ALU.add))

                        def chunk(c, u, turn0, parity, whole):
                            steps = [n for n in range(per)] if whole else [up_at[n] for n in range(ups)]
                            for at, n in enumerate(steps):
                                if n in down_at:
                                    add_down(u + at, turn0, down_at.index(n))
                                elif kind == 1 and n == up_at[1]:
                                    dve.wait_ge(th_done, c + 1)
                                    gf.done(stt(act_in[:, :, :], th[:, :, :], 1.0, ps[:, 0:2, :], ALU.add, ALU.mult))
                                elif n == up_at[-1]:
                                    if kind == 1:
                                        multiplied(dve, u + at, turn0)
                                        uf.done(stt(act_in[:, :, :], act_in[:, :, :], 0.5, ps[:, 2:4, :],
                                                    ALU.mult, ALU.mult))
                                    else:
                                        dve.wait_ge(th_done, c + 1)
                                        uf.done(tt(act_in[:, :, :], th[:, :, :], th[:, :, :], ALU.mult))
                                    dve.wait_ge(hid_hi_done, c + 1)
                                    hl.done(tt(hid_lo[:, parity, :, :], act_in[:, :, :],
                                               hid_hi[:, parity, :, :].bitcast(F32), ALU.subtract))

                        ada_steps, au = Count(dve, ada_step), Count(dve, ada_used)

                        def add_ada(block):
                            out = ada_sums[:, bass.ds(block * 256, 256)]
                            for kt in range(KD):
                                if kt % 4 == 0:
                                    dve.wait_ge(ada_in[kt // 4], 16 * block + 16)
                                src, w = ada[:, kt // 4, 256 * (kt % 4):256 * (kt % 4) + 256], c_col[:, 2, kt:kt + 1]
                                if kt == 0:
                                    ada_steps.done(ts(out, src, w, None, ALU.mult))
                                else:
                                    (au if kt == KD - 1 else ada_steps).done(stt(out, src, w, out, ALU.mult, ALU.add))

                        if kind == 1:
                            dve.wait_ge(ada_th, 1)
                            step.done(stt(c_col[:, 1, :], c_col[:, 1, :], 1.0, c_col[:, 0, :], ALU.add, ALU.mult))
                            step.done(ts(c_col[:, 2, :], c_col[:, 1, :], 0.5, None, ALU.mult))
                            add_ada(0)
                        chunk(0, 0, 0, 0, False)
                        if kind == 1:
                            add_ada(1)
                        for c in range(1, peeled):
                            chunk(c, ups + (c - 1) * per, 0, c % 2, True)
                        counts = {uf: 2, hl: 2, df: 4}
                        if kind == 1:
                            counts.update({gf: 2, ada_steps: 2 * (KD - 1), au: 2})
                        with rounds(dve, n_rounds, counts) as i:
                            for n in range(2):
                                chunk(2 * i + (peeled + n), first_u + n * per, i * turns, (peeled + n) % 2, True)
                                if kind == 1:
                                    add_ada(2 * i + (peeled + 1 + n))
                        if kind == 1:
                            dve.wait_ge(ada_full, 1)
                            step.done(tt(mod[:, bass.ds(l * (2 * ADA_BLOCKS), 2 * ADA_BLOCKS)], ps[:, 0, 0:2 * ADA_BLOCKS],
                                         b_ada[:, :], ALU.add))
                        for n in range(2):
                            add_down(total - 2 + n, 0, n)
                        if kind == 2:
                            dve_add_squares(dve, step, sq, KD, 1)
                            dve_mean(dve, SUM_BANK, 1, cm)
                            dve.wait_ge(spread, 2)
                            xd = Count(dve, x_done)
                            for kt in range(KD):
                                xd.done(stt(sums[:, kt, :], sums[:, kt, :], scale[:, 8 + kt:9 + kt],
                                            ps[:, SPREAD_BANK, :], ALU.mult, ALU.mult))
                                if kt % 2 == 0:
                                    xd.done(tt(x[:, kt, :], x[:, kt, :], sums[:, kt, :], ALU.add))
                phase_end()

        def final_norm():
            with ExitStack() as st:
                sq = sb(st, "n_sq", [P, KD, T])
                gain = sb(st, "n_gain", [P, KD])
                with nc.Block() as block:
                    @block.sync
                    def _(sp):
                        sp.dma_start(gain[:, :], d["par2"][:, P2["norm_final"][0]:P2["norm_final"][1]]).then_inc(small_in, 16)

                    @block.gpsimd
                    def _(pool):
                        pool_rsqrt(pool, 0)

                    @block.tensor
                    def _(pe):
                        pe_norm(pe, sq)

                    @block.scalar
                    def _(act):
                        act_squares(act, x, sq)

                    @block.vector
                    def _(dve):
                        step = Count(dve, dve_step)
                        cm = Count(dve, mean_done)
                        dve_add_squares(dve, step, sq)
                        dve_mean(dve, SUM_BANK, 0, cm)
                        dve.wait_ge(small_in, 16)
                        dve.wait_ge(spread, 1)
                        for kt in range(KD):
                            step.done(dve.scalar_tensor_tensor(x[:, kt, :], x[:, kt, :], gain[:, kt:kt + 1],
                                                               ps[:, SPREAD_BANK, :], ALU.mult, ALU.mult))
                phase_end()

        def order2():
            groups = []
            for p in range(4):
                groups += [("ua", p), ("ub", p)]
            for name in ("q", "k", "v", "gc", "ga", "cv", "wo"):
                groups += [(name, p) for p in range(4)]
            return groups

        G2 = order2()
        UNITS2 = 2 * len(G2)
        at2 = {g: i for i, g in enumerate(G2)}
        COL2 = {"ua": 0, "ub": D, "q": 2 * D, "k": 3 * D, "v": 4 * D, "gc": 5 * D, "ga": 6 * D}
        CONV_AT = 2
        SIDE_TAPS = 6
        FIRST_SIDE = TAPS - SIDE_TAPS
        LN_AT = 18
        ITEM_AT = 21
        ITEMS2 = [(h, n) for h in range(HEADS2) for n in range(NB)]
        HALVES = 4
        N_STEPS = len(ITEMS2) + 3
        STEPS_AT = {}
        for _i in range(N_STEPS):
            _h = 3 + _i * (HALVES * (at2[("wo", 0)] - ITEM_AT) - 3) // N_STEPS
            STEPS_AT.setdefault((ITEM_AT + _h // HALVES, _h % HALVES), []).append(_i)

        HEADS_AT = {at2[("cv", 0)]: (0, 1, 2, 3), at2[("cv", 1)]: (4, 5), at2[("cv", 2)]: (6,), at2[("cv", 3)]: (7,)}

        def mixer2():
            with ExitStack() as st:
                h_hi = sb(st, "m_h_hi", [P, KD, T], F32R)
                h_lo = sb(st, "m_h_lo", [P, KD, T], F32R)
                u = sb(st, "m_u", [P, KD, PAD + T])
                conv = sb(st, "m_conv", [P, KD, T])
                q = sb(st, "m_q", [P, KD, T])
                k = sb(st, "m_k", [P, KD, T])
                vtok = sb(st, "m_vtok", [P, NB, D])
                gc = sb(st, "m_gc", [P, KD, T])
                pr = sb(st, "m_pr", [P, 2, 2, T])
                pt = sb(st, "m_pt", [P, 2, T])
                par = sb(st, "m_par", [P, NP2_COLS])
                small = sb(st, "m_small", [P, 88])
                ga = sq = ln_tanh = u[:, :, 0:T]
                vT = gc
                att = x
                cos_t, sin_t = pr[:, 0, 0, :], pr[:, 0, 1, :]
                rot, taps_w = pr[:, 1, 0, 0:P], pr[:, 1, 1, 0:TAPS * KD]
                tmp, lambdas = pt[:, 0, :], pt[:, 1, 0:4 * HD]
                glu_a, glu_b = q[:, 0:2, :], q[:, 2:4, :]
                gain1, gain_post, neg_lam, head_gain, lam_t = (small[:, 0:8], small[:, 8:16], small[:, 16:17],
                                                               small[:, 17:18], small[:, 18:22])
                stat = [small[:, 24 + 16 * b:40 + 16 * b] for b in range(2)]

                in_range = small[:, 56:88]
                tap_sum, tap_prod = gc[:, 4, :], [gc[:, 5 + m, :] for m in range(3)]
                half_w = pr[:, 1, 1, 256:256 + SIDE_TAPS * KD]

                def pcol(name, i=0, w=1):
                    return par[:, P2[name][0] + i:P2[name][0] + i + w]

                def banks(gi):
                    return ps[:, 2 * (gi % 2):2 * (gi % 2) + 2, :]

                def full(eng, gi):
                    multiplied(eng, 2 * gi + 1)

                def emptied(eng, gi):
                    eng.wait_ge(acc_free[gi % 2], gi // 2 + 1)

                with nc.Block() as block:
                    @block.sync
                    def _(sp):
                        sp.dma_start(par[:, :], d["par2"][:, 0:NP2_COLS]).then_inc(small_in, 16)
                        for t, n in ((taps_w, "conv_w"), (lambdas, "lambdas")):
                            sp.dma_start(t, d["par2"][:, P2[n][0]:P2[n][1]]).then_inc(small_in, 16)
                        for t, n in ((rot, "rot2"), (cos_t, "cos2"), (sin_t, "sin2")):
                            sp.dma_start(t, d["const"][:, CONST[n][0]:CONST[n][1]]).then_inc(small_in, 16)

                        def group(gi):
                            name, p = G2[gi]
                            w = {"cv": d["conv_w_out2"], "wo": d["w_o2"]}.get(name, d["w_in2"])
                            c = COL2.get(name, 0) + 256 * p
                            for i in range(2):
                                load_unit(sp, 2 * gi + i, w[512 * i:512 * i + 512, c:c + 256])

                        for gi in range(len(G2)):
                            group(gi)
                            if gi == 3:
                                sp.wait_ge(h_lo_done, KD)
                                sp.dma_start(spill, x[:, :, :].rearrange("p k t -> p (k t)")).then_inc(spilled, 16)
                            if gi == at2[("wo", 1)]:
                                sp.wait_ge(spilled, 16)
                                sp.wait_ge(heads_done, HEADS2)
                                sp.dma_start(q[:, :, :].rearrange("p k t -> p (k t)"), spill).then_inc(x_back, 16)

                    @block.gpsimd
                    def _(pool):
                        pool_steps, roped = Count(pool, pool_step), Count(pool, rope_done)
                        summed = Count(pool, tap_summed)
                        for un in range(UNITS2):
                            if un == 0:
                                pool_rsqrt(pool, 0)
                            half = (un - 1) // 2 - CONV_AT
                            if un % 2 == 0 and 0 <= half < 2 * KD:
                                for m in range(3):
                                    if half % 2 == 0 and m == 0:
                                        if half:
                                            pool.wait_ge(conv_done, half)
                                        continue
                                    pool.wait_ge(tap_made, 3 * half + m + 1)
                                    first = half % 2 == 0 and m == 1
                                    summed.done(pool.tensor_tensor(tap_sum, tap_prod[0] if first else tap_sum, tap_prod[m],
                                                                   ALU.add))
                            if un % 2 == 1 and 11 <= un // 2 <= 18:
                                i = un // 2 - 11
                                dst = (q if i < 4 else k)[:, 2 * (i % 4):2 * (i % 4) + 2, :]
                                emptied(pool, 8 + i)
                                for o in range(2):
                                    pool.wait_ge(rope_sin, 2 * i + o + 1)
                                    pool_steps.done(pool.tensor_tensor(dst[:, o, :], dst[:, o, :], cos_t, ALU.mult))
                                    roped.done(pool.tensor_tensor(dst[:, o, :], dst[:, o, :], pt[:, o, :], ALU.add))
                            if un == 2 * (LN_AT + 3):
                                pool_rsqrt(pool, 1)
                            if un == 2 * at2[("wo", 1)] + 1:
                                pool_rsqrt(pool, 2, width=32)
                            rest_unit(pool, un)
                        pool_rsqrt(pool, 3)
                        for kt in range(1, KD, 2):
                            pool.wait_ge(x_done, 3 * (kt // 2) + 3)
                            pool.tensor_tensor(x[:, kt, :], x[:, kt, :], q[:, kt, :], ALU.add).then_inc(x_done_odd, 1)

                    @block.tensor
                    def _(pe):
                        pe_norm(pe, sq)
                        h = [(h_hi[:, i, :], h_lo[:, i, :]) for i in range(KD)]

                        def scores(i):
                            hd, n = ITEMS2[i]
                            if i:
                                pe.wait_ge(exps_done, 2 * i)
                            else:
                                pe.wait_ge(vt_done, 4)
                                pe.wait_ge(rope_done, 16)
                            r = slice(64 * (hd % 2), 64 * (hd % 2) + 64)
                            for c in range(2):
                                t = 4 * c + hd // 2
                                ins = pe.matmul(ps[:, 4 + c, 0:(n + 1) * P], q[r, t, n * P:(n + 1) * P],
                                                k[r, t, 0:(n + 1) * P], start=True, stop=True)
                            ins.then_inc(s_full, 1)

                        def probs(i):
                            hd, n = ITEMS2[i]
                            pe.wait_ge(p_ready, i + 1)
                            if i:
                                pe.wait_ge(pt_done, i)
                            for b in range(n + 1):
                                ins = pe.transpose(ps[:, 6, b * P:(b + 1) * P], pr[:, i % 2, 0, b * P:(b + 1) * P], ident[:, :])
                            ins.then_inc(pt_full, 1)

                        def values(i):
                            hd, n = ITEMS2[i]
                            pe.wait_ge(pt_done, i + 1)
                            if i:
                                pe.wait_ge(o_hi, i)
                            for b in range(n + 1):
                                ins = pe.matmul(ps[:, 7, 0:P], vtok[:, b, hd * P:(hd + 1) * P],
                                                pt[:, i % 2, b * P:(b + 1) * P], start=b == 0, stop=b == n)
                            ins.then_inc(o_full, 1)

                        def slot(i):
                            if 3 <= i:
                                values(i - 3)
                            if 2 <= i < len(ITEMS2) + 2:
                                probs(i - 2)
                            if i < len(ITEMS2):
                                scores(i)

                        for gi, (name, p) in enumerate(G2):
                            if gi >= 2:
                                emptied(pe, gi - 2)
                            outs = [banks(gi)[:, 0, :], banks(gi)[:, 1, :]]
                            if gi == LN_AT:
                                pe.wait_ge(conv_done, 16)
                                pe.wait_ge(rope_sin, 16)
                                pe_sum(pe, conv, SUM_BANK, n_sq=KD)
                            if gi == LN_AT + 2:
                                pe_sum(pe, sq, SUM_BANK, squares, 2 * KD, n_sq=KD)
                            if name == "wo" and p == 0:
                                pe.wait_ge(squares, 3 * KD)
                                pe.wait_ge(o_hi, len(ITEMS2))
                                for i, (hd, n) in enumerate(ITEMS2):
                                    ins = pe.matmul(ps[:, 4, i:i + 1], conv[:, hd, n * P:(n + 1) * P], ones[:, 0:1],
                                                    start=True, stop=True)
                                ins.then_inc(sums_done, 1)
                                pe.wait_ge(rstd_kept, 1)
                                for hd in range(HEADS2):
                                    if hd >= 4:
                                        pe.wait_ge(heads_done, hd - 3)
                                    for n in range(NB):
                                        i = hd * NB + n
                                        ins = pe.matmul(ps[:, 4 + hd % 4, n * P:(n + 1) * P],
                                                        rstd[:, i:i + 1].to_broadcast([P, P]), ident[:, :], start=True, stop=True)
                                    ins.then_inc(spread, 1)
                            for half in range(HALVES):
                                i, o = half // 2, half % 2
                                for s in STEPS_AT.get((gi, half), []):
                                    slot(s)

                                def ready(kt):
                                    if gi == 0:
                                        pe.wait_ge(h_lo_done, 4 * i + kt + 1)
                                    if name == "cv" and p == 0:
                                        pe.wait_ge(prod_lo, 4 * i + kt + 1)
                                    if name == "wo" and p == 0:
                                        pe.wait_ge(prod_lo, 8 + 4 * i + kt + 1)

                                multiply_unit(pe, 2 * gi + i, outs, h[4 * i:4 * i + 4], i == 0, i == 1, only=o, ready=ready)
                            if gi == LN_AT:
                                pe_spread(pe, rstd, SPREAD_BANK, ln_mean, 0)
                            if gi == LN_AT + 2:
                                pe_spread(pe, rstd, SPREAD_BANK, rstd_done, 1)
                            if 9 <= gi <= 16:
                                src = (q if gi < 13 else k)[:, 2 * ((gi - 9) % 4):2 * ((gi - 9) % 4) + 2, :]
                                emptied(pe, gi - 1)
                                if gi > 9:
                                    pe.wait_ge(rope_sin, 2 * (gi - 9))
                                for o in range(2):
                                    ins = pe.matmul(ps[:, 6 + o, :], rot, src[:, o, :], start=True, stop=True)
                                ins.then_inc(c7_full, 1)
                            if 17 <= gi <= 20:
                                w = gi - 17
                                emptied(pe, gi - 1)
                                if w:
                                    pe.wait_ge(vt_done, w)
                                for o in range(2):
                                    for n in range(NB):
                                        ins = pe.transpose(ps[:, 4 + o, n * P:(n + 1) * P],
                                                           vT[:, 2 * w + o, n * P:(n + 1) * P], ident[:, :])
                                ins.then_inc(vt_full, 1)
                        pe_sum(pe, conv, SUM_BANK, square_sum, 2)
                        pe_spread(pe, rstd, SPREAD_BANK, rstd_done, 3)

                    @block.scalar
                    def _(act):
                        step = Count(act, act_step)
                        ahead = [0]

                        def prefetch(n):
                            while ahead[0] < min(n, UNITS2):
                                round_unit(act, ahead[0])
                                ahead[0] += 1

                        act_squares(act, x, sq)
                        prefetch(SLOTS)
                        for kt in range(KD):
                            act.wait_ge(normed, kt + 1)
                            act.activation(h_hi[:, kt, :], sq[:, kt, :], ACT.Identity, bias=mod[:, kt:kt + 1])\
                                .then_inc(h_hi_done, 1)
                        pa = Count(act, par_act)
                        act.wait_ge(par_dve, 1)
                        pa.done(act.activation(lam_t[:, 2:4], lam_t[:, 0:2], ACT.Exp))

                        def exps(i):
                            hd, n = ITEMS2[i]
                            w = (n + 1) * P
                            act.wait_ge(s_max, i + 1)
                            if i >= 2:
                                act.wait_ge(pt_full, i - 1)
                            for c in range(2):
                                ed.done(act.activation(pr[:, i % 2, c, 0:w], ps[:, 4 + c, 0:w], ACT.Exp, scale=HD ** -0.5,
                                                       bias=stat[i % 2][:, 2 + c:3 + c],
                                                       accum_out=stat[i % 2][:, 4 + c:5 + c]))

                        def pt_copy(i):
                            hd, n = ITEMS2[i]
                            w = (n + 1) * P
                            act.wait_ge(pt_full, i + 1)
                            act.activation(pt[:, i % 2, 0:w], ps[:, 6, 0:w], ACT.Copy).then_inc(pt_done, 1)

                        def o_copy(i):
                            hd, n = ITEMS2[i]
                            act.wait_ge(o_full, i + 1)
                            if i == 0:
                                act.wait_ge(spilled, 16)
                            act.activation(att[:, hd, n * P:(n + 1) * P], ps[:, 7, 0:P], ACT.Copy).then_inc(o_hi, 1)

                        ed, lt = Count(act, exps_done), Count(act, ln_th)
                        n_prod = [0]

                        def prod_round(dst, src, scale):
                            n_prod[0] += 1
                            act.wait_ge(prod_ready, n_prod[0])
                            act.activation(dst, src, ACT.Copy, scale=scale).then_inc(prod_hi, 1)

                        for gi, (name, p) in enumerate(G2):
                            two = slice(2 * p, 2 * p + 2)
                            done = acc_free[gi % 2]

                            def slot(i):
                                if i < len(ITEMS2):
                                    exps(i)
                                if 2 <= i < len(ITEMS2) + 2:
                                    pt_copy(i - 2)
                                if 3 <= i:
                                    o_copy(i - 3)

                            tap_half = gi - CONV_AT
                            if 0 <= tap_half < 2 * KD:
                                kt = tap_half // 2
                                act.wait_ge(glu_done, kt // 2 + 1)
                                act.wait_ge(half_w_done, 1)
                                if tap_half:
                                    act.wait_ge(tap_summed, 5 * (tap_half // 2) + 2 * (tap_half % 2))
                                for m in range(3):
                                    j = 3 * (tap_half % 2) + m
                                    w = half_w[:, KD * j + kt:KD * j + kt + 1]
                                    src = u[:, kt, FIRST_SIDE + j:FIRST_SIDE + j + T]
                                    bias = pcol("conv_b", kt) if j == 0 else 0.0
                                    act.activation(tap_prod[m], src, ACT.Identity, scale=w, bias=bias).then_inc(tap_made, 1)
                            for half in range(HALVES):
                                for s in STEPS_AT.get((gi, half), []):
                                    slot(s)
                                if half % 2 == 0:
                                    prefetch(2 * gi + 1 + half // 2 + AHEAD)
                            if gi == LN_AT + 1:
                                for kt in range(KD):
                                    act.wait_ge(centred, kt + 1)
                                    act.activation(sq[:, kt, :], conv[:, kt, :], ACT.Square).then_inc(squares, 1)
                            if gi == LN_AT + 3:
                                for kt in range(KD):
                                    act.wait_ge(ln_ready, kt + 1)
                                    lt.done(act.activation(ln_tanh[:, kt, :], conv[:, kt, :], ACT.Tanh, scale=0.5))
                            src = banks(gi)
                            full(act, gi)
                            if name == "ua":
                                if p:
                                    act.wait_ge(glu_done, p)
                                act.activation(glu_a, src, ACT.Copy).then_inc(done, 1)
                            elif name == "ub":
                                act.activation(glu_b, src, ACT.Tanh, scale=0.5).then_inc(done, 1)
                            elif name in ("q", "k"):
                                if name == "q" and p == 0:
                                    act.wait_ge(glu_done, 4)
                                act.activation((q if name == "q" else k)[:, two, :], src, ACT.Copy).then_inc(done, 1)
                            elif name == "v":
                                if p == 2:
                                    act.wait_ge(conv_done, 2 * KD)
                                act.activation(vT[:, two, :], src, ACT.Copy).then_inc(done, 1)
                            elif name in ("gc", "ga"):
                                if name == "ga" and p == 0:
                                    act.wait_ge(prod_ready, KD)
                                act.activation((gc if name == "gc" else ga)[:, two, :], src, ACT.Tanh, scale=0.5)\
                                    .then_inc(done, 1)
                            elif name == "wo":
                                act.activation(att[:, two, :], src, ACT.Copy).then_inc(done, 1)
                                emptied(act, gi)
                                for t in (2 * p, 2 * p + 1):
                                    act.activation(conv[:, t, :], att[:, t, :], ACT.Square).then_inc(squares, 1)
                            if 17 <= gi <= 20:
                                w = gi - 17
                                act.wait_ge(vt_full, w + 1)
                                dst = vtok[:, :, 2 * w * P:(2 * w + 2) * P].rearrange("p n (o c) -> p o n c", o=2)
                                for o in range(2):
                                    ins = act.activation(dst[:, o, :, :], ps[:, 4 + o, :].rearrange("p (n c) -> p n c", n=NB),
                                                         ACT.Copy)
                                    if o == 0:
                                        step.done(ins)
                                    else:
                                        ins.then_inc(vt_done, 1)
                            if gi == at2[("ga", 3)]:
                                for kt in range(KD):
                                    prod_round(h_hi[:, kt, :], conv[:, kt, :], 0.5)
                            for hd in HEADS_AT.get(gi, ()):
                                act.wait_ge(clipped, hd + 1)
                                act.activation(conv[:, hd, :], conv[:, hd, :], ACT.Square, scale=1.0 / 16.0)\
                                    .then_inc(squares, 1)
                            if gi == at2[("cv", 3)]:
                                for kt in range(KD):
                                    prod_round(h_hi[:, kt, :], gc[:, kt, :], 0.5)

                    @block.vector
                    def _(dve):
                        step = Count(dve, dve_step)
                        tt, ts, stt = dve.tensor_tensor, dve.tensor_scalar, dve.scalar_tensor_tensor
                        dve.wait_ge(small_in, 96)
                        step.done(stt(gain1, mod[:, 8:16], 1.0, pcol("pre_norm1", 0, 8), ALU.add, ALU.mult))
                        cm = Count(dve, mean_done)
                        dve_add_squares(dve, step, sq)
                        dve_mean(dve, SUM_BANK, 0, cm)
                        dve.wait_ge(spread, 1)
                        nd = Count(dve, normed)
                        for kt in range(KD + 1):
                            if kt < KD:
                                nd.done(stt(sq[:, kt, :], x[:, kt, :], gain1[:, kt:kt + 1], ps[:, SPREAD_BANK, :],
                                            ALU.mult, ALU.mult))
                            if kt:
                                dve.wait_ge(h_hi_done, kt)
                                stt(h_lo[:, kt - 1, :], sq[:, kt - 1, :], mod[:, kt - 1:kt], h_hi[:, kt - 1, :].bitcast(F32),
                                    ALU.add, ALU.subtract).then_inc(h_lo_done, 1)
                        lam = lambdas.rearrange("p (a b c) -> p a b c", a=2, b=2)
                        prod = tmp[:, 0:2 * HD].rearrange("p (a c) -> p a c", a=2)
                        step.done(tt(prod, lam[:, :, 0, :], lam[:, :, 1, :], ALU.mult))
                        pd = Count(dve, par_dve)
                        pd.done(dve.tensor_reduce(lam_t[:, 0:2], prod, AX.X, ALU.add))
                        step.done(tt(gain_post, mod[:, 16:24], pcol("post_norm1", 0, 8), ALU.mult))
                        step.done(ts(head_gain, pcol("head_norm"), 1.0 - LAM_INIT, None, ALU.mult))
                        dve.wait_ge(par_act, 1)
                        step.done(tt(neg_lam, lam_t[:, 3:4], lam_t[:, 2:3], ALU.subtract))
                        step.done(ts(neg_lam, neg_lam, LAM_INIT, None, ALU.subtract))
                        Count(dve, half_w_done).done(ts(half_w, taps_w[:, KD * FIRST_SIDE:KD * TAPS], 0.5, None, ALU.mult))
                        dve.wait_ge(h_lo_done, KD)
                        step.done(dve.memset(u[:, :, 0:PAD], 0.0))

                        cd = Count(dve, conv_done)

                        def taps(half):
                            kt = half // 2
                            first, last = (0, 13) if half % 2 == 0 else (13, FIRST_SIDE)
                            for j in range(first, last):
                                w = taps_w[:, KD * j + kt:KD * j + kt + 1]
                                src = u[:, kt, j:j + T]
                                if j == 0:
                                    step.done(ts(conv[:, kt, :], src, w, None, ALU.mult))
                                else:
                                    ins = stt(conv[:, kt, :], src, w, conv[:, kt, :], ALU.mult, ALU.add)
                                    (cd if j == 12 else step).done(ins)
                            if half % 2:
                                dve.wait_ge(tap_summed, 5 * (kt + 1))
                                cd.done(stt(conv[:, kt, :], conv[:, kt, :], 0.5, tap_sum, ALU.mult, ALU.add))

                        sm = Count(dve, s_max)
                        rdy = Count(dve, p_ready)

                        def maxima(i):
                            hd, n = ITEMS2[i]
                            w = (n + 1) * P
                            dve.wait_ge(s_full, i + 1)
                            s = stat[i % 2]
                            diag = ps[:, 4:6, n * P:(n + 1) * P]
                            mask = band[:, P:2 * P].unsqueeze(1).to_broadcast([P, 2, P])
                            step.done(tt(diag, diag, mask, ALU.add))
                            step.done(dve.tensor_reduce(s[:, 0:2], ps[:, 4:6, 0:w], AX.X, ALU.max))
                            sm.done(ts(s[:, 2:4], s[:, 0:2], -(HD ** -0.5), None, ALU.mult))

                        def combine(i):
                            hd, n = ITEMS2[i]
                            w = (n + 1) * P
                            s = stat[i % 2]
                            dve.wait_ge(exps_done, 2 * i + 2)
                            step.done(dve.reciprocal(s[:, 6:8], s[:, 4:6]))
                            step.done(tt(s[:, 7:8], s[:, 7:8], neg_lam, ALU.mult))
                            p1, p2 = pr[:, i % 2, 0, 0:w], pr[:, i % 2, 1, 0:w]
                            step.done(ts(p1, p1, s[:, 6:7], None, ALU.mult))
                            rdy.done(stt(p1, p2, s[:, 7:8], p1, ALU.mult, ALU.add))

                        n_prod = [0]
                        pready = Count(dve, prod_ready)
                        pl = Count(dve, prod_lo)

                        def prod_rest(kt, src):
                            n_prod[0] += 1
                            dve.wait_ge(prod_hi, n_prod[0])
                            pl.done(stt(h_lo[:, kt, :], src, 0.5, h_hi[:, kt, :].bitcast(F32), ALU.mult, ALU.subtract))

                        rs = Count(dve, rope_sin)
                        gd, ct = Count(dve, glu_done), Count(dve, centred)
                        lr, hdn = Count(dve, ln_ready), Count(dve, heads_done)
                        for gi, (name, p) in enumerate(G2):
                            two = slice(2 * p, 2 * p + 2)
                            src = banks(gi)
                            if CONV_AT <= gi < CONV_AT + 16:
                                taps(gi - CONV_AT)
                            if gi == LN_AT:
                                dve.wait_ge(sums_done, 2)
                                Count(dve, ln_mean).done(ts(rstd[:, 0:NB], ps[:, SUM_BANK, 0:NB], 1.0 / D, None, ALU.mult))
                                dve.wait_ge(spread, 2)
                                for kt in range(KD):
                                    ct.done(tt(conv[:, kt, :], conv[:, kt, :], ps[:, SPREAD_BANK, :], ALU.subtract))
                            if gi == LN_AT + 2:
                                dve_mean(dve, SUM_BANK, 2, cm)
                                dve.wait_ge(spread, 3)
                                for kt in range(KD):
                                    step.done(stt(conv[:, kt, :], conv[:, kt, :], pcol("conv_ln_g", kt),
                                                  ps[:, SPREAD_BANK, :], ALU.mult, ALU.mult))
                                    lr.done(ts(conv[:, kt, :], conv[:, kt, :], pcol("conv_ln_b", kt), None, ALU.add))
                            if gi == LN_AT + 4:
                                for kt in range(KD):
                                    dve.wait_ge(ln_th, kt + 1)
                                    pready.done(stt(conv[:, kt, :], ln_tanh[:, kt, :], 1.0, conv[:, kt, :], ALU.add, ALU.mult))
                            if 10 <= gi <= 17:
                                dve.wait_ge(c7_full, gi - 9)
                                for o in range(2):
                                    if gi > 10:
                                        dve.wait_ge(rope_done, 2 * (gi - 11) + o + 1)
                                    rs.done(tt(pt[:, o, :], ps[:, 6 + o, :], sin_t, ALU.mult))
                            for half in range(HALVES):
                                for i in STEPS_AT.get((gi, half), []):
                                    if i < len(ITEMS2):
                                        maxima(i)
                                    if 1 <= i <= len(ITEMS2):
                                        combine(i - 1)
                            if name == "ub":
                                emptied(dve, gi - 1)
                                emptied(dve, gi)
                                gd.done(stt(u[:, two, PAD:], glu_b, 1.0, glu_a, ALU.add, ALU.mult))
                            if name == "cv":
                                full(dve, gi)
                                emptied(dve, at2[("gc", p)])
                                for o in range(2):
                                    t = 2 * p + o
                                    step.done(ts(gc[:, t, :], gc[:, t, :], 1.0, None, ALU.add))
                                    ins = stt(gc[:, t, :], src[:, o, :], pcol("conv_b_out", t), gc[:, t, :],
                                              ALU.add, ALU.mult)
                                    if o:
                                        ins.then_inc(acc_free[gi % 2], 1)
                                        emptied(dve, gi)
                                    else:
                                        step.done(ins)
                            if gi == at2[("ga", 3)]:
                                for kt in range(KD):
                                    prod_rest(kt, conv[:, kt, :])
                            if gi == at2[("cv", 0)]:
                                dve.wait_ge(prod_lo, KD)
                                emptied(dve, at2[("ga", 2)])
                                emptied(dve, at2[("ga", 3)])
                            for hd in HEADS_AT.get(gi, ()):
                                dve.wait_ge(o_hi, NB * (hd + 1))
                                ts(conv[:, hd, :], att[:, hd, :], 2.0 ** 64, -2.0 ** 64, ALU.min, ALU.max)\
                                    .then_inc(clipped, 1)
                                step.done(stt(ga[:, hd, :], ga[:, hd, :], 1.0, att[:, hd, :], ALU.add, ALU.mult))
                            if gi == at2[("cv", 3)]:
                                dve.wait_ge(sums_done, 4)
                                step.done(ts(in_range, ps[:, 4, 0:32], 2.0 ** 120, None, ALU.is_lt))
                                step.done(ts(rstd[:, 0:32], ps[:, 4, 0:32], 2.0 ** 120, 256.0 / VD, ALU.min, ALU.mult))
                                cm.done(ts(rstd[:, 0:32], rstd[:, 0:32], EPS, None, ALU.add))
                                dve.wait_ge(rstd_done, 3)
                                tt(rstd[:, 0:32], rstd[:, 0:32], in_range, ALU.mult).then_inc(rstd_kept, 1)
                                for hd in range(HEADS2):
                                    dve.wait_ge(spread, 3 + hd + 1)
                                    hdn.done(stt(ga[:, hd, :], ga[:, hd, :], head_gain, ps[:, 4 + hd % 4, :],
                                                 ALU.mult, ALU.mult))
                                    pready.done(tt(gc[:, hd, :], gc[:, hd, :], ga[:, hd, :], ALU.add))
                                    if hd:
                                        prod_rest(hd - 1, gc[:, hd - 1, :])
                                prod_rest(HEADS2 - 1, gc[:, HEADS2 - 1, :])
                        dve_add_squares(dve, step, conv, 3 * KD, 1)
                        dve_mean(dve, SUM_BANK, 4, cm)
                        dve.wait_ge(spread, 3 + HEADS2 + 1)
                        dve.wait_ge(x_back, 16)
                        xd = Count(dve, x_done)
                        for kt in range(KD):
                            xd.done(stt(x[:, kt, :], x[:, kt, :], gain_post[:, kt:kt + 1], ps[:, SPREAD_BANK, :],
                                        ALU.mult, ALU.mult))
                            if kt % 2 == 0:
                                xd.done(tt(x[:, kt, :], x[:, kt, :], q[:, kt, :], ALU.add))
                phase_end()

        with nc.Fori(0, DEPTH) as l:
            mixer1(l)
            ffn(1, l)
        final_norm()
        mixer2()
        ffn(2, None)


def _cols(v):
    return v.reshape(-1, P).T


def _consts():
    import numpy as np

    c = np.zeros((P, NCONST), np.float32)

    def put(name, a):
        c[:, CONST[name][0]:CONST[name][1]] = a

    put("ident", np.eye(P))
    i = np.arange(P)[:, None]
    j = np.arange(2 * P)[None, :]
    delta = i + P - j
    put("band", np.where((delta >= 0) & (delta < P), 0.0, -1e30))
    put("t", np.broadcast_to(np.arange(T, dtype=np.float32), (P, T)))
    pos = np.arange(T, dtype=np.float32)
    for n, rot, theta in ((1, HD // 4, 500000.0), (2, HD, 10000.0)):
        half = rot // 2
        inv = (np.float32(theta) ** (-np.arange(0, rot, 2, dtype=np.float32) / np.float32(rot))).astype(np.float32)
        ang = (pos[None, :] * inv[:, None]).astype(np.float32).astype(np.float64)
        cos, sin = np.ones((P, T)), np.zeros((P, T))
        r = np.zeros((P, P))
        for p in range(P):
            e = p % HD
            if e < rot:
                cos[p], sin[p] = np.cos(ang[e % half]), np.sin(ang[e % half])
                if e < half:
                    r[p + half, p] = -1.0
                else:
                    r[p - half, p] = 1.0
        put(f"cos{n}", cos)
        put(f"sin{n}", sin)
        put(f"rot{n}", r)
    return c


def _lay_out(v):
    import numpy as np

    f = {n: np.asarray(a) for n, a in v.items()}
    par1 = []
    sinks = f["attn_sinks"].reshape(DEPTH, NKV, 2, 2).transpose(0, 1, 3, 2).reshape(DEPTH, NQ)
    for l in range(DEPTH):
        by_state = [np.ascontiguousarray(f[n][l].reshape(16, 2, 64).transpose(1, 2, 0)).reshape(P, 16)
                    for n in ("ssm_a_re", "ssm_a_im")]
        dt = np.broadcast_to(f["ssm_log_dt"][l].reshape(16, 2).T[:, None, :], (2, 64, 16)).reshape(P, 16)
        par1.append(np.concatenate([
            _cols(f["norm_mix"][l]), _cols(f["norm_ffn"][l]), _cols(f["b_gate"][l]), _cols(f["conv_w"][l]),
            _cols(f["ssm_d"][l]), *by_state, dt, np.broadcast_to(sinks[l], (P, NQ))], axis=1))
    bT = np.zeros((DEPTH, 4, 2, 16, 2, 4, 2, 64), np.float32)
    cT = np.zeros((DEPTH, 2, 64, 2, 4, 4, 2, 16), np.float32)
    for n, (bn, cn) in enumerate((("ssm_b_re", "ssm_c_re"), ("ssm_b_im", "ssm_c_im"))):
        b = f[bn].reshape(DEPTH, 4, 4, 2, 64, 16)
        c = f[cn].reshape(DEPTH, 4, 4, 2, 16, 64)
        for g in range(2):
            bT[:, :, g, :, n, :, g, :] = b[:, :, :, g].transpose(0, 2, 4, 1, 3)
            cT[:, g, :, n, :, :, g, :] = c[:, :, :, g].transpose(0, 4, 1, 2, 3)
    s2 = {n[:-2]: a[0] for n, a in f.items() if n.endswith("_2")}
    lambdas = np.concatenate([s2[n] for n in ("lambda_q1", "lambda_k1", "lambda_q2", "lambda_k2")])
    par2 = np.concatenate([
        _cols(f["norm_final"]), _cols(s2["c"]), _cols(s2["b_ada"]), _cols(s2["pre_norm1"]), _cols(s2["post_norm1"]),
        _cols(s2["conv_b"]), _cols(s2["conv_ln_g"]), _cols(s2["conv_ln_b"]),
        _cols(s2["conv_b_out"]), _cols(s2["head_norm"]), _cols(s2["pre_norm2"]), _cols(s2["post_norm2"]),
        _cols(s2["conv_w"]),
        np.broadcast_to(lambdas, (P, 256))], axis=1)
    ins = {"xT": f["x"][0].T, "par1": np.stack(par1), "par2": par2, "const": _consts(),
           "bT": bT.reshape(DEPTH, P, 2, 4, P), "cT": cT.reshape(DEPTH, P, 2, 4, P)}
    for n in ("w_in", "w_attn_o", "w_conv_o", "w_ssm_glu", "w_ssm_o", "w_mix_o", "w_ffn_in", "w_ffn_out"):
        ins[n] = f[n]
    for n in ("w_ada", "w_in", "conv_w_out", "w_o", "w_ff1", "w_ff2"):
        ins[n + "2"] = s2[n]
    return {n: np.ascontiguousarray(a) for n, a in ins.items()}


def kernel(**inputs):
    import numpy as np
    import concourse.bacc as bacc
    from concourse.bass_utils import run_bass_kernel_spmd

    nc = bacc.Bacc("TRN2", target_bir_lowering=False, num_devices=1)
    arrays, drams = {}, {}
    for name, a in _lay_out(inputs).items():
        arrays[f"in_{name}_dram"] = a
        drams[name] = nc.dram_tensor(f"in_{name}_dram", a.shape, mybir.dt.from_np(a.dtype), kind="ExternalInput").ap()
    drams["out"] = nc.dram_tensor("out_0_dram", (D, T), F32, kind="ExternalOutput").ap()
    build(nc, drams)
    r = run_bass_kernel_spmd(nc, [arrays], core_ids=[0])
    return np.ascontiguousarray(r.results[0]["out_0_dram"].T)[None]
```
